# Optimizing a Trainium2 kernel written in Bass

```python
import math
import jax, jax.numpy as jnp
from jax import lax
import numpy as np

D_MODEL = 1024
BATCH = 1
SEQ = 2048
DEPTH = 1

N_MIXERS = 2
NORM_EPS = 1e-6

GLA_HEADS = 4
GLA_DK = D_MODEL // 2
GLA_DV = D_MODEL
GLA_DK_HEAD = GLA_DK // GLA_HEADS
GLA_DV_HEAD = GLA_DV // GLA_HEADS
GLA_RANK = 16
GLA_TAU = 16.0
GLA_CHUNK = 64
GLA_IN = 2 * GLA_DK + GLA_DV + GLA_RANK + GLA_DV

DSW_HEADS = 16
DSW_HEAD_DIM = D_MODEL // DSW_HEADS
DSW_WIDTH = DSW_HEADS * DSW_HEAD_DIM
DSW_GROUPS = ((128, 1), (512, 4), (2048, 16))
N_GROUPS = len(DSW_GROUPS)
DSW_IN = N_GROUPS * 3 * DSW_WIDTH + DSW_WIDTH

REL_BUCKETS = 32
REL_MAX_DIST = 2048


def rmsnorm(x, g):
    x32 = x.astype(jnp.float32)
    y = x32 * lax.rsqrt(jnp.mean(x32 * x32, axis=-1, keepdims=True) + NORM_EPS)
    return y.astype(x.dtype) * g

def t5_causal_bucket(n):
    max_exact = REL_BUCKETS // 2
    nf = np.maximum(n, 1).astype(np.float32)
    large = max_exact + (np.log(nf / max_exact) / math.log(REL_MAX_DIST / max_exact)
                         * (REL_BUCKETS - max_exact)).astype(np.int32)
    large = np.minimum(large, REL_BUCKETS - 1)
    return np.where(n < max_exact, n, large).astype(np.int32)

def gla_mixer(h, w_in, w_alpha, b_alpha, norm_g, w_out):
    B, S, _ = h.shape
    H, dk, dv, C = GLA_HEADS, GLA_DK_HEAD, GLA_DV_HEAD, GLA_CHUNK
    nc = S // C
    proj = h @ w_in
    q, k, v, g_lr, r = jnp.split(
        proj, [GLA_DK, 2 * GLA_DK, 2 * GLA_DK + GLA_DV, 2 * GLA_DK + GLA_DV + GLA_RANK], axis=-1)
    log_a = jax.nn.log_sigmoid((g_lr @ w_alpha + b_alpha).astype(jnp.float32)) / GLA_TAU

    def chunks(t, d):
        return t.astype(jnp.float32).reshape(B, nc, C, H, d).transpose(0, 3, 1, 2, 4)

    q = chunks(q, dk) * (dk ** -0.5)
    k = chunks(k, dk)
    v = chunks(v, dv)
    b = jnp.cumsum(chunks(log_a, dk), axis=3)

    mid = b[:, :, :, C // 2:C // 2 + 1]
    a_intra = jnp.einsum('bhnid,bhnjd->bhnij', q * jnp.exp(b - mid), k * jnp.exp(mid - b))
    causal = jnp.tril(jnp.ones((C, C), dtype=bool))
    a_intra = jnp.where(causal, a_intra, 0.0)
    o = jnp.einsum('bhnij,bhnje->bhnie', a_intra, v)

    b_last = b[:, :, :, -1:]
    kv = jnp.einsum('bhnjd,bhnje->bhnde', k * jnp.exp(b_last - b), v)
    decay = jnp.exp(b_last[:, :, :, 0])

    def step(state, inp):
        dec, kv_n = inp
        return dec[..., None] * state + kv_n, state

    _, states = lax.scan(step, jnp.zeros((B, H, dk, dv), jnp.float32),
                         (decay.transpose(2, 0, 1, 3), kv.transpose(2, 0, 1, 3, 4)))
    o = o + jnp.einsum('bhnid,nbhde->bhnie', q * jnp.exp(b), states)

    o = o.transpose(0, 2, 3, 1, 4).reshape(B, S, H, dv)
    o = rmsnorm(o, norm_g)
    o = o.reshape(B, S, GLA_DV).astype(h.dtype) * jax.nn.silu(r)
    return o @ w_out

def dilated_group_attn(q, k, v, rel_bias, window, dil):
    B, S, H, Dh = q.shape
    span = window // dil
    L = S // dil
    nb = -(-L // span)
    Lp = nb * span

    def to_sub(t):
        t = t.reshape(B, L, dil, H, Dh).transpose(0, 2, 3, 1, 4)
        return jnp.pad(t, ((0, 0), (0, 0), (0, 0), (0, Lp - L), (0, 0)))

    def banded(t):
        tp = jnp.pad(to_sub(t), ((0, 0), (0, 0), (0, 0), (span, 0), (0, 0)))
        prev = tp[:, :, :, :Lp].reshape(B, dil, H, nb, span, Dh)
        cur = tp[:, :, :, span:].reshape(B, dil, H, nb, span, Dh)
        return jnp.concatenate([prev, cur], axis=-2)

    qs = to_sub(q).reshape(B, dil, H, nb, span, Dh)
    kb, vb = banded(k), banded(v)

    qi = np.arange(span)[:, None]
    kj = np.arange(2 * span)[None, :]
    steps = qi + span - kj
    in_window = (steps >= 0) & (steps <= span)
    bucket = t5_causal_bucket(np.clip(steps, 0, span) * dil)
    bias = rel_bias[bucket].transpose(2, 0, 1).astype(jnp.float32)
    first_block = (np.arange(nb) == 0)[:, None, None]
    mask = in_window[None] & (~first_block | (kj >= span)[None])

    logits = jnp.einsum('bdhnqe,bdhnke->bdhnqk', qs, kb).astype(jnp.float32) * (Dh ** -0.5)
    logits = jnp.where(mask, logits + bias[:, None], -jnp.inf)
    lse = jax.nn.logsumexp(logits, axis=-1)
    p = jnp.exp(logits - lse[..., None])
    o = jnp.einsum('bdhnqk,bdhnke->bdhnqe', p.astype(vb.dtype), vb)

    o = o.reshape(B, dil, H, Lp, Dh)[:, :, :, :L].transpose(0, 3, 1, 2, 4).reshape(B, S, H, Dh)
    lse = lse.reshape(B, dil, H, Lp)[:, :, :, :L].transpose(0, 3, 1, 2).reshape(B, S, H)
    return o, lse

def dilated_mixer(h, w_in, w_out, rel_bias):
    B, S, _ = h.shape
    proj = h @ w_in
    qkv = proj[..., :N_GROUPS * 3 * DSW_WIDTH].reshape(B, S, N_GROUPS, 3, DSW_HEADS, DSW_HEAD_DIM)
    gate = proj[..., N_GROUPS * 3 * DSW_WIDTH:]
    outs, lses = [], []
    for g, (window, dil) in enumerate(DSW_GROUPS):
        o, lse = dilated_group_attn(qkv[:, :, g, 0], qkv[:, :, g, 1], qkv[:, :, g, 2],
                                    rel_bias, window, dil)
        outs.append(o)
        lses.append(lse)
    w = jax.nn.softmax(jnp.stack(lses, axis=0), axis=0)
    o = jnp.sum(w[..., None] * jnp.stack(outs, axis=0).astype(jnp.float32), axis=0)
    o = o.reshape(B, S, DSW_WIDTH).astype(h.dtype) * jax.nn.silu(gate)
    return o @ w_out

def first_inputs(seed: int = 0) -> dict:
    key = jax.random.key(seed)
    ks = jax.random.split(key, 16)
    n_gla = (DEPTH + N_MIXERS - 1) // N_MIXERS
    n_dsw = DEPTH // N_MIXERS
    nrm = jax.random.normal
    f32 = jnp.float32
    return {
        "x": nrm(ks[0], (BATCH, SEQ, D_MODEL), f32),
        "c": nrm(ks[1], (BATCH, D_MODEL), f32),
        "ada_w": nrm(ks[2], (DEPTH, D_MODEL, 3 * D_MODEL), f32) * D_MODEL ** -0.5,
        "ada_b": nrm(ks[3], (DEPTH, 3 * D_MODEL), f32) * 0.02,
        "norm_g": 1.0 + 0.05 * nrm(ks[4], (DEPTH, D_MODEL), f32),
        "gla_w_in": nrm(ks[5], (n_gla, D_MODEL, GLA_IN), f32) * D_MODEL ** -0.5,
        "gla_w_alpha": nrm(ks[6], (n_gla, GLA_RANK, GLA_DK), f32) * GLA_RANK ** -0.5,
        "gla_b_alpha": nrm(ks[7], (n_gla, GLA_DK), f32) * 0.1,
        "gla_norm_g": 1.0 + 0.05 * nrm(ks[8], (n_gla, GLA_DV_HEAD), f32),
        "gla_w_out": nrm(ks[9], (n_gla, GLA_DV, D_MODEL), f32) * GLA_DV ** -0.5,
        "dsw_w_in": nrm(ks[10], (n_dsw, D_MODEL, DSW_IN), f32) * D_MODEL ** -0.5,
        "dsw_w_out": nrm(ks[11], (n_dsw, DSW_WIDTH, D_MODEL), f32) * DSW_WIDTH ** -0.5,
        "rel_bias": nrm(ks[12], (REL_BUCKETS, DSW_HEADS), f32) * 0.5,
        "final_g": 1.0 + 0.05 * nrm(ks[13], (D_MODEL,), f32),
    }

def first_block(x, c, ada_w, ada_b, norm_g, gla_w_in, gla_w_alpha, gla_b_alpha, gla_norm_g,
              gla_w_out, dsw_w_in, dsw_w_out, rel_bias, final_g):
    c_act = jax.nn.silu(c)
    for i in range(DEPTH):
        mod = c_act @ ada_w[i] + ada_b[i]
        shift, scale, gate = jnp.split(mod, 3, axis=-1)
        h = rmsnorm(x, norm_g[i]) * (1.0 + scale[:, None]) + shift[:, None]
        j = i // N_MIXERS
        if i % N_MIXERS == 0:
            y = gla_mixer(h, gla_w_in[j], gla_w_alpha[j], gla_b_alpha[j], gla_norm_g[j], gla_w_out[j])
        else:
            y = dilated_mixer(h, dsw_w_in[j], dsw_w_out[j], rel_bias)
        x = x + gate[:, None] * y
    return rmsnorm(x, final_g)


CTX_LEN = 256
GRID_W = 64
D_MIX = D_MODEL
D_ATTN = D_MIX // 2
D_CONV = D_MIX - D_ATTN
HEAD_DIM = 64
N_Q_HEADS = D_ATTN // HEAD_DIM
N_KV_HEADS = 2
GROUP = N_Q_HEADS // N_KV_HEADS
ROPE_AXIS_DIM = HEAD_DIM // 2
ROPE_THETA = 10000.0
Q_BLOCK = 128
CONV_WIDTH = 31
CONV_PAD = (CONV_WIDTH - 1) // 2
EPS = 1e-6

Q_LO, Q_HI = 0, D_ATTN
K_LO, K_HI = Q_HI, Q_HI + N_KV_HEADS * HEAD_DIM
V_LO, V_HI = K_HI, K_HI + N_KV_HEADS * HEAD_DIM
ZA_LO, ZA_HI = V_HI, V_HI + D_ATTN
GLU_LO, GLU_HI = ZA_HI, ZA_HI + 2 * D_CONV
ZC_LO, ZC_HI = GLU_HI, GLU_HI + D_CONV
D_IN = ZC_HI


def rms_norm(x, w):
    xf = x.astype(jnp.float32)
    y = xf * lax.rsqrt(jnp.mean(xf * xf, axis=-1, keepdims=True) + EPS)
    return (y * w.astype(jnp.float32)).astype(x.dtype)

def layer_norm(x, w, b):
    xf = x.astype(jnp.float32)
    mu = jnp.mean(xf, axis=-1, keepdims=True)
    var = jnp.mean(jnp.square(xf - mu), axis=-1, keepdims=True)
    y = (xf - mu) * lax.rsqrt(var + EPS)
    return (y * w.astype(jnp.float32) + b.astype(jnp.float32)).astype(x.dtype)

def grid_angles(n_tokens, dtype):
    rows = n_tokens // GRID_W
    row = jnp.repeat(jnp.arange(rows, dtype=jnp.float32), GRID_W)
    col = jnp.tile(jnp.arange(GRID_W, dtype=jnp.float32), rows)
    freqs = ROPE_THETA ** (-jnp.arange(0, ROPE_AXIS_DIM, 2, dtype=jnp.float32) / ROPE_AXIS_DIM)
    ang_r = row[:, None] * freqs[None, :]
    ang_c = col[:, None] * freqs[None, :]
    return (jnp.cos(ang_r).astype(dtype), jnp.sin(ang_r).astype(dtype),
            jnp.cos(ang_c).astype(dtype), jnp.sin(ang_c).astype(dtype))

def rope_axis(x, cos, sin):
    cos = cos[None, :, None, :]
    sin = sin[None, :, None, :]
    x1, x2 = jnp.split(x, 2, axis=-1)
    return jnp.concatenate([x1 * cos - x2 * sin, x1 * sin + x2 * cos], axis=-1)

def rope_2d(x, angles):
    cr, sr, cc, sc = angles
    return jnp.concatenate([rope_axis(x[..., :ROPE_AXIS_DIM], cr, sr),
                            rope_axis(x[..., ROPE_AXIS_DIM:], cc, sc)], axis=-1)

def qk_heads(p, qn_w, kn_w):
    B, S, _ = p.shape
    q = p[..., Q_LO:Q_HI].reshape(B, S, N_Q_HEADS, HEAD_DIM)
    k = p[..., K_LO:K_HI].reshape(B, S, N_KV_HEADS, HEAD_DIM)
    v = p[..., V_LO:V_HI].reshape(B, S, N_KV_HEADS, HEAD_DIM)
    return rms_norm(q, qn_w), rms_norm(k, kn_w), v

def kv_heads(p_kv, kn_w):
    B, S, _ = p_kv.shape
    kv = p_kv.reshape(B, S, 2, N_KV_HEADS, HEAD_DIM)
    return rms_norm(kv[:, :, 0], kn_w), kv[:, :, 1]

def attend_blocked(q, k, v):
    B, S, _, _ = q.shape
    scale = 1.0 / math.sqrt(HEAD_DIM)
    qb = q.reshape(B, S // Q_BLOCK, Q_BLOCK, N_KV_HEADS, GROUP, HEAD_DIM).transpose(1, 0, 2, 3, 4, 5)

    def one_block(qblk):
        s = jnp.einsum('bqkgd,bskd->bkgqs', qblk, k).astype(jnp.float32) * scale
        pr = jax.nn.softmax(s, axis=-1).astype(v.dtype)
        return jnp.einsum('bkgqs,bskd->bqkgd', pr, v)

    o = lax.map(one_block, qb)
    return o.transpose(1, 0, 2, 3, 4, 5).reshape(B, S, D_ATTN)

def attend_dense(q, k, v):
    B, C, _, _ = q.shape
    qg = q.reshape(B, C, N_KV_HEADS, GROUP, HEAD_DIM)
    s = jnp.einsum('bqkgd,bskd->bkgqs', qg, k).astype(jnp.float32) / math.sqrt(HEAD_DIM)
    pr = jax.nn.softmax(s, axis=-1).astype(v.dtype)
    return jnp.einsum('bkgqs,bskd->bqkgd', pr, v).reshape(B, C, D_ATTN)

def conformer_conv(glu_in, conv_w, conv_b, ln_w, ln_b, w_pw, b_pw):
    a, g = jnp.split(glu_in, 2, axis=-1)
    u = a * jax.nn.sigmoid(g)
    y = lax.conv_general_dilated(u, conv_w[:, None, :].astype(u.dtype), window_strides=(1,),
                                 padding=[(CONV_PAD, CONV_PAD)],
                                 dimension_numbers=('NWC', 'WIO', 'NWC'),
                                 feature_group_count=D_CONV) + conv_b
    y = jax.nn.silu(layer_norm(y, ln_w, ln_b))
    return y @ w_pw + b_pw

def second_inputs(seed: int = 0) -> dict:
    key = jax.random.key(seed)
    ks = jax.random.split(key, 20)
    nrm = jax.random.normal
    f32 = jnp.float32
    return {
        "x": nrm(ks[0], (BATCH, SEQ, D_MODEL), f32),
        "c": nrm(ks[1], (BATCH, D_MODEL), f32),
        "ctx": nrm(ks[2], (BATCH, CTX_LEN, D_MODEL), f32),
        "c_ctx": nrm(ks[3], (D_MODEL,), f32),
        "w_mod": nrm(ks[4], (DEPTH, D_MODEL, 3 * D_MODEL), f32) * D_MODEL ** -0.5,
        "b_mod": nrm(ks[5], (DEPTH, 3 * D_MODEL), f32) * 0.02,
        "norm_w": 1.0 + 0.05 * nrm(ks[6], (DEPTH, D_MODEL), f32),
        "w_in": nrm(ks[7], (DEPTH, D_MODEL, D_IN), f32) * D_MODEL ** -0.5,
        "q_norm_w": 1.0 + 0.05 * nrm(ks[8], (DEPTH, HEAD_DIM), f32),
        "k_norm_w": 1.0 + 0.05 * nrm(ks[9], (DEPTH, HEAD_DIM), f32),
        "conv_w": nrm(ks[10], (DEPTH, CONV_WIDTH, D_CONV), f32) * CONV_WIDTH ** -0.5,
        "conv_b": nrm(ks[11], (DEPTH, D_CONV), f32) * 0.02,
        "conv_ln_w": 1.0 + 0.05 * nrm(ks[12], (DEPTH, D_CONV), f32),
        "conv_ln_b": nrm(ks[13], (DEPTH, D_CONV), f32) * 0.02,
        "w_pw": nrm(ks[14], (DEPTH, D_CONV, D_CONV), f32) * D_CONV ** -0.5,
        "b_pw": nrm(ks[15], (DEPTH, D_CONV), f32) * 0.02,
        "w_out": nrm(ks[16], (DEPTH, D_MIX, D_MODEL), f32) * D_MIX ** -0.5,
    }

def second_block(x, c, ctx, c_ctx, w_mod, b_mod, norm_w, w_in, q_norm_w, k_norm_w,
              conv_w, conv_b, conv_ln_w, conv_ln_b, w_pw, b_pw, w_out):
    S = x.shape[1]
    angles = grid_angles(S, x.dtype)
    h, hc = x, ctx
    for l in range(DEPTH):
        mod = jax.nn.silu(c) @ w_mod[l] + b_mod[l]
        shift, scale, gate = jnp.split(mod, 3, axis=-1)
        mod_c = jax.nn.silu(c_ctx) @ w_mod[l] + b_mod[l]
        shift_c, scale_c, gate_c = jnp.split(mod_c, 3, axis=-1)

        u = rms_norm(h, norm_w[l]) * (1.0 + scale[:, None, :]) + shift[:, None, :]
        uc = rms_norm(hc, norm_w[l]) * (1.0 + scale_c) + shift_c

        p = u @ w_in[l]
        q, k, v = qk_heads(p, q_norm_w[l], k_norm_w[l])
        q = rope_2d(q, angles)
        k = rope_2d(k, angles)

        if l == DEPTH - 1:
            k_c, v_c = kv_heads(uc @ w_in[l][:, K_LO:V_HI], k_norm_w[l])
        else:
            pc = uc @ w_in[l]
            q_c, k_c, v_c = qk_heads(pc, q_norm_w[l], k_norm_w[l])
            attn_c = attend_dense(q_c, k_c, v_c) * jax.nn.silu(pc[..., ZA_LO:ZA_HI])
            conv_c = conformer_conv(pc[..., GLU_LO:GLU_HI], conv_w[l], conv_b[l], conv_ln_w[l],
                                    conv_ln_b[l], w_pw[l], b_pw[l]) * jax.nn.silu(pc[..., ZC_LO:ZC_HI])
            out_c = jnp.concatenate([attn_c, conv_c], axis=-1) @ w_out[l]

        k_all = jnp.concatenate([k_c, k], axis=1)
        v_all = jnp.concatenate([v_c, v], axis=1)
        attn = attend_blocked(q, k_all, v_all) * jax.nn.silu(p[..., ZA_LO:ZA_HI])

        conv = conformer_conv(p[..., GLU_LO:GLU_HI], conv_w[l], conv_b[l], conv_ln_w[l],
                              conv_ln_b[l], w_pw[l], b_pw[l]) * jax.nn.silu(p[..., ZC_LO:ZC_HI])

        out = jnp.concatenate([attn, conv], axis=-1) @ w_out[l]
        h = h + gate[:, None, :] * out
        if l < DEPTH - 1:
            hc = hc + gate_c * out_c
    return h


def setup_inputs(seed=0):
    out = dict(first_inputs(seed))
    for name, value in second_inputs(seed + 1).items():
        if name != "x":
            out[name + "_2"] = value
    return out


def reference(
    x, c, ada_w, ada_b, norm_g, gla_w_in, gla_w_alpha, gla_b_alpha, gla_norm_g, gla_w_out,
    dsw_w_in, dsw_w_out, rel_bias, final_g, c_2, ctx_2, c_ctx_2, w_mod_2, b_mod_2, norm_w_2,
    w_in_2, q_norm_w_2, k_norm_w_2, conv_w_2, conv_b_2, conv_ln_w_2, conv_ln_b_2, w_pw_2,
    b_pw_2, w_out_2,
):
    x = first_block(
        x, c, ada_w, ada_b, norm_g, gla_w_in, gla_w_alpha, gla_b_alpha, gla_norm_g, gla_w_out,
        dsw_w_in, dsw_w_out, rel_bias, final_g,
    )
    return second_block(
        x, c_2, ctx_2, c_ctx_2, w_mod_2, b_mod_2, norm_w_2, w_in_2, q_norm_w_2, k_norm_w_2,
        conv_w_2, conv_b_2, conv_ln_w_2, conv_ln_b_2, w_pw_2, b_pw_2, w_out_2,
    )


_drawn_inputs = setup_inputs


def setup_inputs(seed=0):
    import zlib

    import numpy as np

    out = dict(_drawn_inputs(seed))
    spreads = {}
    factors = {'ctx_2': 8.0,
     'b_mod_2': 4.063,
     'norm_w_2': 3.521,
     'q_norm_w_2': 8.0,
     'k_norm_w_2': 8.0,
     'conv_b_2': 8.0,
     'conv_ln_w_2': 4.416,
     'conv_ln_b_2': 8.0,
     'b_pw_2': 8.0}
    for name, (base, spread) in spreads.items():
        noise = np.random.default_rng([zlib.crc32(name.encode()), seed]).standard_normal(out[name].shape)
        drawn = base * np.exp(spread * noise) if base else spread * noise
        out[name] = __import__('jax').numpy.asarray(drawn.astype(out[name].dtype))
    for name, factor in factors.items():
        out[name] = (out[name] * factor).astype(out[name].dtype)
    return out
```

```python
from contextlib import ExitStack

import numpy as np

import concourse.bass as bass
from concourse import mybir

F32 = mybir.dt.float32
F32R = mybir.dt.float32r
U32 = mybir.dt.uint32
ALU = mybir.AluOpType
ACT = mybir.ActivationFunctionType
AX_X = mybir.AxisListType.X
ds = bass.ds

P = 128
SEQ, D = 2048, 1024
KT = D // P
TB = 512
NB = SEQ // TB
NT = TB // P
EPS = 1e-6
UP = 1

GLA_H, GLA_DK, GLA_DV, RANK, CHUNK = 4, 128, 256, 16, 64
GLA_QK = 2 * GLA_H * GLA_DK
GLA_VEND = GLA_QK + GLA_H * GLA_DV
GLA_COLS = 3088

VROWS = {}


def _rows(spec):
    at = 0
    for name, n in spec:
        VROWS[name] = (at, n)
        at += n
    return at


NROWS = _rows([("c", 8), ("c_2", 8), ("c_ctx_2", 8), ("ada_b", 24), ("b_mod_2", 24), ("norm_g", 8), ("final_g", 8),
               ("norm_w_2", 8), ("gla_norm_g", 2), ("gla_b_alpha", 4), ("conv_b_2", 4), ("conv_ln_w_2", 4),
               ("conv_ln_b_2", 4), ("b_pw_2", 4), ("q_norm_w_2", 1), ("k_norm_w_2", 1)])


def clear(nc, semaphores):
    nc.clear_and_free_semaphores(semaphores)
    nc.all_engine_barrier()


def pools(nc, ctx, phase):
    def sb(name, shape, dt=F32):
        return ctx.enter_context(nc.sbuf_tensor(f"{phase}_{name}", shape, dt))

    def ps(name, shape, dt=F32):
        return ctx.enter_context(nc.psum_tensor(f"{phase}_{name}", shape, dt))

    made = []
    starters = (nc.sync, nc.scalar, nc.vector, nc.gpsimd, nc.tensor)

    def sem(name):
        made.append(nc.alloc_semaphore(f"{phase}_{name}"))
        starters[len(made) % len(starters)].sem_inc(made[-1], UP)
        return made[-1]

    ctx.callback(lambda: clear(nc, made))
    return sb, ps, sem


def modulation(nc, d, keep):
    with ExitStack() as ctx:
        sb, ps, sem = pools(nc, ctx, "mod")
        SLOTS, WC = 4, 512
        NS = 3 * D // WC
        vrows = sb("vrows", [P, P])
        csil = sb("csil", [P, 24])
        ctan = sb("ctan", [P, 24])
        wslab = [sb(f"wslab{s}", [P, KT, WC]) for s in range(SLOTS)]
        ps_cols = ps("ps_cols", [P, P])
        rows = [sb(f"rows{m}", [1 + m, 3 * D]) for m in range(2)]
        bank = [ps(f"bank{i}", [2, WC]) for i in range(2)]
        ps_mod1 = ps("ps_mod1", [P, 24])
        ps_mod2 = ps("ps_mod2", [P, 24, 2])
        rows_clear, rows_landed, consts_landed = sem("rows_clear"), sem("rows_landed"), sem("consts_landed")
        cols_made, cols_copied, tanh_made, silu_made = (
            sem("cols_made"), sem("cols_copied"), sem("tanh_made"), sem("silu_made"))
        slab_landed = [sem(f"slab_landed{s}") for s in range(SLOTS)]
        slab_used, row_copied = sem("slab_used"), sem("row_copied")
        mods_made, mod_step = sem("mods_made"), sem("mod_step")
        cols, modv, gains, ident = keep["cols"], keep["modv"], keep["gains"], keep["ident"]

        def col(name):
            at, n = VROWS[name]
            return cols[:, at:at + n]

        nc.all_engine_barrier()
        with nc.Block() as block:
            @block.sync
            def _(sp):
                for n in range(2 * NS):
                    w = d["ada_w"] if n < NS else d["w_mod_2"]
                    if n >= SLOTS:
                        sp.wait_ge(slab_used, UP + n - SLOTS + 1)
                    sp.dma_start(wslab[n % SLOTS][:], w.rearrange("(k p) n -> p k n", p=P)[:, :, WC * (n % NS):WC * (n % NS + 1)]
                                 ).then_inc(slab_landed[n % SLOTS], 16)

            @block.scalar
            def _(act):
                act.dma_start(ident[:], d["ident"]).then_inc(consts_landed, 16)
                act.wait_ge(rows_clear, UP + 1)
                for name, (at, n) in VROWS.items():
                    if name in ("q_norm_w_2", "k_norm_w_2"):
                        for half in range(2):
                            act.dma_start(vrows[at:at + 1, 64 * half:64 * half + 64],
                                          d[name].rearrange("(r c) -> r c", r=1)).then_inc(rows_landed, 16)
                    else:
                        act.dma_start(vrows[at:at + n, :], d[name].rearrange("(r c) -> r c", c=P)).then_inc(rows_landed, 16)
                act.wait_ge(cols_copied, UP + 1)
                act.activation(ctan[:], cols[:, 0:24], ACT.Tanh, scale=0.5).then_inc(tanh_made, 1)
                for n in range(2 * NS):
                    m = n // NS
                    act.wait_ge(slab_used, UP + n + 1)
                    act.activation(rows[m][:, WC * (n % NS):WC * (n % NS + 1)], bank[n % 2][0:1 + m, :], ACT.Copy).then_inc(row_copied, 1)

            @block.tensor
            def _(pe):
                pe.wait_ge(consts_landed, UP + 16)
                pe.wait_ge(rows_landed, UP + 16 * (len(VROWS) + 2))
                pe.transpose(ps_cols[:], vrows[:], ident[:]).then_inc(cols_made, 1)
                pe.wait_ge(silu_made, UP + 1)
                def turn_rows(m, out):
                    pe.wait_ge(row_copied, UP + NS * (m + 1))
                    for j in range(3 * KT):
                        pe.transpose(out[:, j:j + 1] if m == 0 else out[:, j, :], rows[m][:, P * j:P * (j + 1)], ident[0:1 + m, 0:1 + m])

                for n in range(2 * NS):
                    m = n // NS
                    pe.wait_ge(slab_landed[n % SLOTS], UP + 16 * (n // SLOTS) + 16)
                    if n >= 2:
                        pe.wait_ge(row_copied, UP + n - 1)
                    for k in range(KT):
                        lhs = csil[:, k:k + 1] if m == 0 else csil[:].rearrange("p (v k) -> p k v", k=8)[:, k, 1:3]
                        last = pe.matmul(bank[n % 2][0:1 + m, :], lhs, wslab[n % SLOTS][:, k, :], start=(k == 0), stop=(k == KT - 1))
                    last.then_inc(slab_used, 1)
                    if n == NS:
                        turn_rows(0, ps_mod1)
                turn_rows(1, ps_mod2)
                pe.drain().then_inc(mods_made, 1)

            @block.vector
            def _(dve):
                dve.memset(vrows[:], 0.0).then_inc(rows_clear, 1)
                dve.wait_ge(cols_made, UP + 1)
                dve.tensor_copy(cols[:], ps_cols[:]).then_inc(cols_copied, 1)
                dve.wait_ge(tanh_made, UP + 1)
                dve.wait_ge(cols_copied, UP + 1)
                dve.scalar_tensor_tensor(csil[:], ctan[:], 1.0, cols[:, 0:24], ALU.add, ALU.mult).then_inc(mod_step, 1)
                dve.wait_ge(mod_step, UP + 1)
                dve.tensor_scalar(csil[:], csil[:], 0.5, None, ALU.mult).then_inc(silu_made, 1)
                dve.wait_ge(mods_made, UP + 1)
                dve.tensor_tensor(modv[:, 0, :], ps_mod1[:], col("ada_b"), ALU.add).then_inc(mod_step, 1)
                for v in range(2):
                    dve.tensor_tensor(modv[:, 1 + v, :], ps_mod2[:, :, v], col("b_mod_2"), ALU.add).then_inc(mod_step, 1)
                dve.wait_ge(mod_step, UP + 4)
                for v, w in enumerate(("norm_g", "norm_w_2", "norm_w_2")):
                    dve.scalar_tensor_tensor(gains[:, v, :], modv[:, v, 8:16], 1.0, col(w), ALU.add, ALU.mult).then_inc(mod_step, 1)
                dve.tensor_scalar(keep["half_gn"][:], col("gla_norm_g"), 0.5, None, ALU.mult).then_inc(mod_step, 1)
                dve.wait_ge(mod_step, UP + 8)


def newton_rsqrt(dve, y, v, t, step, n):
    dve.tensor_tensor(t, y, y, ALU.mult).then_inc(step, 1)
    dve.wait_ge(step, UP + n + 1)
    dve.tensor_tensor(t, t, v, ALU.mult).then_inc(step, 1)
    dve.wait_ge(step, UP + n + 2)
    dve.tensor_scalar(t, t, -0.5, 1.5, ALU.mult, ALU.add).then_inc(step, 1)
    dve.wait_ge(step, UP + n + 3)
    dve.tensor_tensor(y, y, t, ALU.mult).then_inc(step, 1)


def gla_block(nc, d, keep):
    NPROJ = 24
    NW = NPROJ + KT
    PER = NT
    with ExitStack() as ctx:
        sb, ps, sem = pools(nc, ctx, "gla")
        cols, modv, gains, ident = keep["cols"], keep["modv"], keep["gains"], keep["ident"]

        def col(name):
            at, n = VROWS[name]
            return cols[:, at:at + n]

        a_hi = sb("a_hi", [P, KT, TB], F32R)
        a_lo = sb("a_lo", [P, KT, TB], F32R)
        xr = sb("xr", [P, 8, TB])
        xtok = xr[:].rearrange("p a b -> p (a b)").rearrange("p (t n) -> p t n", t=NT)
        o_t = sb("o_t", [P, 8, TB])
        xrc = sb("xrc", [P, 2, NT, P])
        qk = sb("qk", [P, 2, GLA_H, TB])
        v_tok = sb("v_tok", [P, NT, D])
        zb = sb("zb", [P, GLA_H, TB])
        eb = sb("eb", [P, GLA_H, TB])
        tmp = sb("tmp", [P, 6, TB])
        w_raw = [sb(f"w_raw{s}", [P, KT, P]) for s in range(4)]
        w_hi = [sb(f"w_hi{s}", [P, KT, P], F32R) for s in range(2)]
        w_lo = [sb(f"w_lo{s}", [P, KT, P], F32R) for s in range(2)]
        glr_raw = sb("glr_raw", [P, KT, RANK])
        glr_hi = sb("glr_hi", [P, KT, RANK], F32R)
        glr_lo = sb("glr_lo", [P, KT, RANK], F32R)
        glr_t = sb("glr_t", [RANK, TB])
        w_alpha = sb("w_alpha", [RANK, GLA_H * GLA_DK])
        qe, ke, kd, kdt, att = (sb(n, [P, GLA_H, P]) for n in ("qe", "ke", "kd", "kdt", "att"))
        qb = [sb(f"qb{c}", [P, GLA_H, P]) for c in range(2)]
        dec = sb("dec", [P, GLA_H, 2])
        s_in = sb("s_in", [P, 2, GLA_H, GLA_DV])
        s_mid = sb("s_mid", [P, GLA_H, GLA_DV])
        on = sb("on", [P, D])
        sel = sb("sel", [P, P], U32)
        reset = sb("reset", [P, TB])
        ones = sb("ones", [P, P])
        xst = sb("xst", [P, 4, NT])
        ost = sb("ost", [P, 4, GLA_H])
        G = [ps(f"bank_g{i}", [P, TB]) for i in range(2)]
        T = [ps(f"bank_t{i}", [P, TB]) for i in range(2)]
        A = ps("bank_a", [P, TB])
        KV = ps("bank_kv", [P, TB])
        O = ps("bank_o", [P, 2, TB])

        def kv_at(h, c):
            return (KV, T[1])[c][:, GLA_DV * (h % 2):GLA_DV * (h % 2 + 1)]

        scores_seen = sem("scores_seen")
        consts, glr_split, cleared = sem("consts"), sem("glr_split"), sem("cleared")
        x_landed, sq_sum, ms, lnv, rs0, rs_step, xn = (
            sem(n) for n in ("x_landed", "sq_sum", "ms", "lnv", "rs0", "rs_step", "xn"))
        xt, hf, h_hi, h_lo = sem("xt"), sem("hf"), sem("h_hi"), sem("h_lo")
        w_landed = [sem(f"w_landed{s}") for s in range(4)]
        w_rest = [sem(f"w_rest{s}") for s in range(4)]
        w_rounded, proj, proj_out = sem("w_rounded"), sem("proj"), sem("proj_out")
        glr_done, glr_copied, z, zc, zstep, la, scan = (
            sem(n) for n in ("glr_done", "glr_copied", "z", "zc", "zstep", "la", "scan"))
        vt, v_copied = sem("vt"), sem("v_copied")
        dif, exps, qs_dve, qs_pool = sem("dif"), sem("exps"), sem("qs_dve"), sem("qs_pool")
        a_done, kd_done, kdt_copied, at_done = sem("a_done"), sem("kd_done"), sem("kdt_copied"), sem("at_done")
        kv, smid, snew, o_done = sem("kv"), sem("smid"), sem("snew"), sem("o_done")
        osq, oms, oln, ors0, ors_step, on_done, ot, ot_copied = (
            sem(n) for n in ("osq", "oms", "oln", "ors0", "ors_step", "on_done", "ot", "ot_copied"))
        tanh_r, r_done, y_done, y_hi, y_lo = (sem(n) for n in ("tanh_r", "r_done", "y_done", "y_hi", "y_lo"))
        xr_landed, xr_t, xr_copied, x1, sq, sqs = (
            sem(n) for n in ("xr_landed", "xr_t", "xr_copied", "x1", "sq", "sqs"))
        tv, tln, trs0, trs_step, h1, h1_stored = (
            sem(n) for n in ("tv", "tln", "trs0", "trs_step", "h1", "h1_stored"))

        w_in = d["gla_w_in"].rearrange("(k p) n -> p k n", p=P)
        w_out = d["gla_w_out"].rearrange("(k p) n -> p k n", p=P)
        x = d["x"].rearrange("(t p) n -> p t n", p=P)
        h1t = d["h1t"].rearrange("(c p) t -> p c t", p=P)

        def tok(t):
            return slice(P * t, P * (t + 1))

        nc.all_engine_barrier()
        with nc.Block() as block:
            @block.sync
            def _(sp):
                for dst, src in ((sel, "sel"), (reset, "reset"), (ones, "ones")):
                    sp.dma_start(dst[:], d[src]).then_inc(consts, 16)
                sp.dma_start(glr_raw[:], w_in[:, :, GLA_VEND:GLA_VEND + RANK]).then_inc(consts, 16)
                sp.dma_start(w_alpha[:], d["gla_w_alpha"]).then_inc(consts, 16)
                sp.dma_start(xtok, x[:, 0:NT, :]).then_inc(x_landed, 16)

                def load(group, s, src, col0):
                    sp.wait_ge(w_rest[s], UP + group)
                    sp.dma_start(w_raw[s][:], src[:, :, ds(col0 + s * P, P)]).then_inc(w_landed[s], 16)
                for s in range(4):
                    load(0, s, w_in, 0)
                with sp.Fori(0, NB) as b:
                    with sp.Fori(1, 4) as g:
                        for s in range(4):
                            load(b * 8 + g, s, w_in, g * TB)
                    with sp.Fori(4, 6) as g:
                        for s in range(4):
                            load(b * 8 + g, s, w_in, g * TB + RANK)
                    with sp.Fori(0, 2) as g:
                        for s in range(4):
                            load(b * 8 + 6 + g, s, w_out, g * TB)
                            sp.wait_ge(xr_t, UP + b * 8 + g * 4 + s)
                            sp.dma_start(xrc[:, s % 2, :, :], x[:, ds(b * NT, NT), ds(g * TB + s * P, P)]).then_inc(xr_landed, 16)
                            if s == 1:
                                sp.wait_ge(y_done, UP + b * 8 + 8)
                                sp.dma_start(xtok[:, ds(g * 2, 2), :], x[:, ds(((b + 1) % NB) * NT + g * 2, 2), :]).then_inc(x_landed, 16)
                    for s in range(4):
                        load(b * 8 + 8, s, w_in, 0)
                    sp.wait_ge(h1, UP + b * 8 + 8)
                    sp.dma_start(h1t[:, :, ds(b * TB, TB)], o_t[:]).then_inc(h1_stored, 16)
                sp.wait_ge(h1_stored, UP + 16 * NB)
                for s in range(4):
                    sp.wait_ge(w_landed[s], UP + 16 * (8 * NB + 1))

            @block.gpsimd
            def _(pool):
                for m in (qb[0], qb[1], att):
                    pool.memset(m[:], 0.0).then_inc(cleared, 1)
                pool.memset(s_in[:, 0, :, :], 0.0).then_inc(cleared, 1)

                def rest(group, s, n):
                    pool.wait_ge(w_rounded, UP + n + 1)
                    pool.tensor_tensor(w_lo[s % 2][:], w_raw[s][:], w_hi[s % 2][:].bitcast(F32), ALU.subtract).then_inc(w_rest[s], 1)

                def ahead(group, s):
                    rest(group if s < 3 else group + 1, (s + 1) % 4, group * 4 + s + 1)

                def decay_k(b, t):
                    u = b * PER + t
                    pool.wait_ge(exps, UP + u * 5 + 2)
                    pool.wait_ge(a_done, UP + u)
                    pool.tensor_tensor(ke[:], qk[:, 1, :, tok(t)], tmp[:, 1, :].rearrange("p (h i) -> p h i", h=4), ALU.mult).then_inc(qs_pool, 1)
                    pool.wait_ge(exps, UP + u * 5 + 4)
                    pool.wait_ge(kd_done, UP + u)
                    pool.tensor_tensor(kd[:], qk[:, 1, :, tok(t)], tmp[:, 3, :].rearrange("p (h i) -> p h i", h=4), ALU.mult).then_inc(qs_pool, 1)
                rest(0, 0, 0)
                with pool.Fori(0, NB) as b:
                    with pool.Fori(0, 4) as g:
                        for s in range(4):
                            ahead(b * 8 + g, s)
                    decay_k(b, 0)
                    for t in range(PER):
                        ahead(b * 8 + 4 + t // 2, 2 * (t % 2))
                        if t + 1 < PER:
                            decay_k(b, t + 1)
                        ahead(b * 8 + 4 + t // 2, 2 * (t % 2) + 1)
                    with pool.Fori(0, 2) as g:
                        for s in range(4):
                            ahead(b * 8 + 6 + g, s)

            @block.tensor
            def _(pe):
                def gemm(group, s, banks=G, first_wait=None):
                    pe.wait_ge(w_rest[s], UP + group + 1)
                    for k in range(KT):
                        if first_wait is not None:
                            pe.wait_ge(first_wait[0], UP + first_wait[1] + k + 1)
                        for n, (w, a) in enumerate(((w_hi, a_hi), (w_hi, a_lo), (w_lo, a_hi))):
                            last = pe.matmul(banks[s % 2][:], w[s % 2][:, k, :], a[:, k, :], start=(k == 0 and n == 0),
                                             stop=(k == KT - 1 and n == 2))
                    last.then_inc(proj, 1)

                def transpose_x(b):
                    pe.wait_ge(xn, UP + b * 4 + 4)
                    pe.wait_ge(xr_copied, UP + b * 8)
                    for c in range(KT):
                        if c >= 2:
                            pe.wait_ge(hf, UP + b * 8 + c - 1)
                        for t in range(NT):
                            last = pe.transpose(T[c % 2][:, tok(t)], xtok[:, t, P * c:P * (c + 1)], ident[:])
                        last.then_inc(xt, 1)

                def unit(b, t):
                    u = b * PER + t
                    pe.wait_ge(qs_dve, UP + u * 3 + 3)
                    pe.wait_ge(qs_pool, UP + u * 2 + 2)
                    pe.wait_ge(at_done, UP + u)
                    for h in range(GLA_H):
                        last = pe.matmul(A[:, tok(h)], ke[:, h, :], qe[:, h, :], start=True, stop=True)
                    last.then_inc(a_done, 1)
                    pe.wait_ge(ot_copied, UP + u * 2)
                    for h in range(GLA_H):
                        last = pe.transpose(T[0][:, tok(h)], kd[:, h, :], ident[:])
                    last.then_inc(kd_done, 1)

                    def kv_of(h):
                        for c in range(2):
                            half = slice(64 * c, 64 * c + 64)
                            last = pe.matmul(kv_at(h, c), kdt[half, h, :],
                                             v_tok[half, t, GLA_DV * h:GLA_DV * (h + 1)], start=True, stop=True)
                        last.then_inc(kv, 1)

                    def out_of(h):
                        pe.wait_ge(smid, UP + u * 4 + h + 1)
                        o = O[:, h // 2, GLA_DV * (h % 2):GLA_DV * (h % 2 + 1)]
                        pe.matmul(o, att[:, h, :], v_tok[:, t, GLA_DV * h:GLA_DV * (h + 1)], start=True, stop=False)
                        pe.matmul(o, qb[0][:, h, :], s_in[:, t % 2, h, :], start=False, stop=False)
                        pe.matmul(o, qb[1][:, h, :], s_mid[:, h, :], start=False, stop=True).then_inc(o_done, 1)
                    pe.wait_ge(kdt_copied, UP + u + 1)
                    pe.wait_ge(snew, UP + u * 4)
                    kv_of(0)
                    kv_of(1)
                    pe.wait_ge(at_done, UP + u + 1)
                    pe.wait_ge(on_done, UP + u * 4)
                    out_of(0)
                    out_of(1)
                    pe.wait_ge(snew, UP + u * 4 + 2)
                    kv_of(2)
                    kv_of(3)
                    out_of(2)
                    out_of(3)

                def transpose_o(b, t):
                    u = b * PER + t
                    pe.wait_ge(on_done, UP + u * 4 + 4)
                    pe.wait_ge(snew, UP + u * 4 + 4)
                    for half in range(2):
                        for c in range(4):
                            last = pe.transpose(T[half][:, tok(c)], on[:, tok(4 * half + c)], ident[:])
                        last.then_inc(ot, 1)

                pe.wait_ge(consts, UP + 80)
                pe.wait_ge(cleared, UP + 4)
                pe.wait_ge(glr_split, UP + 2)
                transpose_x(0)
                with pe.Fori(0, NB) as b:
                    pe.wait_ge(tv, UP + b)
                    pe.wait_ge(x1, UP + b * 8)
                    for k in range(KT):
                        pe.wait_ge(h_lo, UP + b * 8 + k + 1)
                        for n, (w, a) in enumerate(((glr_hi, a_hi), (glr_hi, a_lo), (glr_lo, a_hi))):
                            last = pe.matmul(A[0:RANK, :], w[:, k, :], a[:, k, :], start=(k == 0 and n == 0),
                                             stop=(k == KT - 1 and n == 2))
                    last.then_inc(glr_done, 1)
                    with pe.Fori(0, 2) as g:
                        for s in range(4):
                            pe.wait_ge(proj_out, UP + b * 16 + g * 4 + s)
                            gemm(b * 8 + g, s)
                    pe.wait_ge(glr_copied, UP + b + 1)
                    for h, bank in enumerate((O[:, 0, :], O[:, 1, :], A[:], KV[:])):
                        pe.matmul(bank, w_alpha[:, tok(h)], glr_t[:], start=True, stop=True).then_inc(z, 1)
                    with pe.Fori(0, 2) as g:
                        def transpose_v(s):
                            pe.wait_ge(proj_out, UP + b * 16 + 8 + g * 4 + s + 2)
                            pe.wait_ge(v_copied, UP + b * 8 + g * 4 + s)
                            for t in range(NT):
                                last = pe.transpose(T[s % 2][:, tok(t)], tmp[:, 4 + s % 2, tok(t)], ident[:])
                            last.then_inc(vt, 1)
                        for s in range(4):
                            pe.wait_ge(proj_out, UP + b * 16 + 8 + g * 4 + s)
                            gemm(b * 8 + 2 + g, s)
                            if s:
                                transpose_v(s - 1)
                        transpose_v(3)
                    pe.wait_ge(zc, UP + b * 4 + 4)
                    pe.wait_ge(v_copied, UP + b * 8 + 9)
                    for t in range(PER):
                        unit(b, t)
                        for i in range(2):
                            r = 2 * t + i
                            if r < 2:
                                pe.wait_ge(proj_out, UP + b * 16 + 17)
                            else:
                                pe.wait_ge(r_done, UP + b * 8 + r - 1)
                            gemm(b * 8 + 4 + r // 4, r % 4)
                            if i == 0:
                                transpose_o(b, t)
                    pe.wait_ge(r_done, UP + b * 8 + 8)
                    pe.wait_ge(ot_copied, UP + b * 8 + 8)

                    def sum_squares(c):
                        pe.wait_ge(sq, UP + b * 8 + c + 1)
                        pe.matmul(A[:], ones[:], tmp[:, c % 2, :], start=(c == 0), stop=(c == KT - 1)).then_inc(sqs, 1)
                    for c in range(KT):
                        if c >= 2:
                            pe.wait_ge(xr_copied, UP + b * 8 + c - 1)
                        pe.wait_ge(xr_landed, UP + b * 128 + 16 * c + 16)
                        for t in range(NT):
                            last = pe.transpose(T[c % 2][:, tok(t)], xrc[:, c % 2, t, :], ident[:])
                        last.then_inc(xr_t, 1)
                        if c >= 2:
                            pe.wait_ge(x1, UP + b * 8 + c - 1)
                        gemm(b * 8 + 6 + c // 4, c % 4, first_wait=(y_lo, b * 8) if c == 0 else None)
                        if c:
                            sum_squares(c - 1)
                    sum_squares(KT - 1)
                    transpose_x(b + 1)

            @block.scalar
            def _(act):
                def round_next(group, s):
                    act.wait_ge(w_landed[(s + 1) % 4], UP + (group if s < 3 else group + 1) * 16 + 16)
                    act.wait_ge(proj, UP + group * 4 + s)
                    act.activation(w_hi[(s + 1) % 2][:], w_raw[(s + 1) % 4][:], ACT.Copy).then_inc(w_rounded, 1)

                def squares_of_x(b, landed):
                    act.wait_ge(x_landed, UP + landed)
                    for t in range(NT):
                        if t:
                            act.wait_ge(sq_sum, UP + b * 4 + t)
                        act.activation(O[:].rearrange("p a b -> p (a b)"), xtok[:, t, :], ACT.Square,
                                       accum_out=xst[:, 0, t:t + 1]).then_inc(sq_sum, 1)
                    act.wait_ge(ms, UP + b + 1)
                    act.activation(xst[:, 2, :], xst[:, 1, :], ACT.Ln).then_inc(lnv, 1)
                    act.wait_ge(lnv, UP + b + 1)
                    act.activation(xst[:, 2, :], xst[:, 2, :], ACT.Exp, scale=-0.5).then_inc(rs0, 1)

                def modulate(b):
                    act.wait_ge(sqs, UP + b * 8)
                    for c in range(KT):
                        act.wait_ge(xt, UP + b * 8 + c + 1)
                        if c >= 2:
                            act.wait_ge(h_lo, UP + b * 8 + c - 1)
                        act.activation(tmp[:, c % 2, :], T[c % 2][:], ACT.Identity, bias=modv[:, 0, c:c + 1],
                                       scale=gains[:, 0, c:c + 1]).then_inc(hf, 1)

                def decays(b, t):
                    u = b * PER + t
                    act.wait_ge(dif, UP + u * 2 + 2)
                    act.wait_ge(qs_dve, UP + u * 3)
                    act.wait_ge(qs_pool, UP + u * 2)
                    act.wait_ge(snew, UP + u * 4)
                    for n, (src, scale) in enumerate(((eb[:, :, tok(0)], 1 / 16), (eb[:, :, tok(0)], -1 / 16),
                                                      (zb[:, :, tok(t)], 1 / 16), (eb[:, :, tok(1)], 1 / 16))):
                        act.activation(tmp[:, n, :].rearrange("p (h i) -> p h i", h=4), src, ACT.Exp, scale=scale).then_inc(exps, 1)
                    ends = zb[:, :, tok(t)].rearrange("p h (c i) -> p h c i", c=2)[:, :, :, CHUNK - 1]
                    act.activation(dec[:], ends, ACT.Exp, scale=1 / 16).then_inc(exps, 1)

                act.wait_ge(w_landed[0], UP + 16)
                act.activation(w_hi[0][:], w_raw[0][:], ACT.Copy).then_inc(w_rounded, 1)
                act.wait_ge(consts, UP + 80)
                act.activation(glr_hi[:], glr_raw[:], ACT.Copy).then_inc(proj_out, 1)
                squares_of_x(0, 16)
                modulate(0)
                with act.Fori(0, NB) as b:
                    act.wait_ge(qs_dve, UP + b * 12)
                    act.wait_ge(qs_pool, UP + b * 8)
                    act.wait_ge(glr_done, UP + b + 1)
                    act.activation(glr_t[:], A[0:RANK, :], ACT.Copy).then_inc(glr_copied, 1)
                    for j in range(8):
                        round_next(b * 8 + j // 4, j % 4)
                        act.wait_ge(proj, UP + b * NW + j + 1)
                        act.activation(qk[:, j // 4, j % 4, :], G[j % 2][:], ACT.Copy,
                                       scale=float(GLA_DK) ** -0.5 if j < 4 else 1.0).then_inc(proj_out, 1)
                    at0 = VROWS["gla_b_alpha"][0]
                    for h, bank in enumerate((O[:, 0, :], O[:, 1, :], A[:], KV[:])):
                        act.wait_ge(z, UP + b * 4 + h + 1)
                        act.activation(zb[:, h, :], bank, ACT.Identity, bias=cols[:, at0 + h:at0 + h + 1]).then_inc(zc, 1)
                    for j in range(8):
                        round_next(b * 8 + 2 + j // 4, j % 4)
                        if j >= 2:
                            act.wait_ge(vt, UP + b * 8 + j - 1)
                        act.wait_ge(proj, UP + b * NW + 8 + j + 1)
                        act.activation(tmp[:, 4 + j % 2, :], G[j % 2][:], ACT.Copy).then_inc(proj_out, 1)
                        if j == 0:
                            act.wait_ge(zc, UP + b * 4 + 4)
                            act.activation(eb[:], zb[:], ACT.Abs).then_inc(zstep, 1)
                        if j == 1:
                            act.wait_ge(zstep, UP + b * 3 + 1)
                            act.activation(eb[:], eb[:], ACT.Exp, scale=-1.0).then_inc(zstep, 1)
                        if j == 2:
                            act.wait_ge(zstep, UP + b * 3 + 2)
                            act.activation(eb[:], eb[:], ACT.Ln, bias=1.0).then_inc(zstep, 1)
                    decays(b, 0)
                    for t in range(PER):
                        u = b * PER + t
                        act.wait_ge(kd_done, UP + u + 1)
                        act.activation(kdt[:].rearrange("p h i -> p (h i)"), T[0][:], ACT.Copy).then_inc(kdt_copied, 1)
                        act.wait_ge(ot, UP + u * 2)
                        for h in range(GLA_H):
                            act.wait_ge(o_done, UP + u * 4 + 2 + h // 2 * 2)
                            act.activation(on[:, GLA_DV * h:GLA_DV * (h + 1)], O[:, h // 2, GLA_DV * (h % 2):GLA_DV * (h % 2 + 1)],
                                           ACT.Square, accum_out=ost[:, 0, h:h + 1]).then_inc(osq, 1)
                        round_next(b * 8 + 4 + t // 2, 2 * (t % 2))
                        act.wait_ge(oms, UP + u + 1)
                        act.activation(ost[:, 2, :], ost[:, 1, :], ACT.Ln).then_inc(oln, 1)
                        act.wait_ge(oln, UP + u + 1)
                        act.activation(ost[:, 2, :], ost[:, 2, :], ACT.Exp, scale=-0.5).then_inc(ors0, 1)
                        act.wait_ge(ors_step, UP + u * 4 + 4)
                        act.wait_ge(osq, UP + u * 4 + 4)
                        for h in range(GLA_H):
                            act.activation(on[:, GLA_DV * h:GLA_DV * (h + 1)], O[:, h // 2, GLA_DV * (h % 2):GLA_DV * (h % 2 + 1)],
                                           ACT.Copy, scale=ost[:, 2, h:h + 1]).then_inc(on_done, 1)
                        if t + 1 < PER:
                            decays(b, t + 1)
                        for i in range(2):
                            r = 2 * t + i
                            if i == 1:
                                round_next(b * 8 + 4 + t // 2, 2 * (t % 2) + 1)
                                act.wait_ge(h1_stored, UP + b * 16)
                                for half in range(2):
                                    act.wait_ge(ot, UP + u * 2 + half + 1)
                                    act.activation(o_t[:, 4 * half:4 * half + 4, tok(t)], T[half][:].rearrange("p (c i) -> p c i", c=4),
                                                   ACT.Copy).then_inc(ot_copied, 1)
                            act.wait_ge(proj, UP + b * NW + 16 + r + 1)
                            if r >= 2:
                                act.wait_ge(r_done, UP + b * 8 + r - 1)
                            act.activation(tmp[:, 4 + r % 2, :], G[r % 2][:], ACT.Tanh, scale=0.5).then_inc(tanh_r, 1)
                    act.wait_ge(proj, UP + b * NW + NPROJ)
                    for c in range(KT):
                        act.wait_ge(y_done, UP + b * 8 + c + 1)
                        act.activation(a_hi[:, c, :], xr[:, c, :], ACT.Copy).then_inc(y_hi, 1)

                    def square_x1(c):
                        act.wait_ge(x1, UP + b * 8 + c + 1)
                        if c >= 2:
                            act.wait_ge(sqs, UP + b * 8 + c - 1)
                        act.activation(tmp[:, c % 2, :], o_t[:, c, :], ACT.Square).then_inc(sq, 1)
                    for c in range(KT):
                        round_next(b * 8 + 6 + c // 4, c % 4)
                        act.wait_ge(xr_t, UP + b * 8 + c + 1)
                        if c >= 2:
                            act.wait_ge(x1, UP + b * 8 + c - 1)
                        act.activation(tmp[:, 2 + c % 2, :], T[c % 2][:], ACT.Copy).then_inc(xr_copied, 1)
                        if c:
                            square_x1(c - 1)
                        if c == 5:
                            squares_of_x(b + 1, b * 32 + 48)
                    square_x1(KT - 1)
                    modulate(b + 1)
                    act.wait_ge(tv, UP + b + 1)
                    act.activation(eb[:, 1, :], eb[:, 0, :], ACT.Ln).then_inc(tln, 1)
                    act.wait_ge(tln, UP + b + 1)
                    act.activation(eb[:, 1, :], eb[:, 1, :], ACT.Exp, scale=-0.5).then_inc(trs0, 1)

            @block.vector
            def _(dve):
                def norm_x(b):
                    dve.wait_ge(sq_sum, UP + b * 4 + 4)
                    dve.tensor_scalar(xst[:, 1, :], xst[:, 0, :], 1.0 / D, EPS, ALU.mult, ALU.add).then_inc(ms, 1)
                    dve.wait_ge(rs0, UP + b + 1)
                    newton_rsqrt(dve, xst[:, 2, :], xst[:, 1, :], xst[:, 3, :], rs_step, b * 4)
                    dve.wait_ge(rs_step, UP + b * 4 + 4)
                    for t in range(NT):
                        dve.tensor_scalar(xtok[:, t, :], xtok[:, t, :], xst[:, 2, t:t + 1], None, ALU.mult).then_inc(xn, 1)

                def split_h(b):
                    dve.wait_ge(proj, UP + b * NW)
                    for c in range(KT):
                        dve.wait_ge(hf, UP + b * 8 + c + 1)
                        dve.tensor_copy(a_hi[:, c, :], tmp[:, c % 2, :]).then_inc(h_hi, 1)
                        dve.wait_ge(h_hi, UP + b * 8 + c + 1)
                        dve.tensor_tensor(a_lo[:, c, :], tmp[:, c % 2, :], a_hi[:, c, :].bitcast(F32), ALU.subtract).then_inc(h_lo, 1)

                def logdiffs(b, t):
                    u = b * PER + t
                    dve.wait_ge(exps, UP + u * 5)
                    bt = zb[:, :, tok(t)].rearrange("p h (c i) -> p h c i", c=2)
                    d1 = eb[:, :, tok(0)].rearrange("p h (c i) -> p h c i", c=2)
                    d2 = eb[:, :, tok(1)].rearrange("p h (c i) -> p h c i", c=2)
                    mid = bt[:, :, :, CHUNK // 2:CHUNK // 2 + 1].broadcast_to([P, GLA_H, 2, CHUNK])
                    end = bt[:, :, :, CHUNK - 1:CHUNK].broadcast_to([P, GLA_H, 2, CHUNK])
                    dve.tensor_tensor(d1, bt, mid, ALU.subtract).then_inc(dif, 1)
                    dve.tensor_tensor(d2, end, bt, ALU.subtract).then_inc(dif, 1)

                def decay_q(b, t):
                    u = b * PER + t
                    e1, e3 = (tmp[:, n, :].rearrange("p (h i) -> p h i", h=4) for n in (0, 2))
                    dve.wait_ge(exps, UP + u * 5 + 3)
                    dve.wait_ge(o_done, UP + u * 4)
                    dve.tensor_tensor(qe[:], qk[:, 0, :, tok(t)], e1, ALU.mult).then_inc(qs_dve, 1)
                    for c in range(2):
                        half = slice(CHUNK * c, CHUNK * (c + 1))
                        dve.tensor_tensor(qb[c][:, :, half], qk[:, 0, :, P * t + CHUNK * c:P * t + CHUNK * (c + 1)], e3[:, :, half],
                                          ALU.mult).then_inc(qs_dve, 1)

                dve.wait_ge(proj_out, UP + 1)
                dve.tensor_tensor(glr_lo[:], glr_raw[:], glr_hi[:].bitcast(F32), ALU.subtract).then_inc(glr_split, 1)
                dve.memset(on[:, 0:1], 0.0).then_inc(glr_split, 1)
                dve.memset(ost[:, 0, 0:1], 0.0).then_inc(v_copied, 1)
                dve.wait_ge(cleared, UP + 4)
                norm_x(0)
                split_h(0)
                with dve.Fori(0, NB) as b:
                    for j in range(8):
                        dve.wait_ge(vt, UP + b * 8 + j + 1)
                        dve.tensor_copy(v_tok[:, :, tok(j)], T[j % 2][:].rearrange("p (t i) -> p t i", t=NT)).then_inc(v_copied, 1)
                        if j == 3:
                            dve.wait_ge(zstep, UP + b * 3 + 3)
                            dve.scalar_tensor_tensor(eb[:], zb[:], 0.0, eb[:], ALU.min, ALU.subtract).then_inc(la, 1)
                            dve.wait_ge(la, UP + b + 1)
                        if j >= 4:
                            h = j - 4
                            dve.tensor_tensor_scan(zb[:, h, :], reset[:], eb[:, h, :], 0.0, ALU.mult, ALU.add).then_inc(scan, 1)
                    dve.wait_ge(scan, UP + b * 4 + 4)
                    logdiffs(b, 0)
                    decay_q(b, 0)
                    for t in range(PER):
                        u = b * PER + t
                        dve.wait_ge(cleared, UP + 4)
                        dve.wait_ge(a_done, UP + u + 1)
                        dve.sem_inc(scores_seen, 1)
                        dve.copy_predicated(att[:], sel[:].rearrange("p (h i) -> p h i", h=1).broadcast_to([P, GLA_H, P]),
                                            A[:].rearrange("p (h i) -> p h i", h=4)).then_inc(at_done, 1)
                        dve.wait_ge(exps, UP + u * 5 + 5)
                        for h in range(GLA_H):
                            dve.wait_ge(kv, UP + u * 4 + 2 + h // 2 * 2)
                            dve.scalar_tensor_tensor(s_mid[:, h, :], s_in[:, t % 2, h, :], dec[:, h, 0:1], kv_at(h, 0),
                                                     ALU.mult, ALU.add).then_inc(smid, 1)
                            dve.wait_ge(smid, UP + u * 4 + h + 1)
                            dve.scalar_tensor_tensor(s_in[:, 1 - t % 2, h, :], s_mid[:, h, :], dec[:, h, 1:2], kv_at(h, 1),
                                                     ALU.mult, ALU.add).then_inc(snew, 1)
                        if t + 1 < PER:
                            logdiffs(b, t + 1)
                        dve.wait_ge(osq, UP + u * 4 + 4)
                        dve.tensor_scalar(ost[:, 1, :], ost[:, 0, :], 1.0 / GLA_DV, EPS, ALU.mult, ALU.add).then_inc(oms, 1)
                        dve.wait_ge(ors0, UP + u + 1)
                        newton_rsqrt(dve, ost[:, 2, :], ost[:, 1, :], ost[:, 3, :], ors_step, u * 4)
                        if t + 1 < PER:
                            decay_q(b, t + 1)
                        for i in range(2):
                            r = 2 * t + i
                            dve.wait_ge(tanh_r, UP + b * 8 + r + 1)
                            dve.scalar_tensor_tensor(xr[:, r, :], tmp[:, 4 + r % 2, :], 1.0, G[r % 2][:], ALU.add, ALU.mult).then_inc(r_done, 1)
                    dve.wait_ge(ot_copied, UP + b * 8 + 8)
                    dve.wait_ge(r_done, UP + b * 8 + 8)

                    def rest_of_y(c):
                        dve.wait_ge(y_hi, UP + b * 8 + c + 1)
                        dve.tensor_tensor(a_lo[:, c, :], xr[:, c, :], a_hi[:, c, :].bitcast(F32), ALU.subtract).then_inc(y_lo, 1)
                    for c in range(KT):
                        dve.scalar_tensor_tensor(xr[:, c, :], xr[:, c, :], keep["half_gn"][:, c % 2:c % 2 + 1], o_t[:, c, :],
                                                 ALU.mult, ALU.mult).then_inc(y_done, 1)
                        if c:
                            rest_of_y(c - 1)
                    rest_of_y(KT - 1)
                    for c in range(KT):
                        dve.wait_ge(proj, UP + b * NW + NPROJ + c + 1)
                        dve.wait_ge(xr_copied, UP + b * 8 + c + 1)
                        dve.scalar_tensor_tensor(o_t[:, c, :], G[c % 2][:], modv[:, 0, 16 + c:17 + c], tmp[:, 2 + c % 2, :],
                                                 ALU.mult, ALU.add).then_inc(x1, 1)
                        if c == 5:
                            norm_x(b + 1)
                    split_h(b + 1)
                    dve.wait_ge(sqs, UP + b * 8 + 8)
                    dve.tensor_scalar(eb[:, 0, :], A[:], 1.0 / D, EPS, ALU.mult, ALU.add).then_inc(tv, 1)
                    dve.wait_ge(trs0, UP + b + 1)
                    newton_rsqrt(dve, eb[:, 1, :], eb[:, 0, :], eb[:, 2, :], trs_step, b * 4)
                    dve.wait_ge(trs_step, UP + b * 4 + 4)
                    for c in range(KT):
                        dve.scalar_tensor_tensor(o_t[:, c, :], o_t[:, c, :], col("final_g")[:, c:c + 1], eb[:, 1, :],
                                                 ALU.mult, ALU.mult).then_inc(h1, 1)
                dve.wait_ge(h1, UP + 8 * NB)


HD, NQH, NKV = 64, 8, 2
KEYS, CTX = SEQ + 256, 256
COL_Q, COL_K, COL_V, COL_ZA, COL_A, COL_G, COL_ZC = 0, 512, 640, 768, 1280, 1792, 2304
TAPS, PAD = 31, 15
LAG = 16
CONV_AT = TB + LAG


def context_keys(nc, d, keep):
    NC = CTX // P
    with ExitStack() as ctx:
        sb, ps, sem = pools(nc, ctx, "ctx")
        cols, modv, gains, ident = keep["cols"], keep["modv"], keep["gains"], keep["ident"]
        xc = sb("xc", [P, NC, D])
        w = sb("w", [P, KT, 2 * P])
        w_hi, w_lo = sb("w_hi", [P, KT, 2 * P], F32R), sb("w_lo", [P, KT, 2 * P], F32R)
        u = sb("u", [P, KT, CTX])
        u_hi, u_lo = sb("u_hi", [P, KT, CTX], F32R), sb("u_lo", [P, KT, CTX], F32R)
        st = sb("st", [P, 4, NC])
        junk = sb("junk", [P, NC, D])
        head_ones = sb("head_ones", [P, P])
        kraw, ksq, kms, krs, kt = (sb(n, [P, CTX]) for n in ("kraw", "ksq", "kms", "krs", "kt"))
        vraw, vout = sb("vraw", [P, CTX]), sb("vout", [P, NC, P])
        XT = [ps(f"bank_xt{i}", [P, 512]) for i in range(2)]
        BK, BV, BS, BT = (ps(n, [P, 512]) for n in ("bank_k", "bank_v", "bank_s", "bank_t"))
        landed, w_landed, ones_landed = sem("landed"), sem("w_landed"), sem("ones_landed")
        sq, ms, ln, rs0, step, xn, xt, um, hi, lo = (sem(n) for n in ("sq", "ms", "ln", "rs0", "step", "xn", "xt", "um", "hi", "lo"))
        whi, wlo, k_done, v_done, k_read, v_read, ssum, kstep, k_out, vt, v_out, stored = (
            sem(n) for n in ("whi", "wlo", "k_done", "v_done", "k_read", "v_read", "ssum", "kstep", "k_out", "vt", "v_out", "stored"))
        at_kw = VROWS["k_norm_w_2"][0]
        nc.all_engine_barrier()
        with nc.Block() as block:
            @block.sync
            def _(sp):
                sp.dma_start(xc[:], d["ctx_2"].rearrange("(t p) n -> p t n", p=P)).then_inc(landed, 16)
                sp.dma_start(w[:], d["w_in_2"].rearrange("(k p) n -> p k n", p=P)[:, :, COL_K:COL_ZA]).then_inc(w_landed, 16)
                sp.dma_start(head_ones[:], d["head_ones"]).then_inc(ones_landed, 16)
                sp.wait_ge(k_out, UP + 1)
                sp.dma_start(d["kt"][:, 0:CTX], kraw[:]).then_inc(stored, 16)
                sp.wait_ge(v_out, UP + 1)
                sp.dma_start(d["vtok"].rearrange("(t p) n -> p t n", p=P)[:, 0:NC, :], vout[:]).then_inc(stored, 16)
                sp.wait_ge(stored, UP + 32)

            @block.scalar
            def _(act):
                act.wait_ge(landed, UP + 16)
                for t in range(NC):
                    act.activation(junk[:, t, :], xc[:, t, :], ACT.Square, accum_out=st[:, 0, t:t + 1]).then_inc(sq, 1)
                act.wait_ge(w_landed, UP + 16)
                act.activation(w_hi[:], w[:], ACT.Copy).then_inc(whi, 1)
                act.wait_ge(ms, UP + 1)
                act.activation(st[:, 2, :], st[:, 1, :], ACT.Ln).then_inc(ln, 1)
                act.wait_ge(ln, UP + 1)
                act.activation(st[:, 2, :], st[:, 2, :], ACT.Exp, scale=-0.5).then_inc(rs0, 1)
                for c in range(KT):
                    act.wait_ge(xt, UP + c + 1)
                    act.activation(u[:, c, :], XT[c % 2][:, 0:CTX], ACT.Identity, bias=modv[:, 2, c:c + 1],
                                   scale=gains[:, 2, c:c + 1]).then_inc(um, 1)
                act.wait_ge(k_done, UP + 1)
                act.activation(ksq[:], BK[:, 0:CTX], ACT.Square).then_inc(k_read, 1)
                act.activation(kraw[:], BK[:, 0:CTX], ACT.Copy).then_inc(k_read, 1)
                act.wait_ge(v_done, UP + 1)
                act.activation(vraw[:], BV[:, 0:CTX], ACT.Copy).then_inc(v_read, 1)
                act.wait_ge(kstep, UP + 1)
                act.activation(krs[:], kms[:], ACT.Ln).then_inc(ln, 1)
                act.wait_ge(ln, UP + 2)
                act.activation(krs[:], krs[:], ACT.Exp, scale=-0.5).then_inc(rs0, 1)
                act.wait_ge(vt, UP + 1)
                act.activation(vout[:], BT[:, 0:CTX].rearrange("p (t i) -> p t i", t=NC), ACT.Copy).then_inc(v_out, 1)

            @block.vector
            def _(dve):
                dve.wait_ge(sq, UP + NC)
                dve.tensor_scalar(st[:, 1, :], st[:, 0, :], 1.0 / D, EPS, ALU.mult, ALU.add).then_inc(ms, 1)
                dve.wait_ge(whi, UP + 1)
                dve.tensor_tensor(w_lo[:], w[:], w_hi[:].bitcast(F32), ALU.subtract).then_inc(wlo, 1)
                dve.wait_ge(rs0, UP + 1)
                newton_rsqrt(dve, st[:, 2, :], st[:, 1, :], st[:, 3, :], step, 0)
                dve.wait_ge(step, UP + 4)
                for t in range(NC):
                    dve.tensor_scalar(xc[:, t, :], xc[:, t, :], st[:, 2, t:t + 1], None, ALU.mult).then_inc(xn, 1)
                for c in range(KT):
                    dve.wait_ge(um, UP + c + 1)
                    dve.tensor_copy(u_hi[:, c, :], u[:, c, :]).then_inc(hi, 1)
                    dve.wait_ge(hi, UP + c + 1)
                    dve.tensor_tensor(u_lo[:, c, :], u[:, c, :], u_hi[:, c, :].bitcast(F32), ALU.subtract).then_inc(lo, 1)
                dve.wait_ge(ssum, UP + 1)
                dve.tensor_scalar(kms[:], BS[:, 0:CTX], 1.0 / HD, EPS, ALU.mult, ALU.add).then_inc(kstep, 1)
                dve.wait_ge(rs0, UP + 2)
                newton_rsqrt(dve, krs[:], kms[:], kt[:], step, 4)
                dve.wait_ge(step, UP + 8)
                dve.wait_ge(k_read, UP + 2)
                dve.scalar_tensor_tensor(kraw[:], kraw[:], cols[:, at_kw:at_kw + 1], krs[:], ALU.mult, ALU.mult).then_inc(k_out, 1)

            @block.tensor
            def _(pe):
                pe.wait_ge(xn, UP + NC)
                for c in range(KT):
                    if c >= 2:
                        pe.wait_ge(um, UP + c - 1)
                    for t in range(NC):
                        last = pe.transpose(XT[c % 2][:, P * t:P * (t + 1)], xc[:, t, P * c:P * (c + 1)], ident[:])
                    last.then_inc(xt, 1)
                pe.wait_ge(wlo, UP + 1)
                for bank, done, col0 in ((BK, k_done, 0), (BV, v_done, P)):
                    for k in range(KT):
                        pe.wait_ge(lo, UP + k + 1)
                        for n, (a, b) in enumerate(((w_hi, u_hi), (w_hi, u_lo), (w_lo, u_hi))):
                            last = pe.matmul(bank[:, 0:CTX], a[:, k, col0:col0 + P], b[:, k, :], start=(k == 0 and n == 0),
                                             stop=(k == KT - 1 and n == 2))
                    last.then_inc(done, 1)
                pe.wait_ge(ones_landed, UP + 16)
                pe.wait_ge(k_read, UP + 1)
                pe.matmul(BS[:, 0:CTX], head_ones[:], ksq[:], start=True, stop=True).then_inc(ssum, 1)
                pe.wait_ge(v_read, UP + 1)
                for t in range(NC):
                    last = pe.transpose(BT[:, P * t:P * (t + 1)], vraw[:, P * t:P * (t + 1)], ident[:])
                last.then_inc(vt, 1)


def projections(nc, d, keep):
    NW = 22
    COLS = ([c for i in range(4) for c in (COL_A + P * i, COL_G + P * i)] + [COL_Q + P * i for i in range(4)] + [COL_K, COL_V]
            + [COL_ZA + P * i for i in range(4)] + [COL_ZC + P * i for i in range(4)])
    NTAP = 4 * TAPS
    with ExitStack() as ctx:
        sb, ps, sem = pools(nc, ctx, "proj")
        cols, modv, gains, ident = keep["cols"], keep["modv"], keep["gains"], keep["ident"]
        u_hi = [sb(f"u_hi{i}", [P, KT, TB], F32R) for i in range(2)]
        u_lo = [sb(f"u_lo{i}", [P, KT, TB], F32R) for i in range(2)]
        hbuf = sb("hbuf", [P, KT, TB])
        w_raw = [sb(f"w_raw{s}", [P, KT, P]) for s in range(4)]
        w_hi = [sb(f"w_hi{s}", [P, KT, P], F32R) for s in range(2)]
        w_lo = [sb(f"w_lo{s}", [P, KT, P], F32R) for s in range(2)]
        UB = 2 * LAG
        conv_in = sb("conv_in", [P, 4, UB + SEQ + PAD])
        CW = TB + LAG
        conv_acc = sb("conv_acc", [P, 4, CW])
        conv_w = sb("conv_w", [P, 4, TAPS])
        conv_rows = sb("conv_rows", [TAPS, TB])
        rot_t, head_ones, ones = sb("rot_t", [P, P]), sb("head_ones", [P, P]), sb("ones", [P, P])
        cos, sin = sb("cos", [P, TB]), sb("sin", [P, TB])
        ga, gt = sb("ga", [P, 2, TB]), sb("gt", [P, 2, TB])
        qraw = sb("qraw", [P, 6, TB])
        qsq = sb("qsq", [P, TB])        
        qms, qrs, qt = sb("qms", [P, TB]), sb("qrs", [P, TB]), sb("qt", [P, TB])
        G = [ps(f"bank_g{i}", [P, TB]) for i in range(2)]
        BN, BS, BR, BV = (ps(n, [P, TB]) for n in ("bank_n", "bank_s", "bank_r", "bank_v"))
        consts, cleared, conv_w_turned, conv_w_done = (sem(n) for n in ("consts", "cleared", "conv_w_turned", "conv_w_done"))
        w_landed = [sem(f"w_landed{s}") for s in range(4)]
        w_rest = [sem(f"w_rest{s}") for s in range(4)]
        w_rounded, proj, evac = sem("w_rounded"), sem("proj"), sem("evac")
        h_landed, hsq, nsum, nms, nln, nrs0, nstep, hm, u_done_hi, u_done = (
            sem(n) for n in ("h_landed", "hsq", "nsum", "nms", "nln", "nrs0", "nstep", "hm", "u_done_hi", "u_done"))
        glu, taps, conv_stored = sem("glu"), sem("taps"), sem("conv_stored")
        q_sq, q_sum, q_ms, q_ln, q_rs0, q_step, q_n, q_rot, q_sin, q_cos, q_done, q_stored, cs_landed = (
            sem(n) for n in ("q_sq", "q_sum", "q_ms", "q_ln", "q_rs0", "q_step", "q_n", "q_rot", "q_sin", "q_cos", "q_done", "q_stored", "cs_landed"))
        vt, v_out, v_stored, z_done = (sem(n) for n in ("vt", "v_out", "v_stored", "z_done"))
        z_stored = [sem(f"z_stored{i}") for i in range(2)]
        zout = sb("zout", [P, 2, TB])
        vraw, vout = qraw[:, 5, :], sb("vout", [P, NT, P])
        hms, hrs, ht = sb("hms", [P, TB]), sb("hrs", [P, TB]), sb("ht", [P, TB])
        hsquare = (ht, hms)
        spare = sb("spare", [P, 1])
        qsin = sb("qsin", [P, 2, TB])
        zraw = sem("zraw")

        w_in = d["w_in_2"].rearrange("(k p) n -> p k n", p=P)
        h1t = d["h1t"].rearrange("(c p) t -> p c t", p=P)
        conv_y = d["conv_y"].rearrange("(c p) t -> p c t", p=P)
        vtok = d["vtok"].rearrange("(t p) n -> p t n", p=P)

        nc.all_engine_barrier()
        with nc.Block() as block:
            @block.sync
            def _(sp):
                for dst, src in ((rot_t, "rot_t"), (head_ones, "head_ones"), (ones, "ones"), (conv_rows, "conv_w_2")):
                    sp.dma_start(dst[:], d[src]).then_inc(consts, 16)
                sp.dma_start(hbuf[:], h1t[:, :, 0:TB]).then_inc(h_landed, 16)

                def load(it, n):
                    s, r = n % 4, n // 4
                    sp.wait_ge(w_rest[s], UP + it * 11 + r)
                    sp.dma_start(w_raw[s][:], w_in[:, :, COLS[n % NW]:COLS[n % NW] + P]).then_inc(w_landed[s], 16)
                for n in range(4):
                    load(0, n)
                sp.wait_ge(cleared, UP + 3)
                sp.wait_ge(u_done, UP + 8)
                sp.dma_start(hbuf[:], h1t[:, :, TB:2 * TB]).then_inc(h_landed, 16)
                with sp.Fori(0, NB // 2) as it:
                    for half in range(2):
                        b = it * 2 + half
                        sp.wait_ge(q_done, UP + b * 5)
                        for dst, src in ((cos, "cos"), (sin, "sin")):
                            sp.dma_start(dst[:], d[src][:, ds(b * TB, TB)]).then_inc(cs_landed, 16)
                        for j in range(NW):
                            load(it, half * NW + j + 4)
                            if j == 20:
                                sp.wait_ge(u_done, UP + b * 8 + 16)
                                sp.dma_start(hbuf[:], h1t[:, :, ds(((b + 2) % NB) * TB, TB)]).then_inc(h_landed, 16)
                            if j == 2:
                                sp.wait_ge(taps, UP + b * NTAP)
                                sp.dma_start(conv_y[:, :, ds(b * TB, CW)], conv_acc[:]).then_inc(conv_stored, 16)
                            if 15 <= j < 20:
                                i = j - 15
                                sp.wait_ge(q_done, UP + b * 5 + i + 1)
                                dst = (d["qt"][P * i:P * (i + 1), ds(b * TB, TB)] if i < 4 else
                                       d["kt"][:, ds(b * TB + CTX, TB)])
                                sp.dma_start(dst, qraw[:, i, :]).then_inc(q_stored, 16)
                            if j == 18:
                                sp.wait_ge(v_out, UP + b + 1)
                                sp.dma_start(vtok[:, ds(b * NT + CTX // P, NT), :], vout[:]).then_inc(v_stored, 16)
                            if j >= 16:
                                for i in ((j - 16,) if j < NW - 1 else (5, 6, 7)):
                                    sp.wait_ge(z_done, UP + b * 8 + i + 1)
                                    dst = d["za" if i < 4 else "zc"][P * (i % 4):P * (i % 4 + 1), ds(b * TB, TB)]
                                    sp.dma_start(dst, zout[:, i % 2, :]).then_inc(z_stored[i % 2], 16)
                sp.wait_ge(taps, UP + NB * NTAP)
                sp.dma_start(conv_y[:, :, NB * TB:NB * TB + CW], conv_acc[:]).then_inc(conv_stored, 16)
                sp.wait_ge(conv_stored, UP + 16 * (NB + 1))
                sp.wait_ge(q_stored, UP + 16 * 5 * NB)
                sp.wait_ge(v_stored, UP + 16 * NB)
                for i in range(2):
                    sp.wait_ge(z_stored[i], UP + 16 * 4 * NB)
                sp.wait_ge(h_landed, UP + 16 * (NB + 2))
                for s in range(4):
                    sp.wait_ge(w_landed[s], UP + 16 * (11 * NB // 2 + 1))

            @block.gpsimd
            def _(pool):
                pool.memset(conv_in[:], 0.0).then_inc(cleared, 2)
                pool.memset(conv_acc[:], 0.0).then_inc(cleared, 1)

                def rest(it, n):
                    s = n % 4
                    pool.wait_ge(w_rounded, UP + it * 44 + n + 1)
                    pool.tensor_tensor(w_lo[n % 2][:], w_raw[s][:], w_hi[n % 2][:].bitcast(F32), ALU.subtract).then_inc(w_rest[s], 1)
                rest(0, 0)
                with pool.Fori(0, NB // 2) as it:
                    for n in range(44):
                        rest(it, n + 1)
                        b, j = it * 2 + n // NW, n % NW
                        if 13 <= j < 18:
                            i = j - 13
                            pool.wait_ge(q_sin, UP + b * 5 + i + 1)
                            pool.wait_ge(q_cos, UP + b * 5 + i + 1)
                            pool.tensor_tensor(qraw[:, i, :], qraw[:, i, :], qsin[:, i % 2, :], ALU.add).then_inc(q_done, 1)
                        if 12 <= j < 17:
                            i = j - 12
                            if i == 0:
                                pool.wait_ge(cs_landed, UP + b * 32 + 32)
                            pool.wait_ge(q_rot, UP + b * 5 + i + 1)
                            pool.tensor_tensor(qraw[:, i, :], qraw[:, i, :], cos[:], ALU.mult).then_inc(q_cos, 1)

            @block.tensor
            def _(pe):
                pe.wait_ge(consts, UP + 64)
                for c in range(4):
                    last = pe.transpose(BS[:, TAPS * c:TAPS * (c + 1)], conv_rows[:, P * c:P * (c + 1)], ident[0:TAPS, 0:TAPS])
                last.then_inc(conv_w_turned, 1)

                def sum_h(b, k):
                    if k == 0:
                        pe.wait_ge(nms, UP + b)
                    pe.wait_ge(hsq, UP + b * 8 + k + 1)
                    pe.matmul(BN[:], ones[:], hsquare[k % 2][:], start=(k == 0), stop=(k == KT - 1)).then_inc(nsum, 1)
                for k in range(KT):
                    sum_h(0, k)

                def turn(it, half, j):
                        b, n = it * 2 + half, half * NW + j
                        pe.wait_ge(w_rest[n % 4], UP + it * 11 + n // 4 + 1)
                        pe.wait_ge(evac, UP + b * NW + j)
                        for k in range(KT):
                            if j == 0:
                                pe.wait_ge(u_done, UP + b * 8 + k + 1)
                            for n, (w, a) in enumerate(((w_hi, u_hi), (w_hi, u_lo), (w_lo, u_hi))):
                                last = pe.matmul(G[j % 2][:], w[j % 2][:, k, :], a[half][:, k, :], start=(k == 0 and n == 0),
                                                 stop=(k == KT - 1 and n == 2))
                        last.then_inc(proj, 1)
                        if 11 <= j < 16:
                            pe.wait_ge(q_n, UP + b * 5 + j - 10)
                            pe.wait_ge(q_sin, UP + b * 5 + j - 11)
                            pe.matmul(BR[:], rot_t[:], qraw[:, j - 11, :], start=True, stop=True).then_inc(q_rot, 1)
                        if 9 <= j < 14:
                            pe.wait_ge(q_sq, UP + b * 5 + j - 8)
                            pe.wait_ge(q_ms, UP + b * 5 + j - 9)
                            pe.matmul(BS[:], head_ones[:], qsq[:], start=True, stop=True).then_inc(q_sum, 1)
                        if j == 15:
                            pe.wait_ge(evac, UP + b * NW + 15)
                            pe.wait_ge(v_out, UP + b)
                            for t in range(NT):
                                last = pe.transpose(BV[:, P * t:P * (t + 1)], vraw[:, P * t:P * (t + 1)], ident[:])
                            last.then_inc(vt, 1)
                        if 5 <= j < 5 + KT // 2:
                            for k in range(2 * (j - 5), 2 * (j - 5) + 2):
                                sum_h(b + 1, k)
                pe.wait_ge(conv_w_done, UP + 1)
                with pe.Fori(0, NB // 2) as it:
                    for half in range(2):
                        for j in range(NW):
                            turn(it, half, j)

            @block.scalar
            def _(act):
                def round_tile(it, n):
                    s = n % 4
                    act.wait_ge(w_landed[s], UP + it * 176 + 16 * (n // 4) + 16)
                    if n:
                        act.wait_ge(proj, UP + it * 44 + n - 1)
                    act.activation(w_hi[n % 2][:], w_raw[s][:], ACT.Copy).then_inc(w_rounded, 1)

                def square_h(b, k):
                    if k >= 2:
                        act.wait_ge(nsum, UP + b * 8 + k - 1)
                    act.activation(hsquare[k % 2][:], hbuf[:, k, :], ACT.Square).then_inc(hsq, 1)

                def rsqrt_h(b):
                    act.wait_ge(nms, UP + b + 1)
                    act.activation(hrs[:], hms[:], ACT.Ln).then_inc(nln, 1)
                    act.wait_ge(nln, UP + b + 1)
                    act.activation(hrs[:], hrs[:], ACT.Exp, scale=-0.5).then_inc(nrs0, 1)

                act.wait_ge(h_landed, UP + 16)
                round_tile(0, 0)
                for k in range(KT):
                    square_h(0, k)
                rsqrt_h(0)
                act.wait_ge(conv_w_turned, UP + 1)
                act.activation(conv_w[:].rearrange("p c k -> p (c k)"), BS[:, 0:NTAP], ACT.Copy, scale=0.5).then_inc(conv_w_done, 1)
                act.wait_ge(conv_w_done, UP + 1)
                act.activation(spare[:], conv_w[:, 0, 0:1], ACT.Copy).then_inc(evac, 1)
                with act.Fori(0, NB // 2) as it:
                    for half in range(2):
                        b = it * 2 + half
                        for j in range(NW):
                            round_tile(it, half * NW + j + 1)
                            if 10 <= j < 15:
                                act.wait_ge(q_ms, UP + b * 5 + j - 9)
                                act.wait_ge(q_n, UP + b * 5 + j - 10)
                                act.activation(qrs[:], qms[:], ACT.Ln).then_inc(q_ln, 1)
                                act.wait_ge(q_ln, UP + b * 5 + j - 9)
                                act.activation(qrs[:], qrs[:], ACT.Exp, scale=-0.5).then_inc(q_rs0, 1)
                            if 4 <= j < 4 + KT // 2:
                                if j == 4:
                                    act.wait_ge(h_landed, UP + b * 16 + 32)
                                    act.wait_ge(nstep, UP + b * 4 + 4)
                                for k in range(2 * (j - 4), 2 * (j - 4) + 2):
                                    square_h(b + 1, k)
                            act.wait_ge(proj, UP + b * NW + j + 1)
                            if j < 8:
                                if j >= 4:
                                    act.wait_ge(glu, UP + b * 4 + j // 2 - 1)
                                else:
                                    act.wait_ge(z_done, UP + b * 8)
                                if j % 2 == 0:
                                    act.activation(ga[:, j // 2 % 2, :], G[0][:], ACT.Copy).then_inc(evac, 1)
                                else:
                                    act.activation(gt[:, j // 2 % 2, :], G[1][:], ACT.Tanh, scale=0.5).then_inc(evac, 1)
                            elif j < 13:
                                i = j - 8
                                if i == 0:
                                    act.wait_ge(q_sum, UP + b * 5)
                                    act.wait_ge(q_stored, UP + b * 80)
                                else:
                                    act.wait_ge(q_sum, UP + b * 5 + i)
                                act.activation(qsq[:], G[j % 2][:], ACT.Square).then_inc(q_sq, 1)
                                act.activation(qraw[:, i, :], G[j % 2][:], ACT.Copy).then_inc(evac, 1)
                            elif j == 13:
                                act.activation(vraw, G[j % 2][:], ACT.Copy).then_inc(evac, 1)
                            else:
                                i = j - 14
                                if i < 2:
                                    act.wait_ge(glu, UP + b * 4 + 4)
                                else:
                                    act.wait_ge(z_done, UP + b * 8 + i - 1)
                                act.activation(ga[:, i % 2, :], G[j % 2][:], ACT.Copy).then_inc(zraw, 1)
                                act.activation(gt[:, i % 2, :], G[j % 2][:], ACT.Tanh, scale=0.5).then_inc(evac, 1)
                            if j == 9:
                                rsqrt_h(b + 1)
                            if j == 16:
                                act.wait_ge(vt, UP + b + 1)
                                act.wait_ge(v_stored, UP + b * 16)
                                act.activation(vout[:], BV[:].rearrange("p (t i) -> p t i", t=NT), ACT.Copy).then_inc(v_out, 1)

            @block.vector
            def _(dve):
                def mean_h(b):
                    dve.wait_ge(nsum, UP + b * 8 + 8)
                    dve.tensor_scalar(hms[:], BN[:], 1.0 / D, EPS, ALU.mult, ALU.add).then_inc(nms, 1)

                def rs_h(b):
                    dve.wait_ge(nrs0, UP + b + 1)
                    newton_rsqrt(dve, hrs[:], hms[:], ht[:], nstep, b * 4)
                    dve.wait_ge(nstep, UP + b * 4 + 4)

                def modulate_h(b, half, k):
                    dve.scalar_tensor_tensor(hbuf[:, k, :], hbuf[:, k, :], gains[:, 1, k:k + 1], hrs[:], ALU.mult, ALU.mult).then_inc(hm, 1)
                    dve.wait_ge(hm, UP + b * 8 + k + 1)
                    dve.tensor_scalar(u_hi[half][:, k, :], hbuf[:, k, :], modv[:, 1, k:k + 1], None, ALU.add).then_inc(u_done_hi, 1)
                    dve.wait_ge(u_done_hi, UP + b * 8 + k + 1)
                    dve.scalar_tensor_tensor(u_lo[half][:, k, :], hbuf[:, k, :], modv[:, 1, k:k + 1], u_hi[half][:, k, :].bitcast(F32),
                                             ALU.add, ALU.subtract).then_inc(u_done, 1)

                def tap(b, m):
                    k, c = m % (2 * TAPS) // 2, m // (2 * TAPS) * 2 + m % 2
                    src = conv_in[:, c, ds(b * TB + (UB - LAG - PAD + k), CW)]
                    if k == 0:
                        dve.tensor_scalar(conv_acc[:, c, :], src, conv_w[:, c, 0:1], None, ALU.mult).then_inc(taps, 1)
                    else:
                        dve.wait_ge(taps, UP + b * NTAP + m - 1)
                        dve.scalar_tensor_tensor(conv_acc[:, c, :], src, conv_w[:, c, k:k + 1], conv_acc[:, c, :], ALU.mult, ALU.add).then_inc(taps, 1)
                TAPS_OF_TURN = [0] * 4 + [10] * 4 + [8] * 2 + [4] * 6 + [8] * 4 + [6] * 2
                assert sum(TAPS_OF_TURN) == NTAP and sum(TAPS_OF_TURN[:8]) <= 2 * TAPS
                at_qw, at_kw = VROWS["q_norm_w_2"][0], VROWS["k_norm_w_2"][0]
                mean_h(0)
                rs_h(0)
                for k in range(KT):
                    modulate_h(0, 0, k)
                dve.wait_ge(cleared, UP + 3)
                dve.wait_ge(conv_w_done, UP + 1)
                with dve.Fori(0, NB // 2) as it:
                    for half in range(2):
                        b = it * 2 + half
                        m = 0
                        for j in range(NW):
                            if j < 8 and j % 2:
                                dve.wait_ge(evac, UP + b * NW + j + 2)
                                dve.scalar_tensor_tensor(conv_in[:, j // 2, ds(b * TB + UB, TB)], gt[:, j // 2 % 2, :], 1.0, ga[:, j // 2 % 2, :],
                                                         ALU.add, ALU.mult).then_inc(glu, 1)
                            if 10 <= j < 15:
                                i = j - 10
                                dve.wait_ge(q_rs0, UP + b * 5 + i + 1)
                                newton_rsqrt(dve, qrs[:], qms[:], qt[:], q_step, b * 20 + i * 4)
                                dve.wait_ge(q_step, UP + b * 20 + i * 4 + 4)
                                at = at_qw if i < 4 else at_kw
                                dve.scalar_tensor_tensor(qraw[:, i, :], qraw[:, i, :], cols[:, at:at + 1], qrs[:], ALU.mult, ALU.mult).then_inc(q_n, 1)
                            if 12 <= j < 17:
                                i = j - 12
                                if i == 0:
                                    dve.wait_ge(cs_landed, UP + b * 32 + 32)
                                dve.wait_ge(q_rot, UP + b * 5 + i + 1)
                                if i < 2:
                                    dve.wait_ge(q_done, UP + b * 5)
                                else:
                                    dve.wait_ge(q_done, UP + b * 5 + i - 1)
                                dve.tensor_tensor(qsin[:, i % 2, :], BR[:], sin[:], ALU.mult).then_inc(q_sin, 1)
                            if 9 <= j < 14:
                                dve.wait_ge(q_sum, UP + b * 5 + j - 8)
                                dve.tensor_scalar(qms[:], BS[:], 1.0 / HD, EPS, ALU.mult, ALU.add).then_inc(q_ms, 1)
                            if j == 9:
                                mean_h(b + 1)
                            if j == 11:
                                rs_h(b + 1)
                                dve.wait_ge(proj, UP + b * NW)
                            if 12 <= j < 12 + KT:
                                modulate_h(b + 1, 1 - half, j - 12)
                            if j >= 14:
                                i = j - 14
                                dve.wait_ge(zraw, UP + b * 8 + i + 1)
                                dve.wait_ge(evac, UP + b * NW + j + 2)
                                dve.wait_ge(z_stored[i % 2], UP + b * 64 + 16 * (i // 2))
                                dve.scalar_tensor_tensor(zout[:, i % 2, :], gt[:, i % 2, :], 1.0, ga[:, i % 2, :], ALU.add, ALU.mult).then_inc(z_done, 1)
                            if j == 4:
                                dve.wait_ge(glu, UP + b * 4 + 2)
                                dve.wait_ge(conv_stored, UP + b * 16 + 16)
                            if j == 8:
                                dve.wait_ge(glu, UP + b * 4 + 4)
                            for _ in range(TAPS_OF_TURN[j]):
                                tap(b, m)
                                m += 1


def attention(nc, d, keep):
    NKT = KEYS // P
    RING, SBANKS = 6, 3
    WEIGH_LAG, SPLIT_LAG = 5, 2
    GROUP_STEPS = (NQH // NKV) * NB
    STEPS = NKV * GROUP_STEPS
    PIECES = [(qt, n) for qt in range(NT) for n in range(-(-KEYS // TB))]
    NP = len(PIECES)
    TURN_PIECES = [[] for _ in range(NKT)]
    for p in range(NP):
        TURN_PIECES[2 + p * 13 // NP].append(p)
    with ExitStack() as ctx:
        sb, ps, sem = pools(nc, ctx, "att")
        ident = keep["ident"]
        k_a = [sb(f"k_a{g}", [P, KEYS], F32R) for g in range(NKV)]
        k_b = [sb(f"k_b{g}", [HD + 1, KEYS], F32R) for g in range(NKV)]
        v_s = [sb(f"v_s{g}", [P, NKT, P], F32R) for g in range(NKV)]
        k_raw = sb("k_raw", [P, KEYS])
        v_raw = sb("v_raw", [P, NKT, HD])
        ones = sb("ones", [P, P])
        q_raw = [sb(f"q_raw{s}", [P, TB]) for s in range(2)]
        q_a = [sb(f"q_a{s}", [P, TB], F32R) for s in range(2)]
        q_b = [sb(f"q_b{s}", [HD + 1, TB], F32R) for s in range(2)]
        mx = sb("mx", [P, NT, 5])
        m = sb("m", [P, NT])
        mz = sb("mz", [P, NT, HD + 1])
        p_f = sb("p_f", [P, RING, TB])
        p_hi = sb("p_hi", [P, RING, TB], F32R)
        p_lo = sb("p_lo", [P, RING, TB], F32R)
        den = [sb(f"den{s}", [P, TB]) for s in range(2)]
        o_hi, o_out = sb("o_hi", [HD, TB]), sb("o_out", [HD, TB])
        recip = sb("recip", [P, NT])
        S = [ps(f"bank_s{i}", [P, TB]) for i in range(SBANKS)]
        M = [ps(f"bank_m{i}", [P, TB]) for i in range(2)]
        O = [ps(f"bank_o{i}", [P, TB]) for i in range(2)]
        B = ps("bank_b", [P, TB])
        (k_landed, v_landed, ones_landed, k_hi_done, k_lo_done, v_hi_done, v_lo_done, cleared, ones_row) = (
            sem(n) for n in ("k_landed", "v_landed", "ones_landed", "k_hi_done", "k_lo_done", "v_hi_done", "v_lo_done", "cleared", "ones_row"))
        loads_begun = sem("loads_begun")
        q_landed = [sem(f"q_landed{s}") for s in range(2)]
        q_hi_done, q_lo_done = sem("q_hi_done"), sem("q_lo_done")
        mx_done, mx_read, m_done, mz_done, row_done, row_read = (
            sem(n) for n in ("mx_done", "mx_read", "m_done", "mz_done", "row_done", "row_read"))
        s_done, p_done, hi_done, lo_done, den_done, pv_done = (
            sem(n) for n in ("s_done", "p_done", "hi_done", "lo_done", "den_done", "pv_done"))
        den_sum, o_hi_done, recip_done, r_row, o_sum, o_done, o_stored = (
            sem(n) for n in ("den_sum", "o_hi_done", "recip_done", "r_row", "o_sum", "o_done", "o_stored"))

        def need(eng, semaphore, n):
            if isinstance(n, int) and n <= 0:
                return
            eng.wait_ge(semaphore, UP + n)

        def steps(eng, body):
            last = GROUP_STEPS - 1
            for g in range(NKV):
                base = g * GROUP_STEPS
                body(base, 0, g, g - 1 if g else None, g)
                body(base + 1, 1, g, g, g)
                with eng.Fori(1, GROUP_STEPS // 2 - 1) as it:
                    for s in range(2):
                        body(it * 2 + (base + s), s, g, g, g)
                body(base + last - 1, 0, g, g, g)
                body(base + last, 1, g, g, g + 1 if g + 1 < NKV else None)

        nc.all_engine_barrier()
        with nc.Block() as block:
            @block.sync
            def _(sp):
                sp.dma_start(ones[:], d["ones"]).then_inc(ones_landed, 16)

                def load_q(i, s):
                    row, col = (i // NB) * HD, (i % NB) * TB
                    for half in range(2):
                        sp.dma_start(q_raw[s][HD * half:HD * (half + 1), :], d["qt"][ds(row, HD), ds(col, TB)]).then_inc(q_landed[s], 16)
                load_q(0, 0)
                load_q(1, 1)
                for g in range(NKV):
                    if g:
                        sp.wait_ge(k_lo_done, UP + g)
                        sp.wait_ge(k_hi_done, UP + g)
                    for half in range(2):
                        sp.dma_start(k_raw[HD * half:HD * (half + 1), :], d["kt"][HD * g:HD * (g + 1), :]).then_inc(k_landed, 16)
                    if g:
                        sp.wait_ge(v_lo_done, UP + g)
                    sp.dma_start(v_raw[:], d["vtok"].rearrange("(t p) n -> p t n", p=P)[:, :, HD * g:HD * (g + 1)]).then_inc(v_landed, 16)

                def body(i, s, g, before, after):
                    if not (isinstance(i, int) and i + 2 >= STEPS):
                        sp.wait_ge(q_hi_done, UP + 2 * i + 2)
                        sp.sem_inc(loads_begun, 1)
                        sp.wait_ge(q_lo_done, UP + i + 1)
                        sp.sem_inc(loads_begun, 1)
                        load_q(i + 2, s)
                    if before is not None:
                        sp.wait_ge(o_done, UP + i)
                        sp.dma_start(d["att"][ds(((i - 1) // NB) * HD, HD), ds(((i - 1) % NB) * TB, TB)], o_out[:]).then_inc(o_stored, 16)
                steps(sp, body)
                sp.wait_ge(o_done, UP + STEPS)
                sp.dma_start(d["att"][HD * (NQH - 1):HD * NQH, TB * (NB - 1):TB * NB], o_out[:]).then_inc(o_stored, 16)
                sp.wait_ge(o_stored, UP + 16 * STEPS)

            @block.gpsimd
            def _(pool):
                pool.memset(mz[:], 0.0).then_inc(cleared, 1)

                def body(i, s, g, before, after):
                    need(pool, den_sum, i - 1)
                    for kt in range(1, NKT):
                        pool.wait_ge(p_done, UP + i * NKT + kt + 1)
                        if kt > 1:
                            pool.wait_ge(den_done, UP + i * (NKT - 1) + kt - 1)
                        pool.tensor_tensor(den[s][:], p_f[:, 0, :] if kt == 1 else den[s][:], p_f[:, kt % RING, :], ALU.add).then_inc(den_done, 1)
                steps(pool, body)

            @block.tensor
            def _(pe):
                def piece(i, s, g, p):
                    qt, n = PIECES[p]
                    width = min(TB, KEYS - TB * n)
                    if p == 0:
                        pe.wait_ge(q_hi_done, UP + 2 * i + 2)
                        pe.wait_ge(q_lo_done, UP + i + 1)
                    need(pe, mx_read, i * NP + p - 1)
                    pe.matmul(M[p % 2][:, 0:width], q_a[s][:, P * qt:P * (qt + 1)], k_a[g][:, TB * n:TB * n + width],
                              start=True, stop=True).then_inc(mx_done, 1)

                def max_row(i):
                    pe.wait_ge(mz_done, UP + i + 1)
                    need(pe, o_done, i - 1)
                    for qt in range(NT):
                        last = pe.matmul(B[0:HD + 1, P * qt:P * (qt + 1)], mz[:, qt, :], ident[:], start=True, stop=True)
                    last.then_inc(row_done, 1)

                def weigh(i, s, g, kt):
                    pe.wait_ge(lo_done, UP + i * NKT + kt + 1)
                    if kt == 0:
                        need(pe, o_sum, i - 1)
                    pe.matmul(O[s][:], v_s[g][:, kt, :], p_hi[:, kt % RING, :], start=(kt == 0), stop=False)
                    pe.matmul(O[s][:], v_s[g][:, kt, :], p_lo[:, kt % RING, :], start=False, stop=(kt == NKT - 1)).then_inc(pv_done, 1)

                def sum_den(i, s):
                    pe.wait_ge(den_done, UP + (i + 1) * (NKT - 1))
                    pe.wait_ge(row_read, UP + i + 1)
                    for qt in range(NT):
                        last = pe.matmul(B[:, qt:qt + 1], den[s][:, P * qt:P * (qt + 1)], ones[:, 0:1], start=True, stop=True)
                    last.then_inc(den_sum, 1)

                def spread_reciprocal(i):
                    pe.wait_ge(recip_done, UP + i + 1)
                    for qt in range(NT):
                        last = pe.matmul(B[0:HD, P * qt:P * (qt + 1)], recip[:, qt:qt + 1].broadcast_to([P, HD]), ident[:],
                                         start=True, stop=True)
                    last.then_inc(r_row, 1)

                def body(i, s, g, before, after):
                    pe.wait_ge(row_read, UP + i + 1)
                    for kt in range(NKT):
                        need(pe, p_done, i * NKT + kt - SBANKS + 1)
                        keys = slice(P * kt, P * (kt + 1))
                        pe.matmul(S[kt % SBANKS][:], k_a[g][:, keys], q_a[s][:], start=True, stop=False)
                        pe.matmul(S[kt % SBANKS][:], k_b[g][:, keys], q_b[s][:], start=False, stop=True).then_inc(s_done, 1)
                        if kt >= WEIGH_LAG:
                            weigh(i, s, g, kt - WEIGH_LAG)
                        elif before is not None:
                            weigh(i - 1, 1 - s, before, NKT - WEIGH_LAG + kt)
                        if kt == 4 and before is not None:
                            sum_den(i - 1, 1 - s)
                        if kt == 6 and before is not None:
                            spread_reciprocal(i - 1)
                        if after is not None:
                            for p in TURN_PIECES[kt]:
                                piece(i + 1, 1 - s, after, p)
                            if kt == 16:
                                max_row(i + 1)
                pe.wait_ge(ones_landed, UP + 16)
                pe.wait_ge(cleared, UP + 1)
                pe.wait_ge(k_lo_done, UP + NKV)
                pe.wait_ge(v_lo_done, UP + NKV)
                pe.wait_ge(ones_row, UP + NKV)
                for p in range(NP):
                    piece(0, 0, 0, p)
                max_row(0)
                steps(pe, body)
                for kt in range(NKT - WEIGH_LAG, NKT):
                    weigh(STEPS - 1, 1, NKV - 1, kt)
                sum_den(STEPS - 1, 1)
                spread_reciprocal(STEPS - 1)

            @block.scalar
            def _(act):
                for g in range(NKV):
                    act.wait_ge(k_landed, UP + 32 * g + 32)
                    act.activation(k_a[g][:], k_raw[:], ACT.Copy).then_inc(k_hi_done, 1)
                    act.wait_ge(v_landed, UP + 16 * g + 16)
                    act.activation(v_s[g][:, :, 0:HD], v_raw[:], ACT.Copy).then_inc(v_hi_done, 1)

                def round_q(i, s):
                    act.wait_ge(q_landed[s], UP + 32 * (i // 2) + 32)
                    need(act, s_done, (i - 1) * NKT)
                    for dst, rows in ((q_a[s], P), (q_b[s], HD)):
                        act.activation(dst[0:rows, :], q_raw[s][0:rows, :], ACT.Copy).then_inc(q_hi_done, 1)

                def read_row(i, s):
                    act.wait_ge(row_done, UP + i + 1)
                    act.activation(q_b[s][HD:HD + 1, :], B[HD:HD + 1, :], ACT.Copy).then_inc(row_read, 1)

                def round_p(i, kt):
                    act.wait_ge(p_done, UP + i * NKT + kt + 1)
                    need(act, pv_done, i * NKT + kt - RING + 1)
                    act.activation(p_hi[:, kt % RING, :], p_f[:, kt % RING, :], ACT.Copy).then_inc(hi_done, 1)

                def finish(i, s):
                    act.wait_ge(pv_done, UP + (i + 1) * NKT)
                    need(act, o_done, i)
                    act.activation(o_hi[:], O[s][HD:P, :], ACT.Copy).then_inc(o_hi_done, 1)

                def body(i, s, g, before, after):
                    for kt in range(NKT):
                        act.wait_ge(s_done, UP + i * NKT + kt + 1)
                        need(act, lo_done, i * NKT + kt - RING + 1)
                        used = 1 if kt == RING else kt - RING + (kt < RING)
                        need(act, den_done, i * (NKT - 1) + used)
                        act.activation(p_f[:, kt % RING, :], S[kt % SBANKS][:], ACT.Exp, scale=float(HD) ** -0.5).then_inc(p_done, 1)
                        if kt:
                            round_p(i, kt - 1)
                        elif before is not None:
                            round_p(i - 1, NKT - 1)
                        if kt == 0 and after is not None:
                            round_q(i + 1, 1 - s)
                        if kt == 7 and before is not None:
                            finish(i - 1, 1 - s)
                        if kt == 16 and after is not None:
                            read_row(i + 1, 1 - s)
                round_q(0, 0)
                read_row(0, 0)
                steps(act, body)
                round_p(STEPS - 1, NKT - 1)
                finish(STEPS - 1, 1)

            @block.vector
            def _(dve):
                dve.wait_ge(ones_landed, UP + 16)
                for g in range(NKV):
                    for t in range(NKT):
                        last = dve.tensor_copy(k_b[g][HD:HD + 1, P * t:P * (t + 1)], ones[HD:HD + 1, :])
                    last.then_inc(ones_row, 1)
                    dve.wait_ge(k_hi_done, UP + g + 1)
                    dve.tensor_tensor(k_b[g][0:HD, :], k_raw[0:HD, :], k_a[g][0:HD, :].bitcast(F32), ALU.subtract).then_inc(k_lo_done, 1)
                    dve.wait_ge(v_hi_done, UP + g + 1)
                    dve.tensor_tensor(v_s[g][:, :, HD:P], v_raw[:], v_s[g][:, :, 0:HD].bitcast(F32), ALU.subtract).then_inc(v_lo_done, 1)

                def split_q(i, s):
                    dve.wait_ge(q_hi_done, UP + 2 * i + 2)
                    dve.tensor_tensor(q_a[s][HD:P, :], q_raw[s][HD:P, :], q_a[s][HD:P, :].bitcast(F32), ALU.subtract).then_inc(q_lo_done, 1)

                def reduce(i, p):
                    qt, n = PIECES[p]
                    dve.wait_ge(mx_done, UP + i * NP + p + 1)
                    if p == 0:
                        need(dve, m_done, i)
                    dve.reduce_max(mx[:, qt, n:n + 1], M[p % 2][:, 0:min(TB, KEYS - TB * n)], AX_X).then_inc(mx_read, 1)

                def column(i):
                    dve.wait_ge(mx_read, UP + (i + 1) * NP)
                    need(dve, mz_done, i)
                    dve.reduce_max(m[:], mx[:], AX_X).then_inc(m_done, 1)
                    dve.wait_ge(m_done, UP + i + 1)
                    dve.wait_ge(cleared, UP + 1)
                    need(dve, row_done, i)
                    dve.tensor_scalar(mz[:, :, HD], m[:], -1.0, None, ALU.mult).then_inc(mz_done, 1)

                def split_p(i, kt):
                    dve.wait_ge(hi_done, UP + i * NKT + kt + 1)
                    need(dve, pv_done, i * NKT + kt - RING + 1)
                    dve.tensor_tensor(p_lo[:, kt % RING, :], p_f[:, kt % RING, :], p_hi[:, kt % RING, :].bitcast(F32), ALU.subtract).then_inc(lo_done, 1)

                def finish(i, s):
                    dve.wait_ge(o_hi_done, UP + i + 1)
                    dve.tensor_tensor(o_hi[:], O[s][0:HD, :], o_hi[:], ALU.add).then_inc(o_sum, 1)
                    dve.wait_ge(r_row, UP + i + 1)
                    dve.wait_ge(o_sum, UP + i + 1)
                    need(dve, o_stored, 16 * i)
                    dve.tensor_tensor(o_out[:], o_hi[:], B[0:HD, :], ALU.mult).then_inc(o_done, 1)

                def invert(i):
                    dve.wait_ge(den_sum, UP + i + 1)
                    need(dve, r_row, i)
                    dve.reciprocal(recip[:], B[:, 0:NT]).then_inc(recip_done, 1)

                def body(i, s, g, before, after):
                    for kt in range(NKT):
                        if kt >= SPLIT_LAG:
                            split_p(i, kt - SPLIT_LAG)
                        elif before is not None:
                            split_p(i - 1, NKT - SPLIT_LAG + kt)
                        if kt == 0 and after is not None:
                            split_q(i + 1, 1 - s)
                        if after is not None:
                            for p in TURN_PIECES[kt]:
                                reduce(i + 1, p)
                            if kt == 15:
                                column(i + 1)
                        if kt == 4 and before is not None:
                            invert(i - 1)
                        if kt == 10 and before is not None:
                            finish(i - 1, 1 - s)
                split_q(0, 0)
                for p in range(NP):
                    reduce(0, p)
                column(0)
                steps(dve, body)
                for kt in range(NKT - SPLIT_LAG, NKT):
                    split_p(STEPS - 1, kt)
                invert(STEPS - 1)
                finish(STEPS - 1, 1)


def output(nc, d, keep):
    NC = 4
    TILES = NC + KT
    with ExitStack() as ctx:
        sb, ps, sem = pools(nc, ctx, "out")
        cols, modv, ident = keep["cols"], keep["modv"], keep["ident"]

        def col(name, j):
            at = VROWS[name][0] + j
            return cols[:, at:at + 1]
        wo_hi, wo_lo = sb("wo_hi", [P, KT, D], F32R), sb("wo_lo", [P, KT, D], F32R)
        wp_hi, wp_lo = sb("wp_hi", [P, NC, TB], F32R), sb("wp_lo", [P, NC, TB], F32R)
        y = sb("y", [P, NC, TB])
        at = sb("at", [P, NC, TB])
        z = sb("z", [P, KT, TB])
        h1 = sb("h1", [P, KT, TB])
        c_hi, c_lo = sb("c_hi", [P, NC, TB], F32R), sb("c_lo", [P, NC, TB], F32R)
        f_hi, f_lo = sb("f_hi", [P, KT, TB], F32R), sb("f_lo", [P, KT, TB], F32R)
        sq = sb("sq", [P, TB])
        th = sb("th", [P, TB])
        rs = sb("rs", [P, TB])
        ob = sb("ob", [P, 2, NT, P])
        ones = sb("ones", [P, P])
        half_lnb = sb("half_lnb", [P, NC])
        w_raw = [h1[:].rearrange("p a b -> p (a b)")[:, D * i:D * (i + 1)] for i in range(4)]
        G = [ps(f"bank_g{i}", [P, TB]) for i in range(2)]
        T = [ps(f"bank_t{i}", [P, TB]) for i in range(2)]
        BM, BV = ps("bank_m", [P, TB]), ps("bank_v", [P, TB])
        w_landed = [sem(f"w_landed{i}") for i in range(4)]
        loads_begun = sem("loads_begun")
        ones_landed, w_hi_done, w_lo_done, lnb_done = (sem(n) for n in ("ones_landed", "w_hi_done", "w_lo_done", "lnb_done"))
        y_landed, at_landed, za_landed, zc_landed, h1_landed = (
            sem(n) for n in ("y_landed", "at_landed", "za_landed", "zc_landed", "h1_landed"))
        biased, mean_sum, centred, squared, var_sum, var_done, ln_done, rs0_done, rs_step, normed, tanh_done, shifted, swished, c_hi_done, c_lo_done = (
            sem(n) for n in ("biased", "mean_sum", "centred", "squared", "var_sum", "var_done", "ln_done", "rs0_done", "rs_step",
                             "normed", "tanh_done", "shifted", "swished", "c_hi_done", "c_lo_done"))
        prod, gated, f_hi_done, f_lo_done, x_out, turned, t_read = (
            sem(n) for n in ("prod", "gated", "f_hi_done", "f_lo_done", "x_out", "turned", "t_read"))
        stored = [sem(f"stored{i}") for i in range(2)]
        NWT = KT + 2

        def tiles(name):
            return d[name].rearrange("(c p) t -> p c t", p=P)

        nc.all_engine_barrier()
        with nc.Block() as block:
            @block.sync
            def _(sp):
                sp.dma_start(ones[:], d["ones"]).then_inc(ones_landed, 16)
                y_src = tiles("conv_y")
                sp.dma_start(y[:], y_src[:, :, CONV_AT:CONV_AT + TB]).then_inc(y_landed, 16)
                for n in range(NWT):
                    if n >= 4:
                        sp.wait_ge(w_lo_done, UP + n - 3)
                    if n < 2:
                        src = d["w_pw_2"].rearrange("(k p) n -> p k n", p=P)[:, 2 * n:2 * n + 2, :]
                        dst = w_raw[n % 4].rearrange("p (k n) -> p k n", k=2)
                    else:
                        src, dst = d["w_out_2"][P * (n - 2):P * (n - 1), :], w_raw[n % 4]
                    sp.dma_start(dst, src).then_inc(w_landed[n % 4], 16)
                sp.dma_start(at[:], tiles("att")[:, :, 0:TB]).then_inc(at_landed, 16)
                sp.dma_start(z[:, 0:NC, :], tiles("za")[:, :, 0:TB]).then_inc(za_landed, 16)
                sp.dma_start(z[:, NC:KT, :], tiles("zc")[:, :, 0:TB]).then_inc(zc_landed, 16)
                sp.wait_ge(w_lo_done, UP + NWT)
                sp.dma_start(h1[:], tiles("h1t")[:, :, 0:TB]).then_inc(h1_landed, 16)
                with sp.Fori(0, NB) as b:
                    nxt = sp.snap((b + 1) % NB)
                    sp.wait_ge(c_lo_done, UP + 4 * b + 4)
                    sp.sem_inc(loads_begun, 1)
                    sp.dma_start(y[:], y_src[:, :, ds(nxt * TB + CONV_AT, TB)]).then_inc(y_landed, 16)
                    sp.wait_ge(gated, UP + 8 * b + 4)
                    sp.sem_inc(loads_begun, 1)
                    sp.dma_start(at[:], tiles("att")[:, :, ds(nxt * TB, TB)]).then_inc(at_landed, 16)
                    sp.wait_ge(f_lo_done, UP + 8 * b + 8)
                    sp.sem_inc(loads_begun, 1)
                    sp.dma_start(z[:, 0:NC, :], tiles("za")[:, :, ds(nxt * TB, TB)]).then_inc(za_landed, 16)
                    sp.dma_start(z[:, NC:KT, :], tiles("zc")[:, :, ds(nxt * TB, TB)]).then_inc(zc_landed, 16)
                    out = d["out"].rearrange("(t p) n -> p t n", p=P)
                    for c in range(KT):
                        sp.wait_ge(t_read, UP + 8 * b + c + 1)
                        sp.sem_inc(loads_begun, 1)
                        sp.dma_start(out[:, ds(b * NT, NT), P * c:P * (c + 1)], ob[:, c % 2, :, :]).then_inc(stored[c % 2], 16)
                    sp.dma_start(h1[:], tiles("h1t")[:, :, ds(nxt * TB, TB)]).then_inc(h1_landed, 16)
                for i in range(2):
                    sp.wait_ge(stored[i], UP + 16 * 4 * NB)
                for s in (y_landed, at_landed, za_landed, zc_landed, h1_landed):
                    sp.wait_ge(s, UP + 16 * (NB + 1))

            @block.tensor
            def _(pe):
                def sums(b, bank, ready, src, done):
                    for k in range(NC):
                        pe.wait_ge(ready, UP + b * 4 + k + 1)
                        pe.matmul(bank[:], ones[:], src(k), start=(k == 0), stop=(k == NC - 1)).then_inc(done, 1)

                def turn_back(b, c):
                    pe.wait_ge(x_out, UP + 8 * b + c + 1)
                    if c >= 2:
                        pe.wait_ge(t_read, UP + 8 * b + c - 1)
                    else:
                        pe.wait_ge(t_read, UP + 8 * b)
                    for t in range(NT):
                        last = pe.transpose(T[c % 2][:, P * t:P * (t + 1)], h1[:, c, P * t:P * (t + 1)], ident[:])
                    last.then_inc(turned, 1)

                def product(b, n, kts, w_hi, w_lo, cols_of, a_hi, a_lo, ready):
                    if n < 2:
                        pe.wait_ge(x_out, UP + KT * b)
                    elif n < NC + 2:
                        pe.wait_ge(gated, UP + KT * b + NC + n - 1)
                    else:
                        pe.wait_ge(x_out, UP + KT * b + n - NC - 1)
                    for k in range(kts):
                        pe.wait_ge(ready, UP + b * kts + k + 1)
                        for i, (w, a) in enumerate(((w_hi, a_hi), (w_hi, a_lo), (w_lo, a_hi))):
                            last = pe.matmul(G[n % 2][:], w[:, k, cols_of], a[:, k, :], start=(k == 0 and i == 0),
                                             stop=(k == kts - 1 and i == 2))
                    last.then_inc(prod, 1)
                pe.wait_ge(ones_landed, UP + 16)
                sums(0, BM, biased, lambda k: y[:, k, :], mean_sum)
                sums(0, BV, squared, lambda k: sq[:], var_sum)
                pe.wait_ge(w_lo_done, UP + NWT)
                with pe.Fori(0, NB) as b:
                    for j in range(NC):
                        product(b, j, NC, wp_hi, wp_lo, slice(P * j, P * (j + 1)), c_hi, c_lo, c_lo_done)
                    for c in range(KT):
                        product(b, NC + c, KT, wo_hi, wo_lo, slice(P * c, P * (c + 1)), f_hi, f_lo, f_lo_done)
                        if c:
                            turn_back(b, c - 1)
                        if c == 1:
                            sums(b + 1, BM, biased, lambda k: y[:, k, :], mean_sum)
                        if c == 3:
                            sums(b + 1, BV, squared, lambda k: sq[:], var_sum)
                    turn_back(b, KT - 1)

            @block.scalar
            def _(act):
                def square_y(b):
                    for k in range(NC):
                        act.wait_ge(centred, UP + 4 * b + k + 1)
                        act.wait_ge(var_sum, UP + 4 * b + k)
                        act.activation(sq[:], y[:, k, :], ACT.Square).then_inc(squared, 1)

                def rsqrt_y(b):
                    act.wait_ge(var_done, UP + b + 1)
                    act.activation(rs[:], sq[:], ACT.Ln).then_inc(ln_done, 1)
                    act.wait_ge(ln_done, UP + b + 1)
                    act.activation(rs[:], rs[:], ACT.Exp, scale=-0.5).then_inc(rs0_done, 1)

                def tanh_y(b):
                    for k in range(NC):
                        act.wait_ge(normed, UP + 4 * b + k + 1)
                        act.wait_ge(swished, UP + 4 * b + k)
                        act.activation(th[:], y[:, k, :], ACT.Tanh, scale=0.5, bias=half_lnb[:, k:k + 1]).then_inc(tanh_done, 1)

                def round_y(b):
                    if not isinstance(b, int):
                        act.wait_ge(prod, UP + TILES * b - KT)
                    for k in range(NC):
                        act.wait_ge(swished, UP + 4 * b + k + 1)
                        act.activation(c_hi[:, k, :], y[:, k, :], ACT.Copy).then_inc(c_hi_done, 1)

                def read_turned(b, c):
                    act.wait_ge(turned, UP + 8 * b + c + 1)
                    act.wait_ge(stored[c % 2], UP + 64 * b + 16 * (c // 2))
                    act.activation(ob[:, c % 2, :, :], T[c % 2][:].rearrange("p (t i) -> p t i", t=NT), ACT.Copy).then_inc(t_read, 1)
                at0 = VROWS["conv_ln_b_2"][0]
                act.activation(half_lnb[:], cols[:, at0:at0 + NC], ACT.Copy, scale=0.5).then_inc(lnb_done, 1)
                act.wait_ge(lnb_done, UP + 1)
                for n in range(NWT):
                    act.wait_ge(w_landed[n % 4], UP + 16 * (n // 4) + 16)
                    dst = wp_hi[:, 2 * n:2 * n + 2, :] if n < 2 else wo_hi[:, n - 2, :]
                    src = w_raw[n % 4].rearrange("p (k n) -> p k n", k=2) if n < 2 else w_raw[n % 4]
                    act.activation(dst, src, ACT.Copy, scale=0.5).then_inc(w_hi_done, 1)
                square_y(0)
                rsqrt_y(0)
                tanh_y(0)
                round_y(0)
                with act.Fori(0, NB) as b:
                    act.wait_ge(prod, UP + TILES * b)
                    for k in range(KT):
                        act.wait_ge(gated, UP + 8 * b + k + 1)
                        act.activation(f_hi[:, k, :], z[:, k, :], ACT.Copy).then_inc(f_hi_done, 1)
                    for c in range(KT):
                        if c:
                            read_turned(b, c - 1)
                        if c == 2:
                            square_y(b + 1)
                        if c == 4:
                            rsqrt_y(b + 1)
                        if c == 5:
                            tanh_y(b + 1)
                        if c == 6:
                            round_y(b + 1)
                    read_turned(b, KT - 1)

            @block.vector
            def _(dve):
                def bias_y(b):
                    dve.wait_ge(y_landed, UP + 16 * b + 16)
                    for k in range(NC):
                        dve.tensor_scalar(y[:, k, :], y[:, k, :], col("conv_b_2", k), None, ALU.add).then_inc(biased, 1)

                def centre_y(b):
                    dve.wait_ge(mean_sum, UP + 4 * b + 4)
                    for k in range(NC):
                        dve.scalar_tensor_tensor(y[:, k, :], BM[:], -1.0 / TB, y[:, k, :], ALU.mult, ALU.add).then_inc(centred, 1)

                def var_y(b):
                    dve.wait_ge(var_sum, UP + 4 * b + 4)
                    dve.tensor_scalar(sq[:], BV[:], 1.0 / TB, EPS, ALU.mult, ALU.add).then_inc(var_done, 1)

                def norm_y(b):
                    dve.wait_ge(rs0_done, UP + b + 1)
                    newton_rsqrt(dve, rs[:], sq[:], th[:], rs_step, 4 * b)
                    dve.wait_ge(rs_step, UP + 4 * b + 4)
                    for k in range(NC):
                        dve.scalar_tensor_tensor(y[:, k, :], y[:, k, :], col("conv_ln_w_2", k), rs[:], ALU.mult, ALU.mult).then_inc(normed, 1)

                def swish_y(b):
                    for k in range(NC):
                        dve.wait_ge(tanh_done, UP + 4 * b + k + 1)
                        dve.tensor_scalar(y[:, k, :], y[:, k, :], col("conv_ln_b_2", k), None, ALU.add).then_inc(shifted, 1)
                        dve.wait_ge(shifted, UP + 4 * b + k + 1)
                        dve.scalar_tensor_tensor(y[:, k, :], th[:], 1.0, y[:, k, :], ALU.add, ALU.mult).then_inc(swished, 1)

                def rest_y(b):
                    for k in range(NC):
                        dve.wait_ge(c_hi_done, UP + 4 * b + k + 1)
                        dve.tensor_tensor(c_lo[:, k, :], y[:, k, :], c_hi[:, k, :].bitcast(F32), ALU.subtract).then_inc(c_lo_done, 1)

                def rest_f(b, k):
                    dve.wait_ge(f_hi_done, UP + 8 * b + k + 1)
                    dve.tensor_tensor(f_lo[:, k, :], z[:, k, :], f_hi[:, k, :].bitcast(F32), ALU.subtract).then_inc(f_lo_done, 1)

                def rest_w(n):
                    dve.wait_ge(w_hi_done, UP + n + 1)
                    if n < 2:
                        hi, lo = (w[:, 2 * n:2 * n + 2, :] for w in (wp_hi, wp_lo))
                        raw = w_raw[n % 4].rearrange("p (k n) -> p k n", k=2)
                    else:
                        hi, lo, raw = wo_hi[:, n - 2, :], wo_lo[:, n - 2, :], w_raw[n % 4]
                    dve.scalar_tensor_tensor(lo, raw, 0.5, hi.bitcast(F32), ALU.mult, ALU.subtract).then_inc(w_lo_done, 1)
                bias_y(0)
                centre_y(0)
                for n in range(NWT):
                    rest_w(n)
                var_y(0)
                norm_y(0)
                swish_y(0)
                rest_y(0)
                with dve.Fori(0, NB) as b:
                    dve.wait_ge(at_landed, UP + 16 * b + 16)
                    dve.wait_ge(za_landed, UP + 16 * b + 16)
                    for k in range(NC):
                        dve.tensor_tensor(z[:, k, :], at[:, k, :], z[:, k, :], ALU.mult).then_inc(gated, 1)
                    for k in range(NC):
                        rest_f(b, k)
                    dve.wait_ge(zc_landed, UP + 16 * b + 16)
                    for j in range(NC):
                        dve.wait_ge(prod, UP + TILES * b + j + 1)
                        dve.scalar_tensor_tensor(z[:, NC + j, :], G[j % 2][:], col("b_pw_2", j), z[:, NC + j, :], ALU.add, ALU.mult).then_inc(gated, 1)
                        rest_f(b, NC + j)
                    bias_y(b + 1)
                    dve.wait_ge(h1_landed, UP + 16 * b + 16)
                    for c in range(KT):
                        dve.wait_ge(prod, UP + TILES * b + NC + c + 1)
                        dve.scalar_tensor_tensor(h1[:, c, :], G[c % 2][:], modv[:, 1, 16 + c:17 + c], h1[:, c, :], ALU.mult, ALU.add).then_inc(x_out, 1)
                        if c == 1:
                            centre_y(b + 1)
                        if c == 3:
                            var_y(b + 1)
                        if c == 4:
                            norm_y(b + 1)
                        if c == 5:
                            swish_y(b + 1)
                        if c == 6:
                            rest_y(b + 1)

SCRATCH = {"h1t": (D, SEQ), "qt": (512, SEQ), "kt": (P, KEYS), "vtok": (KEYS, P), "za": (512, SEQ), "zc": (512, SEQ),
           "conv_y": (512, CONV_AT + SEQ), "att": (512, SEQ)}
PHASES = [modulation, gla_block, context_keys, projections, attention, output]


def program(nc, d, phases=PHASES):
    with ExitStack() as ctx:
        keep = {"ident": ctx.enter_context(nc.sbuf_tensor("ident_sb", [P, P], F32)),
                "cols": ctx.enter_context(nc.sbuf_tensor("cols", [P, P], F32)),
                "modv": ctx.enter_context(nc.sbuf_tensor("modv", [P, 3, 24], F32)),
                "gains": ctx.enter_context(nc.sbuf_tensor("gains", [P, 3, 8], F32)),
                "half_gn": ctx.enter_context(nc.sbuf_tensor("half_gn", [P, 2], F32))}
        for phase in phases:
            phase(nc, d, keep)


def shape_constants():
    i = np.arange(P)
    sel = ((i[:, None] <= i[None, :]) & (i[:, None] // CHUNK == i[None, :] // CHUNK)).astype(np.uint32)
    reset = np.broadcast_to((np.arange(TB) % CHUNK != 0).astype(np.float32), (P, TB)).copy()
    rot = np.zeros((P, P), np.float32)
    for m in range(P):
        if m % 32 < 16:
            rot[m + 16, m] = -1.0
        else:
            rot[m - 16, m] = 1.0
    freqs = np.float32(10000.0) ** (-np.arange(0, 32, 2, dtype=np.float32) / np.float32(32))
    t = np.arange(SEQ)
    place = np.where((i % HD < 32)[:, None], (t // 64)[None, :], (t % 64)[None, :]).astype(np.float32)
    angle = place * freqs[i % 16][:, None].astype(np.float32)
    head_ones = (i[:, None] // HD == i[None, :] // HD).astype(np.float32)
    return {"ident": np.eye(P, dtype=np.float32), "sel": sel, "reset": reset, "ones": np.ones((P, P), np.float32),
            "rot_t": rot, "head_ones": head_ones, "cos": np.cos(angle), "sin": np.sin(angle)}


_INS = ["x", "ctx_2", "c", "c_2", "c_ctx_2", "ada_w", "ada_b", "norm_g", "gla_w_in", "gla_w_alpha", "gla_b_alpha", "gla_norm_g",
        "gla_w_out", "final_g", "w_mod_2", "b_mod_2", "norm_w_2", "w_in_2", "q_norm_w_2", "k_norm_w_2", "conv_w_2", "conv_b_2",
        "conv_ln_w_2", "conv_ln_b_2", "w_pw_2", "b_pw_2", "w_out_2"]
_LEADING_ONE = [n for n in _INS if n not in ("final_g", "c_ctx_2")]


def kernel(**inputs):
    import concourse.bacc as bacc
    from concourse.bass_utils import run_bass_kernel_spmd

    nc = bacc.Bacc("TRN2", target_bir_lowering=False, num_devices=1)
    arrays, d = {}, {}
    for name in _INS:
        a = np.ascontiguousarray(inputs[name])
        arrays[name] = a[0] if name in _LEADING_ONE else a
    arrays.update(shape_constants())
    feeds = {}
    for name, a in arrays.items():
        d[name] = nc.dram_tensor(f"in_{name}", a.shape, mybir.dt.from_np(a.dtype), kind="ExternalInput").ap()
        feeds[f"in_{name}"] = a
    for name, shape in SCRATCH.items():
        d[name] = nc.dram_tensor(f"scratch_{name}", shape, F32).ap()
    d["out"] = nc.dram_tensor("out_0", (SEQ, D), F32, kind="ExternalOutput").ap()
    program(nc, d)
    result = run_bass_kernel_spmd(nc, [feeds], core_ids=[0])
    return np.asarray(result.results[0]["out_0"]).reshape(1, SEQ, D)
```

```python
from contextlib import ExitStack

import numpy as np

import concourse.bass as bass
from concourse import mybir

F32 = mybir.dt.float32
F32R = mybir.dt.float32r
U32 = mybir.dt.uint32
ALU = mybir.AluOpType
ACT = mybir.ActivationFunctionType
AX_X = mybir.AxisListType.X
ds = bass.ds

P = 128
SEQ, D = 2048, 1024
KT = D // P
TB = 512
NB = SEQ // TB
NT = TB // P
EPS = 1e-6
UP = 1

GLA_H, GLA_DK, GLA_DV, RANK, CHUNK = 4, 128, 256, 16, 64
GLA_QK = 2 * GLA_H * GLA_DK
GLA_VEND = GLA_QK + GLA_H * GLA_DV
GLA_COLS = 3088

VROWS = {}


def _rows(spec):
    at = 0
    for name, n in spec:
        VROWS[name] = (at, n)
        at += n
    return at


NROWS = _rows([("c", 8), ("c_2", 8), ("c_ctx_2", 8), ("ada_b", 24), ("b_mod_2", 24), ("norm_g", 8), ("final_g", 8),
               ("norm_w_2", 8), ("gla_norm_g", 2), ("gla_b_alpha", 4), ("conv_b_2", 4), ("conv_ln_w_2", 4),
               ("conv_ln_b_2", 4), ("b_pw_2", 4), ("q_norm_w_2", 1), ("k_norm_w_2", 1)])


def clear(nc, semaphores):
    nc.clear_and_free_semaphores(semaphores)
    nc.all_engine_barrier()


def pools(nc, ctx, phase):
    def sb(name, shape, dt=F32):
        return ctx.enter_context(nc.sbuf_tensor(f"{phase}_{name}", shape, dt))

    def ps(name, shape, dt=F32):
        return ctx.enter_context(nc.psum_tensor(f"{phase}_{name}", shape, dt))

    made = []
    starters = (nc.sync, nc.scalar, nc.vector, nc.gpsimd, nc.tensor)

    def sem(name):
        made.append(nc.alloc_semaphore(f"{phase}_{name}"))
        starters[len(made) % len(starters)].sem_inc(made[-1], UP)
        return made[-1]

    ctx.callback(lambda: clear(nc, made))
    return sb, ps, sem


def modulation(nc, d, keep):
    with ExitStack() as ctx:
        sb, ps, sem = pools(nc, ctx, "mod")
        SLOTS, WC = 4, 512
        NS = 3 * D // WC
        vrows = sb("vrows", [P, P])
        csil = sb("csil", [P, 24])
        ctan = sb("ctan", [P, 24])
        wslab = [sb(f"wslab{s}", [P, KT, WC]) for s in range(SLOTS)]
        ps_cols = ps("ps_cols", [P, P])
        rows = [sb(f"rows{m}", [1 + m, 3 * D]) for m in range(2)]
        bank = [ps(f"bank{i}", [2, WC]) for i in range(2)]
        ps_mod1 = ps("ps_mod1", [P, 24])
        ps_mod2 = ps("ps_mod2", [P, 24, 2])
        rows_clear, rows_landed, consts_landed = sem("rows_clear"), sem("rows_landed"), sem("consts_landed")
        cols_made, cols_copied, tanh_made, silu_made = (
            sem("cols_made"), sem("cols_copied"), sem("tanh_made"), sem("silu_made"))
        slab_landed = [sem(f"slab_landed{s}") for s in range(SLOTS)]
        slab_used, row_copied = sem("slab_used"), sem("row_copied")
        mods_made, mod_step = sem("mods_made"), sem("mod_step")
        cols, modv, gains, ident = keep["cols"], keep["modv"], keep["gains"], keep["ident"]

        def col(name):
            at, n = VROWS[name]
            return cols[:, at:at + n]

        nc.all_engine_barrier()
        with nc.Block() as block:
            @block.sync
            def _(sp):
                for n in range(2 * NS):
                    w = d["ada_w"] if n < NS else d["w_mod_2"]
                    if n >= SLOTS:
                        sp.wait_ge(slab_used, UP + n - SLOTS + 1)
                    sp.dma_start(wslab[n % SLOTS][:], w.rearrange("(k p) n -> p k n", p=P)[:, :, WC * (n % NS):WC * (n % NS + 1)]
                                 ).then_inc(slab_landed[n % SLOTS], 16)

            @block.scalar
            def _(act):
                act.dma_start(ident[:], d["ident"]).then_inc(consts_landed, 16)
                act.wait_ge(rows_clear, UP + 1)
                for name, (at, n) in VROWS.items():
                    if name in ("q_norm_w_2", "k_norm_w_2"):
                        for half in range(2):
                            act.dma_start(vrows[at:at + 1, 64 * half:64 * half + 64],
                                          d[name].rearrange("(r c) -> r c", r=1)).then_inc(rows_landed, 16)
                    else:
                        act.dma_start(vrows[at:at + n, :], d[name].rearrange("(r c) -> r c", c=P)).then_inc(rows_landed, 16)
                act.wait_ge(cols_copied, UP + 1)
                act.activation(ctan[:], cols[:, 0:24], ACT.Tanh, scale=0.5).then_inc(tanh_made, 1)
                for n in range(2 * NS):
                    m = n // NS
                    act.wait_ge(slab_used, UP + n + 1)
                    act.activation(rows[m][:, WC * (n % NS):WC * (n % NS + 1)], bank[n % 2][0:1 + m, :], ACT.Copy).then_inc(row_copied, 1)

            @block.tensor
            def _(pe):
                pe.wait_ge(consts_landed, UP + 16)
                pe.wait_ge(rows_landed, UP + 16 * (len(VROWS) + 2))
                pe.transpose(ps_cols[:], vrows[:], ident[:]).then_inc(cols_made, 1)
                pe.wait_ge(silu_made, UP + 1)
                def turn_rows(m, out):
                    pe.wait_ge(row_copied, UP + NS * (m + 1))
                    for j in range(3 * KT):
                        pe.transpose(out[:, j:j + 1] if m == 0 else out[:, j, :], rows[m][:, P * j:P * (j + 1)], ident[0:1 + m, 0:1 + m])

                for n in range(2 * NS):
                    m = n // NS
                    pe.wait_ge(slab_landed[n % SLOTS], UP + 16 * (n // SLOTS) + 16)
                    if n >= 2:
                        pe.wait_ge(row_copied, UP + n - 1)
                    for k in range(KT):
                        lhs = csil[:, k:k + 1] if m == 0 else csil[:].rearrange("p (v k) -> p k v", k=8)[:, k, 1:3]
                        last = pe.matmul(bank[n % 2][0:1 + m, :], lhs, wslab[n % SLOTS][:, k, :], start=(k == 0), stop=(k == KT - 1))
                    last.then_inc(slab_used, 1)
                    if n == NS:
                        turn_rows(0, ps_mod1)
                turn_rows(1, ps_mod2)
                pe.drain().then_inc(mods_made, 1)

            @block.vector
            def _(dve):
                dve.memset(vrows[:], 0.0).then_inc(rows_clear, 1)
                dve.wait_ge(cols_made, UP + 1)
                dve.tensor_copy(cols[:], ps_cols[:]).then_inc(cols_copied, 1)
                dve.wait_ge(tanh_made, UP + 1)
                dve.wait_ge(cols_copied, UP + 1)
                dve.scalar_tensor_tensor(csil[:], ctan[:], 1.0, cols[:, 0:24], ALU.add, ALU.mult).then_inc(mod_step, 1)
                dve.wait_ge(mod_step, UP + 1)
                dve.tensor_scalar(csil[:], csil[:], 0.5, None, ALU.mult).then_inc(silu_made, 1)
                dve.wait_ge(mods_made, UP + 1)
                dve.tensor_tensor(modv[:, 0, :], ps_mod1[:], col("ada_b"), ALU.add).then_inc(mod_step, 1)
                for v in range(2):
                    dve.tensor_tensor(modv[:, 1 + v, :], ps_mod2[:, :, v], col("b_mod_2"), ALU.add).then_inc(mod_step, 1)
                dve.wait_ge(mod_step, UP + 4)
                for v, w in enumerate(("norm_g", "norm_w_2", "norm_w_2")):
                    dve.scalar_tensor_tensor(gains[:, v, :], modv[:, v, 8:16], 1.0, col(w), ALU.add, ALU.mult).then_inc(mod_step, 1)
                dve.tensor_scalar(keep["half_gn"][:], col("gla_norm_g"), 0.5, None, ALU.mult).then_inc(mod_step, 1)
                dve.wait_ge(mod_step, UP + 8)


def newton_rsqrt(dve, y, v, t, step, n):
    dve.tensor_tensor(t, v, y, ALU.mult).then_inc(step, 1)
    dve.wait_ge(step, UP + n + 1)
    dve.scalar_tensor_tensor(t, t, -0.5, y, ALU.mult, ALU.mult).then_inc(step, 1)
    dve.wait_ge(step, UP + n + 2)
    dve.scalar_tensor_tensor(y, t, 1.5, y, ALU.add, ALU.mult).then_inc(step, 2)


SMALL_STEPS = 14


def small_rsqrt(dve, y, v, t, step, n):
    dve.tensor_scalar(t.bitcast(U32), v.bitcast(U32), 1, None, ALU.logical_shift_right).then_inc(step, 1)
    dve.wait_ge(step, UP + n + 1)
    dve.tensor_scalar(y.bitcast(U32), t.bitcast(U32), -1.0, float(0x5f3759df), ALU.mult, ALU.add).then_inc(step, 1)
    for i in range(3):
        dve.wait_ge(step, UP + n + 2 + 4 * i)
        newton_rsqrt(dve, y, v, t, step, n + 2 + 4 * i)


def gla_block(nc, d, keep):
    NPROJ = 24
    NW = NPROJ + KT
    PER = NT
    with ExitStack() as ctx:
        sb, ps, sem = pools(nc, ctx, "gla")
        cols, modv, gains, ident = keep["cols"], keep["modv"], keep["gains"], keep["ident"]

        def col(name):
            at, n = VROWS[name]
            return cols[:, at:at + n]

        a_hi = sb("a_hi", [P, KT, TB], F32R)
        a_lo = sb("a_lo", [P, KT, TB], F32R)
        xr = sb("xr", [P, 8, TB])
        xtok = xr[:].rearrange("p a b -> p (a b)").rearrange("p (t n) -> p t n", t=NT)
        o_t = sb("o_t", [P, 8, TB])
        xrc = sb("xrc", [P, 2, NT, P])
        qk = sb("qk", [P, 2, GLA_H, TB])
        v_tok = sb("v_tok", [P, NT, D])
        zb = sb("zb", [P, GLA_H, TB])
        eb = sb("eb", [P, GLA_H, TB])
        tmp = sb("tmp", [P, 6, TB])
        w_raw = [sb(f"w_raw{s}", [P, KT, P]) for s in range(4)]
        w_hi = [sb(f"w_hi{s}", [P, KT, P], F32R) for s in range(2)]
        w_lo = [sb(f"w_lo{s}", [P, KT, P], F32R) for s in range(2)]
        glr_raw = sb("glr_raw", [P, KT, RANK])
        glr_hi = sb("glr_hi", [P, KT, RANK], F32R)
        glr_lo = sb("glr_lo", [P, KT, RANK], F32R)
        glr_t = sb("glr_t", [RANK, TB])
        w_alpha = sb("w_alpha", [RANK, GLA_H * GLA_DK])
        qe, ke, kd, kdt, att = (sb(n, [P, GLA_H, P]) for n in ("qe", "ke", "kd", "kdt", "att"))
        qb = [sb(f"qb{c}", [P, GLA_H, P]) for c in range(2)]
        dec = sb("dec", [P, GLA_H, 2])
        s_in = sb("s_in", [P, 2, GLA_H, GLA_DV])
        s_mid = sb("s_mid", [P, GLA_H, GLA_DV])
        on = sb("on", [P, D])
        sel = sb("sel", [P, P], U32)
        reset = sb("reset", [P, TB])
        ones = sb("ones", [P, P])
        xst = sb("xst", [P, 4, NT])
        ost = sb("ost", [P, 4, GLA_H])
        G = [ps(f"bank_g{i}", [P, TB]) for i in range(2)]
        T = [ps(f"bank_t{i}", [P, TB]) for i in range(2)]
        A = ps("bank_a", [P, TB])
        KV = ps("bank_kv", [P, TB])
        O = ps("bank_o", [P, 2, TB])

        def kv_at(h, c):
            return (KV, T[1])[c][:, GLA_DV * (h % 2):GLA_DV * (h % 2 + 1)]

        scores_seen = sem("scores_seen")
        consts, glr_split, cleared = sem("consts"), sem("glr_split"), sem("cleared")
        x_landed, sq_sum, ms, rs_step, xn = (
            sem(n) for n in ("x_landed", "sq_sum", "ms", "rs_step", "xn"))
        xt, hf, h_hi, h_lo = sem("xt"), sem("hf"), sem("h_hi"), sem("h_lo")
        w_landed = [sem(f"w_landed{s}") for s in range(4)]
        w_rest = [sem(f"w_rest{s}") for s in range(4)]
        w_rounded, proj, proj_out = sem("w_rounded"), sem("proj"), sem("proj_out")
        glr_done, glr_copied, z, zc, zstep, la, scan = (
            sem(n) for n in ("glr_done", "glr_copied", "z", "zc", "zstep", "la", "scan"))
        vt, v_copied = sem("vt"), sem("v_copied")
        dif, exps, qs_dve, qs_pool = sem("dif"), sem("exps"), sem("qs_dve"), sem("qs_pool")
        a_done, kd_done, kdt_copied, at_done = sem("a_done"), sem("kd_done"), sem("kdt_copied"), sem("at_done")
        kv, smid, snew, o_done = sem("kv"), sem("smid"), sem("snew"), sem("o_done")
        osq, oms, ors_step, on_done, ot, ot_copied = (
            sem(n) for n in ("osq", "oms", "ors_step", "on_done", "ot", "ot_copied"))
        tanh_r, r_done, y_done, y_hi, y_lo = (sem(n) for n in ("tanh_r", "r_done", "y_done", "y_hi", "y_lo"))
        xr_landed, xr_t, xr_copied, x1, sq, sq_added, sqs = (
            sem(n) for n in ("xr_landed", "xr_t", "xr_copied", "x1", "sq", "sq_added", "sqs"))
        tv, tln, trs0, trs_step, h1, h1_stored = (
            sem(n) for n in ("tv", "tln", "trs0", "trs_step", "h1", "h1_stored"))

        w_in = d["gla_w_in"].rearrange("(k p) n -> p k n", p=P)
        w_out = d["gla_w_out"].rearrange("(k p) n -> p k n", p=P)
        x = d["x"].rearrange("(t p) n -> p t n", p=P)
        h1t = d["h1t"].rearrange("(c p) t -> p c t", p=P)

        def tok(t):
            return slice(P * t, P * (t + 1))

        nc.all_engine_barrier()
        with nc.Block() as block:
            @block.sync
            def _(sp):
                sp.dma_start(xtok, x[:, 0:NT, :]).then_inc(x_landed, 16)
                for dst, src in ((sel, "sel"), (reset, "reset"), (ones, "ones")):
                    sp.dma_start(dst[:], d[src]).then_inc(consts, 16)
                sp.dma_start(glr_raw[:], w_in[:, :, GLA_VEND:GLA_VEND + RANK]).then_inc(consts, 16)
                sp.dma_start(w_alpha[:], d["gla_w_alpha"]).then_inc(consts, 16)

                def load(group, s, src, col0):
                    sp.wait_ge(w_rest[s], UP + group)
                    sp.dma_start(w_raw[s][:], src[:, :, ds(col0 + s * P, P)]).then_inc(w_landed[s], 16)
                for s in range(4):
                    load(0, s, w_in, 0)
                with sp.Fori(0, NB) as b:
                    with sp.Fori(1, 4) as g:
                        for s in range(4):
                            load(b * 8 + g, s, w_in, g * TB)
                    with sp.Fori(4, 6) as g:
                        for s in range(4):
                            load(b * 8 + g, s, w_in, g * TB + RANK)
                    with sp.Fori(0, 2) as g:
                        for s in range(4):
                            load(b * 8 + 6 + g, s, w_out, g * TB)
                            sp.wait_ge(xr_t, UP + b * 8 + g * 4 + s)
                            sp.dma_start(xrc[:, s % 2, :, :], x[:, ds(b * NT, NT), ds(g * TB + s * P, P)]).then_inc(xr_landed, 16)
                            if s == 1:
                                sp.wait_ge(y_done, UP + b * 8 + 8)
                                sp.dma_start(xtok[:, ds(g * 2, 2), :], x[:, ds(((b + 1) % NB) * NT + g * 2, 2), :]).then_inc(x_landed, 16)
                    for s in range(4):
                        load(b * 8 + 8, s, w_in, 0)
                    sp.wait_ge(h1, UP + b * 8 + 8)
                    sp.dma_start(h1t[:, :, ds(b * TB, TB)], o_t[:]).then_inc(h1_stored, 16)
                sp.wait_ge(h1_stored, UP + 16 * NB)
                for s in range(4):
                    sp.wait_ge(w_landed[s], UP + 16 * (8 * NB + 1))

            @block.gpsimd
            def _(pool):
                for m in (qb[0], qb[1], att):
                    pool.memset(m[:], 0.0).then_inc(cleared, 1)
                pool.memset(s_in[:, 0, :, :], 0.0).then_inc(cleared, 1)

                def rest(group, s, n):
                    pool.wait_ge(w_rounded, UP + n + 1)
                    pool.tensor_tensor(w_lo[s % 2][:], w_raw[s][:], w_hi[s % 2][:].bitcast(F32), ALU.subtract).then_inc(w_rest[s], 1)

                def ahead(group, s):
                    rest(group if s < 3 else group + 1, (s + 1) % 4, group * 4 + s + 1)

                def decay_k(b, t):
                    u = b * PER + t
                    pool.wait_ge(exps, UP + u * 5 + 2)
                    pool.wait_ge(a_done, UP + u)
                    pool.tensor_tensor(ke[:], qk[:, 1, :, tok(t)], tmp[:, 1, :].rearrange("p (h i) -> p h i", h=4), ALU.mult).then_inc(qs_pool, 1)
                    pool.wait_ge(exps, UP + u * 5 + 4)
                    pool.wait_ge(kd_done, UP + u)
                    pool.tensor_tensor(kd[:], qk[:, 1, :, tok(t)], tmp[:, 3, :].rearrange("p (h i) -> p h i", h=4), ALU.mult).then_inc(qs_pool, 1)
                rest(0, 0, 0)
                with pool.Fori(0, NB) as b:
                    with pool.Fori(0, 3) as g:
                        for s in range(4):
                            ahead(b * 8 + g, s)
                    for s in range(4):
                        ahead(b * 8 + 3, s)
                        if s == 2:
                            decay_k(b, 0)
                    for t in range(PER):
                        ahead(b * 8 + 4 + t // 2, 2 * (t % 2))
                        if t + 1 < PER:
                            decay_k(b, t + 1)
                        ahead(b * 8 + 4 + t // 2, 2 * (t % 2) + 1)
                    with pool.Fori(0, 2) as g:
                        for s in range(4):
                            ahead(b * 8 + 6 + g, s)

            @block.tensor
            def _(pe):
                def gemm(group, s, banks=G, first_wait=None, between=None):
                    pe.wait_ge(w_rest[s], UP + group + 1)
                    for k in range(KT):
                        if k == BETWEEN_AT and between is not None:
                            between()
                        if first_wait is not None:
                            pe.wait_ge(first_wait[0], UP + first_wait[1] + k + 1)
                        for n, (w, a) in enumerate(((w_hi, a_hi), (w_hi, a_lo), (w_lo, a_hi))):
                            last = pe.matmul(banks[s % 2][:], w[s % 2][:, k, :], a[:, k, :], start=(k == 0 and n == 0),
                                             stop=(k == KT - 1 and n == 2))
                    last.then_inc(proj, 1)

                def transpose_x(b):
                    pe.wait_ge(xn, UP + b * 4 + 4)
                    pe.wait_ge(xr_copied, UP + b * 8)
                    for c in range(KT):
                        if c >= 2:
                            pe.wait_ge(hf, UP + b * 8 + c - 1)
                        for t in range(NT):
                            last = pe.transpose(T[c % 2][:, tok(t)], xtok[:, t, P * c:P * (c + 1)], ident[:])
                        last.then_inc(xt, 1)

                BETWEEN_AT = KT - 2

                def scores(b, t):
                    u = b * PER + t
                    pe.wait_ge(qs_dve, UP + u * 3 + 3)
                    pe.wait_ge(qs_pool, UP + u * 2 + 2)
                    pe.wait_ge(at_done, UP + u)
                    for h in range(GLA_H):
                        last = pe.matmul(A[:, tok(h)], ke[:, h, :], qe[:, h, :], start=True, stop=True)
                    last.then_inc(a_done, 1)
                    pe.wait_ge(snew, UP + u * 4)
                    for h in range(GLA_H):
                        last = pe.transpose(KV[:, tok(h)], kd[:, h, :], ident[:])
                    last.then_inc(kd_done, 1)

                def unit(b, t):
                    u = b * PER + t

                    def kv_of(h):
                        for c in range(2):
                            half = slice(64 * c, 64 * c + 64)
                            last = pe.matmul(kv_at(h, c), kdt[half, h, :],
                                             v_tok[half, t, GLA_DV * h:GLA_DV * (h + 1)], start=True, stop=True)
                        last.then_inc(kv, 1)

                    def out_of(h):
                        pe.wait_ge(smid, UP + u * 4 + h + 1)
                        o = O[:, h // 2, GLA_DV * (h % 2):GLA_DV * (h % 2 + 1)]
                        pe.matmul(o, att[:, h, :], v_tok[:, t, GLA_DV * h:GLA_DV * (h + 1)], start=True, stop=False)
                        pe.matmul(o, qb[0][:, h, :], s_in[:, t % 2, h, :], start=False, stop=False)
                        pe.matmul(o, qb[1][:, h, :], s_mid[:, h, :], start=False, stop=True).then_inc(o_done, 1)
                    pe.wait_ge(kdt_copied, UP + u + 1)
                    pe.wait_ge(ot_copied, UP + u * 2)
                    kv_of(0)
                    kv_of(1)
                    pe.wait_ge(at_done, UP + u + 1)
                    pe.wait_ge(on_done, UP + u * 4)
                    out_of(0)
                    out_of(1)
                    pe.wait_ge(snew, UP + u * 4 + 2)
                    kv_of(2)
                    kv_of(3)
                    out_of(2)
                    out_of(3)

                def transpose_o(b, t):
                    u = b * PER + t
                    pe.wait_ge(on_done, UP + u * 4 + 4)
                    pe.wait_ge(snew, UP + u * 4 + 4)
                    for half in range(2):
                        for c in range(4):
                            last = pe.transpose(T[half][:, tok(c)], on[:, tok(4 * half + c)], ident[:])
                        last.then_inc(ot, 1)

                pe.wait_ge(consts, UP + 80)
                pe.wait_ge(cleared, UP + 4)
                pe.wait_ge(glr_split, UP + 2)
                transpose_x(0)
                with pe.Fori(0, NB) as b:
                    pe.wait_ge(tv, UP + b)
                    pe.wait_ge(x1, UP + b * 8)
                    for k in range(KT):
                        pe.wait_ge(h_lo, UP + b * 8 + k + 1)
                        for n, (w, a) in enumerate(((glr_hi, a_hi), (glr_hi, a_lo), (glr_lo, a_hi))):
                            last = pe.matmul(A[0:RANK, :], w[:, k, :], a[:, k, :], start=(k == 0 and n == 0),
                                             stop=(k == KT - 1 and n == 2))
                    last.then_inc(glr_done, 1)
                    with pe.Fori(0, 2) as g:
                        for s in range(4):
                            pe.wait_ge(proj_out, UP + b * 16 + g * 4 + s)
                            gemm(b * 8 + g, s)
                    pe.wait_ge(glr_copied, UP + b + 1)
                    for h, bank in enumerate((O[:, 0, :], O[:, 1, :], A[:], KV[:])):
                        pe.matmul(bank, w_alpha[:, tok(h)], glr_t[:], start=True, stop=True).then_inc(z, 1)

                    def transpose_v(j):
                        pe.wait_ge(proj_out, UP + b * 16 + 8 + j + 2)
                        pe.wait_ge(v_copied, UP + b * 8 + j)
                        for t in range(NT):
                            last = pe.transpose(T[j % 2][:, tok(t)], tmp[:, 4 + j % 2, tok(t)], ident[:])
                        last.then_inc(vt, 1)
                    for j in range(8):
                        pe.wait_ge(proj_out, UP + b * 16 + 8 + j)
                        gemm(b * 8 + 2 + j // 4, j % 4)
                        if j:
                            transpose_v(j - 1)
                    pe.wait_ge(zc, UP + b * 4 + 4)
                    scores(b, 0)
                    transpose_v(7)
                    pe.wait_ge(v_copied, UP + b * 8 + 9)
                    for t in range(PER):
                        unit(b, t)
                        for i in range(2):
                            r = 2 * t + i
                            if r < 2:
                                pe.wait_ge(proj_out, UP + b * 16 + 17)
                            else:
                                pe.wait_ge(r_done, UP + b * 8 + r - 1)
                            ahead = i == 1 and t + 1 < PER
                            gemm(b * 8 + 4 + r // 4, r % 4, between=(lambda: scores(b, t + 1)) if ahead else None)
                            if i == 0:
                                transpose_o(b, t)
                    pe.wait_ge(r_done, UP + b * 8 + 8)
                    pe.wait_ge(ot_copied, UP + b * 8 + 8)

                    for c in range(KT):
                        if c >= 2:
                            pe.wait_ge(xr_copied, UP + b * 8 + c - 1)
                        pe.wait_ge(xr_landed, UP + b * 128 + 16 * c + 16)
                        for t in range(NT):
                            last = pe.transpose(T[c % 2][:, tok(t)], xrc[:, c % 2, t, :], ident[:])
                        last.then_inc(xr_t, 1)
                        if c >= 2:
                            pe.wait_ge(x1, UP + b * 8 + c - 1)
                        gemm(b * 8 + 6 + c // 4, c % 4, first_wait=(y_lo, b * 8) if c == 0 else None)
                    transpose_x(b + 1)
                    pe.wait_ge(sq_added, UP + (b + 1) * (KT - 1))
                    pe.matmul(A[:], ones[:], eb[:, 3, :], start=True, stop=True).then_inc(sqs, 1)

            @block.scalar
            def _(act):
                def round_next(group, s):
                    act.wait_ge(w_landed[(s + 1) % 4], UP + (group if s < 3 else group + 1) * 16 + 16)
                    act.wait_ge(proj, UP + group * 4 + s)
                    act.activation(w_hi[(s + 1) % 2][:], w_raw[(s + 1) % 4][:], ACT.Copy).then_inc(w_rounded, 1)

                def squares_of_x(b, landed):
                    act.wait_ge(x_landed, UP + landed)
                    for t in range(NT):
                        if t:
                            act.wait_ge(sq_sum, UP + b * 4 + t)
                        act.activation(O[:].rearrange("p a b -> p (a b)"), xtok[:, t, :], ACT.Square,
                                       accum_out=xst[:, 0, t:t + 1]).then_inc(sq_sum, 1)

                def modulate(b):
                    act.wait_ge(sq_added, UP + b * (KT - 1))
                    for c in range(KT):
                        act.wait_ge(xt, UP + b * 8 + c + 1)
                        if c >= 2:
                            act.wait_ge(h_lo, UP + b * 8 + c - 1)
                        act.activation(tmp[:, c % 2, :], T[c % 2][:], ACT.Identity, bias=modv[:, 0, c:c + 1],
                                       scale=gains[:, 0, c:c + 1]).then_inc(hf, 1)

                def decays(b, t):
                    u = b * PER + t
                    act.wait_ge(dif, UP + u * 2 + 2)
                    act.wait_ge(qs_dve, UP + u * 3)
                    act.wait_ge(qs_pool, UP + u * 2)
                    act.wait_ge(snew, UP + u * 4)
                    for n, (src, scale) in enumerate(((eb[:, :, tok(0)], 1 / 16), (eb[:, :, tok(0)], -1 / 16),
                                                      (zb[:, :, tok(t)], 1 / 16), (eb[:, :, tok(1)], 1 / 16))):
                        act.activation(tmp[:, n, :].rearrange("p (h i) -> p h i", h=4), src, ACT.Exp, scale=scale).then_inc(exps, 1)
                    ends = zb[:, :, tok(t)].rearrange("p h (c i) -> p h c i", c=2)[:, :, :, CHUNK - 1]
                    act.activation(dec[:], ends, ACT.Exp, scale=1 / 16).then_inc(exps, 1)

                act.wait_ge(w_landed[0], UP + 16)
                act.activation(w_hi[0][:], w_raw[0][:], ACT.Copy).then_inc(w_rounded, 1)
                act.wait_ge(consts, UP + 80)
                act.activation(glr_hi[:], glr_raw[:], ACT.Copy).then_inc(proj_out, 1)
                squares_of_x(0, 16)
                modulate(0)
                with act.Fori(0, NB) as b:
                    act.wait_ge(qs_dve, UP + b * 12)
                    act.wait_ge(qs_pool, UP + b * 8)
                    act.wait_ge(glr_done, UP + b + 1)
                    act.activation(glr_t[:], A[0:RANK, :], ACT.Copy).then_inc(glr_copied, 1)
                    for j in range(8):
                        round_next(b * 8 + j // 4, j % 4)
                        act.wait_ge(proj, UP + b * NW + j + 1)
                        act.activation(qk[:, j // 4, j % 4, :], G[j % 2][:], ACT.Copy,
                                       scale=float(GLA_DK) ** -0.5 if j < 4 else 1.0).then_inc(proj_out, 1)
                    at0 = VROWS["gla_b_alpha"][0]
                    for h, bank in enumerate((O[:, 0, :], O[:, 1, :], A[:], KV[:])):
                        act.wait_ge(z, UP + b * 4 + h + 1)
                        act.activation(zb[:, h, :], bank, ACT.Identity, bias=cols[:, at0 + h:at0 + h + 1]).then_inc(zc, 1)
                    for j in range(8):
                        round_next(b * 8 + 2 + j // 4, j % 4)
                        if j == 6:
                            decays(b, 0)
                        if j >= 2:
                            act.wait_ge(vt, UP + b * 8 + j - 1)
                        act.wait_ge(proj, UP + b * NW + 8 + j + 1)
                        act.activation(tmp[:, 4 + j % 2, :], G[j % 2][:], ACT.Copy).then_inc(proj_out, 1)
                        if j == 0:
                            act.wait_ge(zc, UP + b * 4 + 4)
                            act.activation(eb[:], zb[:], ACT.Abs).then_inc(zstep, 1)
                        if j == 1:
                            act.wait_ge(zstep, UP + b * 3 + 1)
                            act.activation(eb[:], eb[:], ACT.Exp, scale=-1.0).then_inc(zstep, 1)
                        if j == 2:
                            act.wait_ge(zstep, UP + b * 3 + 2)
                            act.activation(eb[:], eb[:], ACT.Ln, bias=1.0).then_inc(zstep, 1)
                    def copy_kdt(t):
                        act.wait_ge(kd_done, UP + b * PER + t + 1)
                        act.activation(kdt[:].rearrange("p h i -> p (h i)"), KV[:], ACT.Copy).then_inc(kdt_copied, 1)
                    copy_kdt(0)
                    for t in range(PER):
                        u = b * PER + t
                        act.wait_ge(ot, UP + u * 2)
                        for h in range(GLA_H):
                            act.wait_ge(o_done, UP + u * 4 + 2 + h // 2 * 2)
                            act.activation(on[:, GLA_DV * h:GLA_DV * (h + 1)], O[:, h // 2, GLA_DV * (h % 2):GLA_DV * (h % 2 + 1)],
                                           ACT.Square, accum_out=ost[:, 0, h:h + 1]).then_inc(osq, 1)
                        round_next(b * 8 + 4 + t // 2, 2 * (t % 2))
                        act.wait_ge(ors_step, UP + u * SMALL_STEPS + SMALL_STEPS)
                        act.wait_ge(osq, UP + u * 4 + 4)
                        for h in range(GLA_H):
                            act.activation(on[:, GLA_DV * h:GLA_DV * (h + 1)], O[:, h // 2, GLA_DV * (h % 2):GLA_DV * (h % 2 + 1)],
                                           ACT.Copy, scale=ost[:, 2, h:h + 1]).then_inc(on_done, 1)
                        if t + 1 < PER:
                            decays(b, t + 1)
                        for i in range(2):
                            r = 2 * t + i
                            if i == 1:
                                round_next(b * 8 + 4 + t // 2, 2 * (t % 2) + 1)
                                act.wait_ge(h1_stored, UP + b * 16)
                                for half in range(2):
                                    act.wait_ge(ot, UP + u * 2 + half + 1)
                                    act.activation(o_t[:, 4 * half:4 * half + 4, tok(t)], T[half][:].rearrange("p (c i) -> p c i", c=4),
                                                   ACT.Copy).then_inc(ot_copied, 1)
                                if t + 1 < PER:
                                    copy_kdt(t + 1)
                            act.wait_ge(proj, UP + b * NW + 16 + r + 1)
                            if r >= 2:
                                act.wait_ge(r_done, UP + b * 8 + r - 1)
                            act.activation(tmp[:, 4 + r % 2, :], G[r % 2][:], ACT.Tanh, scale=0.5).then_inc(tanh_r, 1)
                    act.wait_ge(proj, UP + b * NW + NPROJ)
                    for c in range(KT):
                        act.wait_ge(y_done, UP + b * 8 + c + 1)
                        act.activation(a_hi[:, c, :], xr[:, c, :], ACT.Copy).then_inc(y_hi, 1)

                    def square_x1(c):
                        act.wait_ge(x1, UP + b * 8 + c + 1)
                        if c >= 2:
                            act.wait_ge(sq_added, UP + b * (KT - 1) + max(c - 2, 1))
                        act.activation(tmp[:, c % 2, :], o_t[:, c, :], ACT.Square).then_inc(sq, 1)
                    for c in range(KT):
                        round_next(b * 8 + 6 + c // 4, c % 4)
                        act.wait_ge(xr_t, UP + b * 8 + c + 1)
                        if c >= 2:
                            act.wait_ge(x1, UP + b * 8 + c - 1)
                        act.activation(tmp[:, 2 + c % 2, :], T[c % 2][:], ACT.Copy).then_inc(xr_copied, 1)
                        if c:
                            square_x1(c - 1)
                        if c == 5:
                            squares_of_x(b + 1, b * 32 + 48)
                    square_x1(KT - 1)
                    modulate(b + 1)
                    act.wait_ge(tv, UP + b + 1)
                    act.activation(eb[:, 1, :], eb[:, 0, :], ACT.Ln).then_inc(tln, 1)
                    act.wait_ge(tln, UP + b + 1)
                    act.activation(eb[:, 1, :], eb[:, 1, :], ACT.Exp, scale=-0.5).then_inc(trs0, 1)

            @block.vector
            def _(dve):
                def norm_x(b):
                    dve.wait_ge(sq_sum, UP + b * 4 + 4)
                    dve.tensor_scalar(xst[:, 1, :], xst[:, 0, :], 1.0 / D, EPS, ALU.mult, ALU.add).then_inc(ms, 1)
                    dve.wait_ge(ms, UP + b + 1)
                    small_rsqrt(dve, xst[:, 2, :], xst[:, 1, :], xst[:, 3, :], rs_step, b * SMALL_STEPS)
                    dve.wait_ge(rs_step, UP + b * SMALL_STEPS + SMALL_STEPS)
                    for t in range(NT):
                        dve.tensor_scalar(xtok[:, t, :], xtok[:, t, :], xst[:, 2, t:t + 1], None, ALU.mult).then_inc(xn, 1)

                def split_h(b):
                    dve.wait_ge(proj, UP + b * NW)
                    for c in range(KT):
                        dve.wait_ge(hf, UP + b * 8 + c + 1)
                        dve.tensor_copy(a_hi[:, c, :], tmp[:, c % 2, :]).then_inc(h_hi, 1)
                        dve.wait_ge(h_hi, UP + b * 8 + c + 1)
                        dve.tensor_tensor(a_lo[:, c, :], tmp[:, c % 2, :], a_hi[:, c, :].bitcast(F32), ALU.subtract).then_inc(h_lo, 1)

                def logdiffs(b, t):
                    u = b * PER + t
                    dve.wait_ge(exps, UP + u * 5)
                    bt = zb[:, :, tok(t)].rearrange("p h (c i) -> p h c i", c=2)
                    d1 = eb[:, :, tok(0)].rearrange("p h (c i) -> p h c i", c=2)
                    d2 = eb[:, :, tok(1)].rearrange("p h (c i) -> p h c i", c=2)
                    mid = bt[:, :, :, CHUNK // 2:CHUNK // 2 + 1].broadcast_to([P, GLA_H, 2, CHUNK])
                    end = bt[:, :, :, CHUNK - 1:CHUNK].broadcast_to([P, GLA_H, 2, CHUNK])
                    dve.tensor_tensor(d1, bt, mid, ALU.subtract).then_inc(dif, 1)
                    dve.tensor_tensor(d2, end, bt, ALU.subtract).then_inc(dif, 1)

                def decay_q(b, t):
                    u = b * PER + t
                    e1, e3 = (tmp[:, n, :].rearrange("p (h i) -> p h i", h=4) for n in (0, 2))
                    dve.wait_ge(exps, UP + u * 5 + 3)
                    dve.wait_ge(o_done, UP + u * 4)
                    dve.tensor_tensor(qe[:], qk[:, 0, :, tok(t)], e1, ALU.mult).then_inc(qs_dve, 1)
                    for c in range(2):
                        half = slice(CHUNK * c, CHUNK * (c + 1))
                        dve.tensor_tensor(qb[c][:, :, half], qk[:, 0, :, P * t + CHUNK * c:P * t + CHUNK * (c + 1)], e3[:, :, half],
                                          ALU.mult).then_inc(qs_dve, 1)

                dve.wait_ge(proj_out, UP + 1)
                dve.tensor_tensor(glr_lo[:], glr_raw[:], glr_hi[:].bitcast(F32), ALU.subtract).then_inc(glr_split, 1)
                dve.memset(on[:, 0:1], 0.0).then_inc(glr_split, 1)
                dve.memset(ost[:, 0, 0:1], 0.0).then_inc(v_copied, 1)
                dve.wait_ge(cleared, UP + 4)
                norm_x(0)
                split_h(0)
                with dve.Fori(0, NB) as b:
                    for j in range(8):
                        if j == 6:
                            decay_q(b, 0)
                        dve.wait_ge(vt, UP + b * 8 + j + 1)
                        dve.tensor_copy(v_tok[:, :, tok(j)], T[j % 2][:].rearrange("p (t i) -> p t i", t=NT)).then_inc(v_copied, 1)
                        if j == 2:
                            dve.wait_ge(zstep, UP + b * 3 + 3)
                            dve.scalar_tensor_tensor(eb[:], zb[:], 0.0, eb[:], ALU.min, ALU.subtract).then_inc(la, 1)
                            dve.wait_ge(la, UP + b + 1)
                        if j == 3:
                            for h in range(GLA_H):
                                dve.tensor_tensor_scan(zb[:, h, :], reset[:], eb[:, h, :], 0.0, ALU.mult, ALU.add).then_inc(scan, 1)
                        if j == 4:
                            dve.wait_ge(scan, UP + b * 4 + 4)
                            logdiffs(b, 0)
                    def mask_scores(t):
                        dve.wait_ge(cleared, UP + 4)
                        dve.wait_ge(a_done, UP + b * PER + t + 1)
                        dve.sem_inc(scores_seen, 1)
                        dve.copy_predicated(att[:], sel[:].rearrange("p (h i) -> p h i", h=1).broadcast_to([P, GLA_H, P]),
                                            A[:].rearrange("p (h i) -> p h i", h=4)).then_inc(at_done, 1)
                    mask_scores(0)
                    for t in range(PER):
                        u = b * PER + t
                        dve.wait_ge(exps, UP + u * 5 + 5)
                        for h in range(GLA_H):
                            dve.wait_ge(kv, UP + u * 4 + 2 + h // 2 * 2)
                            dve.scalar_tensor_tensor(s_mid[:, h, :], s_in[:, t % 2, h, :], dec[:, h, 0:1], kv_at(h, 0),
                                                     ALU.mult, ALU.add).then_inc(smid, 1)
                            dve.wait_ge(smid, UP + u * 4 + h + 1)
                            dve.scalar_tensor_tensor(s_in[:, 1 - t % 2, h, :], s_mid[:, h, :], dec[:, h, 1:2], kv_at(h, 1),
                                                     ALU.mult, ALU.add).then_inc(snew, 1)
                        if t + 1 < PER:
                            logdiffs(b, t + 1)
                        dve.wait_ge(osq, UP + u * 4 + 4)
                        dve.tensor_scalar(ost[:, 1, :], ost[:, 0, :], 1.0 / GLA_DV, EPS, ALU.mult, ALU.add).then_inc(oms, 1)
                        dve.wait_ge(oms, UP + u + 1)
                        small_rsqrt(dve, ost[:, 2, :], ost[:, 1, :], ost[:, 3, :], ors_step, u * SMALL_STEPS)
                        if t + 1 < PER:
                            decay_q(b, t + 1)
                        for i in range(2):
                            r = 2 * t + i
                            if i == 1 and t + 1 < PER:
                                mask_scores(t + 1)
                            dve.wait_ge(tanh_r, UP + b * 8 + r + 1)
                            dve.scalar_tensor_tensor(xr[:, r, :], tmp[:, 4 + r % 2, :], 1.0, G[r % 2][:], ALU.add, ALU.mult).then_inc(r_done, 1)
                    dve.wait_ge(ot_copied, UP + b * 8 + 8)
                    dve.wait_ge(r_done, UP + b * 8 + 8)

                    def rest_of_y(c):
                        dve.wait_ge(y_hi, UP + b * 8 + c + 1)
                        dve.tensor_tensor(a_lo[:, c, :], xr[:, c, :], a_hi[:, c, :].bitcast(F32), ALU.subtract).then_inc(y_lo, 1)
                    for c in range(KT):
                        dve.scalar_tensor_tensor(xr[:, c, :], xr[:, c, :], keep["half_gn"][:, c % 2:c % 2 + 1], o_t[:, c, :],
                                                 ALU.mult, ALU.mult).then_inc(y_done, 1)
                        if c:
                            rest_of_y(c - 1)
                    rest_of_y(KT - 1)

                    def add_squares(c):
                        dve.wait_ge(sq, UP + b * 8 + c + 1)
                        if c == 1:
                            dve.wait_ge(exps, UP + (b + 1) * PER * 5)
                        else:
                            dve.wait_ge(sq_added, UP + b * (KT - 1) + c - 1)
                        dve.tensor_tensor(eb[:, 3, :], tmp[:, 0, :] if c == 1 else eb[:, 3, :], tmp[:, c % 2, :], ALU.add).then_inc(sq_added, 1)
                    for c in range(KT):
                        dve.wait_ge(proj, UP + b * NW + NPROJ + c + 1)
                        dve.wait_ge(xr_copied, UP + b * 8 + c + 1)
                        dve.scalar_tensor_tensor(o_t[:, c, :], G[c % 2][:], modv[:, 0, 16 + c:17 + c], tmp[:, 2 + c % 2, :],
                                                 ALU.mult, ALU.add).then_inc(x1, 1)
                        if c >= 2:
                            add_squares(c - 1)
                        if c == 5:
                            norm_x(b + 1)
                    add_squares(KT - 1)
                    split_h(b + 1)
                    dve.wait_ge(sqs, UP + b + 1)
                    dve.tensor_scalar(eb[:, 0, :], A[:], 1.0 / D, EPS, ALU.mult, ALU.add).then_inc(tv, 1)
                    dve.wait_ge(trs0, UP + b + 1)
                    newton_rsqrt(dve, eb[:, 1, :], eb[:, 0, :], eb[:, 2, :], trs_step, b * 4)
                    dve.wait_ge(trs_step, UP + b * 4 + 4)
                    for c in range(KT):
                        dve.scalar_tensor_tensor(o_t[:, c, :], o_t[:, c, :], col("final_g")[:, c:c + 1], eb[:, 1, :],
                                                 ALU.mult, ALU.mult).then_inc(h1, 1)
                dve.wait_ge(h1, UP + 8 * NB)


HD, NQH, NKV = 64, 8, 2
KEYS, CTX = SEQ + 256, 256
COL_Q, COL_K, COL_V, COL_ZA, COL_A, COL_G, COL_ZC = 0, 512, 640, 768, 1280, 1792, 2304
TAPS, PAD = 31, 15
LAG = 16
CONV_AT = TB + LAG


def context_keys(nc, d, keep):
    NC = CTX // P
    with ExitStack() as ctx:
        sb, ps, sem = pools(nc, ctx, "ctx")
        cols, modv, gains, ident = keep["cols"], keep["modv"], keep["gains"], keep["ident"]
        xc = sb("xc", [P, NC, D])
        w = sb("w", [P, KT, 2 * P])
        w_hi, w_lo = sb("w_hi", [P, KT, 2 * P], F32R), sb("w_lo", [P, KT, 2 * P], F32R)
        u = sb("u", [P, KT, CTX])
        u_hi, u_lo = sb("u_hi", [P, KT, CTX], F32R), sb("u_lo", [P, KT, CTX], F32R)
        st = sb("st", [P, 4, NC])
        junk = sb("junk", [P, NC, D])
        head_ones = sb("head_ones", [P, P])
        kraw, ksq, kms, krs, kt = (sb(n, [P, CTX]) for n in ("kraw", "ksq", "kms", "krs", "kt"))
        vraw, vout = sb("vraw", [P, CTX]), sb("vout", [P, NC, P])
        XT = [ps(f"bank_xt{i}", [P, 512]) for i in range(2)]
        BK, BV, BS, BT = (ps(n, [P, 512]) for n in ("bank_k", "bank_v", "bank_s", "bank_t"))
        landed, w_landed, ones_landed = sem("landed"), sem("w_landed"), sem("ones_landed")
        sq, ms, ln, rs0, step, xn, xt, um, hi, lo = (sem(n) for n in ("sq", "ms", "ln", "rs0", "step", "xn", "xt", "um", "hi", "lo"))
        whi, wlo, k_done, v_done, k_read, v_read, ssum, kstep, k_out, vt, v_out, stored = (
            sem(n) for n in ("whi", "wlo", "k_done", "v_done", "k_read", "v_read", "ssum", "kstep", "k_out", "vt", "v_out", "stored"))
        at_kw = VROWS["k_norm_w_2"][0]
        nc.all_engine_barrier()
        with nc.Block() as block:
            @block.sync
            def _(sp):
                sp.dma_start(xc[:], d["ctx_2"].rearrange("(t p) n -> p t n", p=P)).then_inc(landed, 16)
                sp.dma_start(w[:], d["w_in_2"].rearrange("(k p) n -> p k n", p=P)[:, :, COL_K:COL_ZA]).then_inc(w_landed, 16)
                sp.dma_start(head_ones[:], d["head_ones"]).then_inc(ones_landed, 16)
                sp.wait_ge(k_out, UP + 1)
                sp.dma_start(d["kt"][:, 0:CTX], kraw[:]).then_inc(stored, 16)
                sp.wait_ge(v_out, UP + 1)
                sp.dma_start(d["vtok"].rearrange("(t p) n -> p t n", p=P)[:, 0:NC, :], vout[:]).then_inc(stored, 16)
                sp.wait_ge(stored, UP + 32)

            @block.scalar
            def _(act):
                act.wait_ge(landed, UP + 16)
                for t in range(NC):
                    act.activation(junk[:, t, :], xc[:, t, :], ACT.Square, accum_out=st[:, 0, t:t + 1]).then_inc(sq, 1)
                act.wait_ge(w_landed, UP + 16)
                act.activation(w_hi[:], w[:], ACT.Copy).then_inc(whi, 1)
                act.wait_ge(ms, UP + 1)
                act.activation(st[:, 2, :], st[:, 1, :], ACT.Ln).then_inc(ln, 1)
                act.wait_ge(ln, UP + 1)
                act.activation(st[:, 2, :], st[:, 2, :], ACT.Exp, scale=-0.5).then_inc(rs0, 1)
                for c in range(KT):
                    act.wait_ge(xt, UP + c + 1)
                    act.activation(u[:, c, :], XT[c % 2][:, 0:CTX], ACT.Identity, bias=modv[:, 2, c:c + 1],
                                   scale=gains[:, 2, c:c + 1]).then_inc(um, 1)
                act.wait_ge(k_done, UP + 1)
                act.activation(ksq[:], BK[:, 0:CTX], ACT.Square).then_inc(k_read, 1)
                act.activation(kraw[:], BK[:, 0:CTX], ACT.Copy).then_inc(k_read, 1)
                act.wait_ge(v_done, UP + 1)
                act.activation(vraw[:], BV[:, 0:CTX], ACT.Copy).then_inc(v_read, 1)
                act.wait_ge(kstep, UP + 1)
                act.activation(krs[:], kms[:], ACT.Ln).then_inc(ln, 1)
                act.wait_ge(ln, UP + 2)
                act.activation(krs[:], krs[:], ACT.Exp, scale=-0.5).then_inc(rs0, 1)
                act.wait_ge(vt, UP + 1)
                act.activation(vout[:], BT[:, 0:CTX].rearrange("p (t i) -> p t i", t=NC), ACT.Copy).then_inc(v_out, 1)

            @block.vector
            def _(dve):
                dve.wait_ge(sq, UP + NC)
                dve.tensor_scalar(st[:, 1, :], st[:, 0, :], 1.0 / D, EPS, ALU.mult, ALU.add).then_inc(ms, 1)
                dve.wait_ge(whi, UP + 1)
                dve.tensor_tensor(w_lo[:], w[:], w_hi[:].bitcast(F32), ALU.subtract).then_inc(wlo, 1)
                dve.wait_ge(rs0, UP + 1)
                newton_rsqrt(dve, st[:, 2, :], st[:, 1, :], st[:, 3, :], step, 0)
                dve.wait_ge(step, UP + 4)
                for t in range(NC):
                    dve.tensor_scalar(xc[:, t, :], xc[:, t, :], st[:, 2, t:t + 1], None, ALU.mult).then_inc(xn, 1)
                for c in range(KT):
                    dve.wait_ge(um, UP + c + 1)
                    dve.tensor_copy(u_hi[:, c, :], u[:, c, :]).then_inc(hi, 1)
                    dve.wait_ge(hi, UP + c + 1)
                    dve.tensor_tensor(u_lo[:, c, :], u[:, c, :], u_hi[:, c, :].bitcast(F32), ALU.subtract).then_inc(lo, 1)
                dve.wait_ge(ssum, UP + 1)
                dve.tensor_scalar(kms[:], BS[:, 0:CTX], 1.0 / HD, EPS, ALU.mult, ALU.add).then_inc(kstep, 1)
                dve.wait_ge(rs0, UP + 2)
                newton_rsqrt(dve, krs[:], kms[:], kt[:], step, 4)
                dve.wait_ge(step, UP + 8)
                dve.wait_ge(k_read, UP + 2)
                dve.scalar_tensor_tensor(kraw[:], kraw[:], cols[:, at_kw:at_kw + 1], krs[:], ALU.mult, ALU.mult).then_inc(k_out, 1)

            @block.tensor
            def _(pe):
                pe.wait_ge(xn, UP + NC)
                for c in range(KT):
                    if c >= 2:
                        pe.wait_ge(um, UP + c - 1)
                    for t in range(NC):
                        last = pe.transpose(XT[c % 2][:, P * t:P * (t + 1)], xc[:, t, P * c:P * (c + 1)], ident[:])
                    last.then_inc(xt, 1)
                pe.wait_ge(wlo, UP + 1)
                for bank, done, col0 in ((BK, k_done, 0), (BV, v_done, P)):
                    for k in range(KT):
                        pe.wait_ge(lo, UP + k + 1)
                        for n, (a, b) in enumerate(((w_hi, u_hi), (w_hi, u_lo), (w_lo, u_hi))):
                            last = pe.matmul(bank[:, 0:CTX], a[:, k, col0:col0 + P], b[:, k, :], start=(k == 0 and n == 0),
                                             stop=(k == KT - 1 and n == 2))
                    last.then_inc(done, 1)
                pe.wait_ge(ones_landed, UP + 16)
                pe.wait_ge(k_read, UP + 1)
                pe.matmul(BS[:, 0:CTX], head_ones[:], ksq[:], start=True, stop=True).then_inc(ssum, 1)
                pe.wait_ge(v_read, UP + 1)
                for t in range(NC):
                    last = pe.transpose(BT[:, P * t:P * (t + 1)], vraw[:, P * t:P * (t + 1)], ident[:])
                last.then_inc(vt, 1)


def projections(nc, d, keep):
    NW = 22
    COLS = ([c for i in range(4) for c in (COL_A + P * i, COL_G + P * i)] + [COL_Q + P * i for i in range(4)] + [COL_K, COL_V]
            + [COL_ZA + P * i for i in range(4)] + [COL_ZC + P * i for i in range(4)])
    NTAP = 4 * TAPS
    TAPS_OF_TURN = [10, 10, 8] + [0] * 2 + [8] * 5 + [2] * 6 + [8] * 4 + [6] * 2
    CARRIED = sum(TAPS_OF_TURN[:4])
    assert sum(TAPS_OF_TURN) == NTAP and sum(TAPS_OF_TURN[4:8]) <= NTAP // 2
    with ExitStack() as ctx:
        sb, ps, sem = pools(nc, ctx, "proj")
        cols, modv, gains, ident = keep["cols"], keep["modv"], keep["gains"], keep["ident"]
        u_hi = [sb(f"u_hi{i}", [P, KT, TB], F32R) for i in range(2)]
        u_lo = [sb(f"u_lo{i}", [P, KT, TB], F32R) for i in range(2)]
        hbuf = sb("hbuf", [P, KT, TB])
        w_raw = [sb(f"w_raw{s}", [P, KT, P]) for s in range(4)]
        w_hi = [sb(f"w_hi{s}", [P, KT, P], F32R) for s in range(2)]
        w_lo = [sb(f"w_lo{s}", [P, KT, P], F32R) for s in range(2)]
        UB = 2 * LAG
        conv_in = sb("conv_in", [P, 4, UB + SEQ + PAD])
        CW = TB + LAG
        conv_acc = sb("conv_acc", [P, 4, CW])
        conv_w = sb("conv_w", [P, 4, TAPS])
        rot_t, head_ones, ones = sb("rot_t", [P, P]), sb("head_ones", [P, P]), sb("ones", [P, P])
        cos, sin = sb("cos", [P, TB]), sb("sin", [P, TB])
        ga, gt = sb("ga", [P, 2, TB]), sb("gt", [P, 2, TB])
        qraw = sb("qraw", [P, 6, TB])
        conv_rows = qraw[0:TAPS, 4, :]
        qsq = sb("qsq", [P, TB])        
        qms, qrs, qt = sb("qms", [P, 2, TB]), sb("qrs", [P, 2, TB]), sb("qt", [P, TB])
        G = [ps(f"bank_g{i}", [P, TB]) for i in range(2)]
        BN, BS, BR, BV = (ps(n, [P, TB]) for n in ("bank_n", "bank_s", "bank_r", "bank_v"))
        consts, cleared, conv_w_turned, conv_w_done = (sem(n) for n in ("consts", "cleared", "conv_w_turned", "conv_w_done"))
        w_landed = [sem(f"w_landed{s}") for s in range(4)]
        w_rest = [sem(f"w_rest{s}") for s in range(4)]
        w_rounded, proj, evac = sem("w_rounded"), sem("proj"), sem("evac")
        h_landed, hsq, hadded, nsum, nms, nln, nrs0, nstep, hm, u_done_hi, u_done = (
            sem(n) for n in ("h_landed", "hsq", "hadded", "nsum", "nms", "nln", "nrs0", "nstep", "hm", "u_done_hi", "u_done"))
        glu, taps, conv_stored = sem("glu"), sem("taps"), sem("conv_stored")
        q_sq, q_sum, q_ms, q_ln, q_rs0, q_step, q_n, q_rot, q_sin, q_cos, q_done, q_stored, cs_landed = (
            sem(n) for n in ("q_sq", "q_sum", "q_ms", "q_ln", "q_rs0", "q_step", "q_n", "q_rot", "q_sin", "q_cos", "q_done", "q_stored", "cs_landed"))
        vt, v_out, v_stored, z_done = (sem(n) for n in ("vt", "v_out", "v_stored", "z_done"))
        z_stored = [sem(f"z_stored{i}") for i in range(2)]
        zout = sb("zout", [P, 2, TB])
        vraw = qraw[:, 5, :]
        vout = vraw.rearrange("p (t i) -> p t i", t=NT)
        hms, hrs, ht = sb("hms", [P, TB]), sb("hrs", [P, TB]), sb("ht", [P, TB])
        hsquare = (ht, hms)
        spare = sb("spare", [P, 1])
        qsin = sb("qsin", [P, 2, TB])
        zraw = sem("zraw")

        w_in = d["w_in_2"].rearrange("(k p) n -> p k n", p=P)
        h1t = d["h1t"].rearrange("(c p) t -> p c t", p=P)
        conv_y = d["conv_y"].rearrange("(c p) t -> p c t", p=P)
        vtok = d["vtok"].rearrange("(t p) n -> p t n", p=P)

        def add_h(eng, b, k):
            eng.wait_ge(hsq, UP + b * KT + k + 1)
            if k > 1:
                eng.wait_ge(hadded, UP + b * (KT - 1) + k - 1)
            eng.tensor_tensor(hrs[:], hsquare[0][:] if k == 1 else hrs[:], hsquare[k % 2][:], ALU.add).then_inc(hadded, 1)

        nc.all_engine_barrier()
        with nc.Block() as block:
            @block.sync
            def _(sp):
                sp.dma_start(hbuf[:], h1t[:, :, 0:TB]).then_inc(h_landed, 16)
                for dst, src in ((rot_t, "rot_t"), (head_ones, "head_ones"), (ones, "ones"), (conv_rows, "conv_w_2")):
                    sp.dma_start(dst[:], d[src]).then_inc(consts, 16)

                def load(it, n):
                    s, r = n % 4, n // 4
                    sp.wait_ge(w_rest[s], UP + it * 11 + r)
                    sp.dma_start(w_raw[s][:], w_in[:, :, COLS[n % NW]:COLS[n % NW] + P]).then_inc(w_landed[s], 16)
                for n in range(4):
                    load(0, n)
                sp.wait_ge(cleared, UP + 3)
                sp.wait_ge(u_done, UP + 8)
                sp.dma_start(hbuf[:], h1t[:, :, TB:2 * TB]).then_inc(h_landed, 16)
                with sp.Fori(0, NB // 2) as it:
                    for half in range(2):
                        b = it * 2 + half
                        sp.wait_ge(q_done, UP + b * 5)
                        for dst, src in ((cos, "cos"), (sin, "sin")):
                            sp.dma_start(dst[:], d[src][:, ds(b * TB, TB)]).then_inc(cs_landed, 16)
                        for j in range(NW):
                            load(it, half * NW + j + 4)
                            if j == 20:
                                sp.wait_ge(u_done, UP + b * 8 + 16)
                                sp.dma_start(hbuf[:], h1t[:, :, ds(((b + 2) % NB) * TB, TB)]).then_inc(h_landed, 16)
                            if j == 3:
                                sp.wait_ge(taps, UP + b * NTAP + CARRIED)
                                sp.dma_start(conv_y[:, :, ds(b * TB, CW)], conv_acc[:]).then_inc(conv_stored, 16)
                            if 16 <= j < 21:
                                i = j - 16
                                sp.wait_ge(q_done, UP + b * 5 + i + 1)
                                dst = (d["qt"][P * i:P * (i + 1), ds(b * TB, TB)] if i < 4 else
                                       d["kt"][:, ds(b * TB + CTX, TB)])
                                sp.dma_start(dst, qraw[:, i, :]).then_inc(q_stored, 16)
                            if j == 18:
                                sp.wait_ge(v_out, UP + b + 1)
                                sp.dma_start(vtok[:, ds(b * NT + CTX // P, NT), :], vout).then_inc(v_stored, 16)
                            if j >= 16:
                                for i in ((j - 16,) if j < NW - 1 else (5, 6, 7)):
                                    sp.wait_ge(z_done, UP + b * 8 + i + 1)
                                    dst = d["za" if i < 4 else "zc"][P * (i % 4):P * (i % 4 + 1), ds(b * TB, TB)]
                                    sp.dma_start(dst, zout[:, i % 2, :]).then_inc(z_stored[i % 2], 16)
                sp.wait_ge(taps, UP + NB * NTAP + CARRIED)
                sp.dma_start(conv_y[:, :, NB * TB:NB * TB + CW], conv_acc[:]).then_inc(conv_stored, 16)
                sp.wait_ge(conv_stored, UP + 16 * (NB + 1))
                sp.wait_ge(q_stored, UP + 16 * 5 * NB)
                sp.wait_ge(v_stored, UP + 16 * NB)
                for i in range(2):
                    sp.wait_ge(z_stored[i], UP + 16 * 4 * NB)
                sp.wait_ge(h_landed, UP + 16 * (NB + 2))
                for s in range(4):
                    sp.wait_ge(w_landed[s], UP + 16 * (11 * NB // 2 + 1))

            @block.gpsimd
            def _(pool):
                pool.memset(conv_in[:], 0.0).then_inc(cleared, 2)
                pool.memset(conv_acc[:], 0.0).then_inc(cleared, 1)

                def rest(it, n):
                    s = n % 4
                    pool.wait_ge(w_rounded, UP + it * 44 + n + 1)
                    pool.tensor_tensor(w_lo[n % 2][:], w_raw[s][:], w_hi[n % 2][:].bitcast(F32), ALU.subtract).then_inc(w_rest[s], 1)
                rest(0, 0)
                with pool.Fori(0, NB // 2) as it:
                    for n in range(44):
                        rest(it, n + 1)
                        b, j = it * 2 + n // NW, n % NW
                        if 4 <= j < 4 + KT // 2:
                            if j == 4:
                                pool.wait_ge(u_done, UP + b * KT + KT)
                            for k in range(max(2 * (j - 4), 1), 2 * (j - 4) + 2):
                                add_h(pool, b + 1, k)
                        if 14 <= j < 19:
                            i = j - 14
                            pool.wait_ge(q_sin, UP + b * 5 + i + 1)
                            pool.wait_ge(q_cos, UP + b * 5 + i + 1)
                            pool.tensor_tensor(qraw[:, i, :], qraw[:, i, :], qsin[:, i % 2, :], ALU.add).then_inc(q_done, 1)
                        if 13 <= j < 18:
                            i = j - 13
                            if i == 0:
                                pool.wait_ge(cs_landed, UP + b * 32 + 32)
                            pool.wait_ge(q_rot, UP + b * 5 + i + 1)
                            pool.tensor_tensor(qraw[:, i, :], qraw[:, i, :], cos[:], ALU.mult).then_inc(q_cos, 1)

            @block.tensor
            def _(pe):
                pe.wait_ge(consts, UP + 64)
                for c in range(4):
                    last = pe.transpose(BS[:, TAPS * c:TAPS * (c + 1)], conv_rows[:, P * c:P * (c + 1)], ident[0:TAPS, 0:TAPS])
                last.then_inc(conv_w_turned, 1)

                def sum_h(b):
                    pe.wait_ge(nms, UP + b)
                    pe.wait_ge(hadded, UP + (b + 1) * (KT - 1))
                    pe.matmul(BN[:], ones[:], hrs[:], start=True, stop=True).then_inc(nsum, 1)
                sum_h(0)

                def turn(it, half, j):
                        b, n = it * 2 + half, half * NW + j
                        pe.wait_ge(w_rest[n % 4], UP + it * 11 + n // 4 + 1)
                        pe.wait_ge(evac, UP + b * NW + j)
                        for k in range(KT):
                            if j == 0:
                                pe.wait_ge(u_done, UP + b * 8 + k + 1)
                            for n, (w, a) in enumerate(((w_hi, u_hi), (w_hi, u_lo), (w_lo, u_hi))):
                                last = pe.matmul(G[j % 2][:], w[j % 2][:, k, :], a[half][:, k, :], start=(k == 0 and n == 0),
                                                 stop=(k == KT - 1 and n == 2))
                        last.then_inc(proj, 1)
                        if 12 <= j < 17:
                            pe.wait_ge(q_n, UP + b * 5 + j - 11)
                            pe.wait_ge(q_sin, UP + b * 5 + j - 12)
                            pe.matmul(BR[:], rot_t[:], qraw[:, j - 12, :], start=True, stop=True).then_inc(q_rot, 1)
                        if 9 <= j < 14:
                            pe.wait_ge(q_sq, UP + b * 5 + j - 8)
                            pe.wait_ge(q_ms, UP + b * 5 + j - 9)
                            pe.matmul(BS[:], head_ones[:], qsq[:], start=True, stop=True).then_inc(q_sum, 1)
                        if j == 15:
                            pe.wait_ge(evac, UP + b * NW + 15)
                            pe.wait_ge(v_out, UP + b)
                            for t in range(NT):
                                last = pe.transpose(BV[:, P * t:P * (t + 1)], vraw[:, P * t:P * (t + 1)], ident[:])
                            last.then_inc(vt, 1)
                        if j == 8:
                            sum_h(b + 1)
                pe.wait_ge(conv_w_done, UP + 1)
                with pe.Fori(0, NB // 2) as it:
                    for half in range(2):
                        for j in range(NW):
                            turn(it, half, j)

            @block.scalar
            def _(act):
                def round_tile(it, n):
                    s = n % 4
                    act.wait_ge(w_landed[s], UP + it * 176 + 16 * (n // 4) + 16)
                    if n:
                        act.wait_ge(proj, UP + it * 44 + n - 1)
                    act.activation(w_hi[n % 2][:], w_raw[s][:], ACT.Copy).then_inc(w_rounded, 1)

                def square_h(b, k):
                    if k >= 2:
                        act.wait_ge(hadded, UP + b * (KT - 1) + max(k - 2, 1))
                    act.activation(hsquare[k % 2][:], hbuf[:, k, :], ACT.Square).then_inc(hsq, 1)

                def rsqrt_h(b):
                    act.wait_ge(nms, UP + b + 1)
                    act.activation(hrs[:], hms[:], ACT.Ln).then_inc(nln, 1)
                    act.wait_ge(nln, UP + b + 1)
                    act.activation(hrs[:], hrs[:], ACT.Exp, scale=-0.5).then_inc(nrs0, 1)

                act.wait_ge(h_landed, UP + 16)
                round_tile(0, 0)
                for k in range(KT):
                    square_h(0, k)
                rsqrt_h(0)
                act.wait_ge(conv_w_turned, UP + 1)
                act.activation(conv_w[:].rearrange("p c k -> p (c k)"), BS[:, 0:NTAP], ACT.Copy, scale=0.5).then_inc(conv_w_done, 1)
                act.wait_ge(conv_w_done, UP + 1)
                act.activation(spare[:], conv_w[:, 0, 0:1], ACT.Copy).then_inc(evac, 1)
                with act.Fori(0, NB // 2) as it:
                    for half in range(2):
                        b = it * 2 + half
                        for j in range(NW):
                            round_tile(it, half * NW + j + 1)
                            if 10 <= j < 15:
                                act.wait_ge(q_ms, UP + b * 5 + j - 9)
                                i = j - 10
                                act.wait_ge(q_n, UP + b * 5 + max(i - 1, 0))
                                act.activation(qrs[:, i % 2, :], qms[:, i % 2, :], ACT.Ln).then_inc(q_ln, 1)
                                act.wait_ge(q_ln, UP + b * 5 + j - 9)
                                act.activation(qrs[:, i % 2, :], qrs[:, i % 2, :], ACT.Exp, scale=-0.5).then_inc(q_rs0, 1)
                            if 4 <= j < 4 + KT // 2:
                                if j == 4:
                                    act.wait_ge(h_landed, UP + b * 16 + 32)
                                    act.wait_ge(nstep, UP + b * 4 + 4)
                                for k in range(2 * (j - 4), 2 * (j - 4) + 2):
                                    square_h(b + 1, k)
                            act.wait_ge(proj, UP + b * NW + j + 1)
                            if j < 8:
                                if j >= 4:
                                    act.wait_ge(glu, UP + b * 4 + j // 2 - 1)
                                else:
                                    act.wait_ge(z_done, UP + b * 8)
                                if j % 2 == 0:
                                    act.activation(ga[:, j // 2 % 2, :], G[0][:], ACT.Copy).then_inc(evac, 1)
                                else:
                                    act.activation(gt[:, j // 2 % 2, :], G[1][:], ACT.Tanh, scale=0.5).then_inc(evac, 1)
                            elif j < 13:
                                i = j - 8
                                if i == 0:
                                    act.wait_ge(q_sum, UP + b * 5)
                                    act.wait_ge(q_stored, UP + b * 80)
                                else:
                                    act.wait_ge(q_sum, UP + b * 5 + i)
                                act.activation(qsq[:], G[j % 2][:], ACT.Square).then_inc(q_sq, 1)
                                act.activation(qraw[:, i, :], G[j % 2][:], ACT.Copy).then_inc(evac, 1)
                            elif j == 13:
                                act.wait_ge(v_stored, UP + b * 16)
                                act.activation(vraw, G[j % 2][:], ACT.Copy).then_inc(evac, 1)
                            else:
                                i = j - 14
                                if i < 2:
                                    act.wait_ge(glu, UP + b * 4 + 4)
                                else:
                                    act.wait_ge(z_done, UP + b * 8 + i - 1)
                                act.activation(ga[:, i % 2, :], G[j % 2][:], ACT.Copy).then_inc(zraw, 1)
                                act.activation(gt[:, i % 2, :], G[j % 2][:], ACT.Tanh, scale=0.5).then_inc(evac, 1)
                            if j == 9:
                                rsqrt_h(b + 1)
                            if j == 16:
                                act.wait_ge(vt, UP + b + 1)
                                act.activation(vout, BV[:].rearrange("p (t i) -> p t i", t=NT), ACT.Copy).then_inc(v_out, 1)

            @block.vector
            def _(dve):
                def mean_h(b):
                    dve.wait_ge(nsum, UP + b + 1)
                    dve.tensor_scalar(hms[:], BN[:], 1.0 / D, EPS, ALU.mult, ALU.add).then_inc(nms, 1)

                def rs_h(b):
                    dve.wait_ge(nrs0, UP + b + 1)
                    newton_rsqrt(dve, hrs[:], hms[:], ht[:], nstep, b * 4)
                    dve.wait_ge(nstep, UP + b * 4 + 4)

                def modulate_h(b, half, k):
                    dve.scalar_tensor_tensor(hbuf[:, k, :], hbuf[:, k, :], gains[:, 1, k:k + 1], hrs[:], ALU.mult, ALU.mult).then_inc(hm, 1)
                    dve.wait_ge(hm, UP + b * 8 + k + 1)
                    dve.tensor_scalar(u_hi[half][:, k, :], hbuf[:, k, :], modv[:, 1, k:k + 1], None, ALU.add).then_inc(u_done_hi, 1)
                    dve.wait_ge(u_done_hi, UP + b * 8 + k + 1)
                    dve.scalar_tensor_tensor(u_lo[half][:, k, :], hbuf[:, k, :], modv[:, 1, k:k + 1], u_hi[half][:, k, :].bitcast(F32),
                                             ALU.add, ALU.subtract).then_inc(u_done, 1)

                def tap(b, m, before):
                    k, c = m % (2 * TAPS) // 2, m // (2 * TAPS) * 2 + m % 2
                    src = conv_in[:, c, ds(b * TB + (UB - LAG - PAD + k), CW)]
                    if k == 0:
                        dve.tensor_scalar(conv_acc[:, c, :], src, conv_w[:, c, 0:1], None, ALU.mult).then_inc(taps, 1)
                    else:
                        dve.wait_ge(taps, UP + before)
                        dve.scalar_tensor_tensor(conv_acc[:, c, :], src, conv_w[:, c, k:k + 1], conv_acc[:, c, :], ALU.mult, ALU.add).then_inc(taps, 1)

                def carried_taps(b, former, first, count):
                    for i in range(first, first + count):
                        tap(former, NTAP - CARRIED + i, b * NTAP + max(i - 1, 0))
                at_qw, at_kw = VROWS["q_norm_w_2"][0], VROWS["k_norm_w_2"][0]
                for k in range(1, KT):
                    add_h(dve, 0, k)
                mean_h(0)
                rs_h(0)
                for k in range(KT):
                    modulate_h(0, 0, k)
                dve.wait_ge(cleared, UP + 3)
                dve.wait_ge(conv_w_done, UP + 1)
                with dve.Fori(0, NB // 2) as it:
                    for half in range(2):
                        b = it * 2 + half
                        former = dve.snap((b + (NB - 1)) % NB)
                        for j in range(NW):
                            if j < 8 and j % 2:
                                if j == 5:
                                    dve.wait_ge(taps, UP + b * NTAP + CARRIED)
                                dve.wait_ge(evac, UP + b * NW + j + 2)
                                dve.scalar_tensor_tensor(conv_in[:, j // 2, ds(b * TB + UB, TB)], gt[:, j // 2 % 2, :], 1.0, ga[:, j // 2 % 2, :],
                                                         ALU.add, ALU.mult).then_inc(glu, 1)
                            if 11 <= j < 16:
                                i = j - 11
                                dve.wait_ge(q_rs0, UP + b * 5 + i + 1)
                                newton_rsqrt(dve, qrs[:, i % 2, :], qms[:, i % 2, :], qt[:], q_step, b * 20 + i * 4)
                                dve.wait_ge(q_step, UP + b * 20 + i * 4 + 4)
                                at = at_qw if i < 4 else at_kw
                                dve.scalar_tensor_tensor(qraw[:, i, :], qraw[:, i, :], cols[:, at:at + 1], qrs[:, i % 2, :], ALU.mult, ALU.mult).then_inc(q_n, 1)
                            if 13 <= j < 18:
                                i = j - 13
                                if i == 0:
                                    dve.wait_ge(cs_landed, UP + b * 32 + 32)
                                dve.wait_ge(q_rot, UP + b * 5 + i + 1)
                                if i < 2:
                                    dve.wait_ge(q_done, UP + b * 5)
                                else:
                                    dve.wait_ge(q_done, UP + b * 5 + i - 1)
                                dve.tensor_tensor(qsin[:, i % 2, :], BR[:], sin[:], ALU.mult).then_inc(q_sin, 1)
                            if 9 <= j < 14:
                                dve.wait_ge(q_sum, UP + b * 5 + j - 8)
                                dve.tensor_scalar(qms[:, (j - 9) % 2, :], BS[:], 1.0 / HD, EPS, ALU.mult, ALU.add).then_inc(q_ms, 1)
                            if j == 9:
                                mean_h(b + 1)
                            if j == 11:
                                rs_h(b + 1)
                                dve.wait_ge(proj, UP + b * NW)
                            if 12 <= j < 12 + KT:
                                modulate_h(b + 1, 1 - half, j - 12)
                            if j >= 14:
                                i = j - 14
                                dve.wait_ge(zraw, UP + b * 8 + i + 1)
                                dve.wait_ge(evac, UP + b * NW + j + 2)
                                dve.wait_ge(z_stored[i % 2], UP + b * 64 + 16 * (i // 2))
                                dve.scalar_tensor_tensor(zout[:, i % 2, :], gt[:, i % 2, :], 1.0, ga[:, i % 2, :], ALU.add, ALU.mult).then_inc(z_done, 1)
                            if j == 5:
                                dve.wait_ge(glu, UP + b * 4 + 2)
                                dve.wait_ge(conv_stored, UP + b * 16 + 16)
                            if j == 8:
                                dve.wait_ge(glu, UP + b * 4 + 4)
                            done = sum(TAPS_OF_TURN[:j])
                            if done < CARRIED:
                                carried_taps(b, former, done, TAPS_OF_TURN[j])
                            else:
                                for m in range(done - CARRIED, done - CARRIED + TAPS_OF_TURN[j]):
                                    tap(b, m, b * NTAP + CARRIED + m - 1)
                carried_taps(NB, NB - 1, 0, CARRIED)


def attention(nc, d, keep):
    NKT = KEYS // P
    RING, SBANKS, MBANKS = 6, 2, 3
    WEIGH_LAG, SPLIT_LAG = 5, 2
    GROUP_STEPS = (NQH // NKV) * NB
    STEPS = NKV * GROUP_STEPS
    PIECES = [(qt, n) for qt in range(NT) for n in range(-(-KEYS // TB))]
    NP = len(PIECES)
    TURN_PIECES = [[] for _ in range(NKT)]
    for p in range(NP):
        TURN_PIECES[2 + p * 12 // NP].append(p)
    with ExitStack() as ctx:
        sb, ps, sem = pools(nc, ctx, "att")
        ident = keep["ident"]
        k_a = [sb(f"k_a{g}", [P, KEYS], F32R) for g in range(NKV)]
        k_b = [sb(f"k_b{g}", [HD + 1, KEYS], F32R) for g in range(NKV)]
        v_s = [sb(f"v_s{g}", [P, NKT, P], F32R) for g in range(NKV)]
        k_raw = sb("k_raw", [P, KEYS])
        v_raw = sb("v_raw", [P, NKT, HD])
        ones = sb("ones", [P, P])
        q_raw = [sb(f"q_raw{s}", [P, TB]) for s in range(2)]
        q_a = [sb(f"q_a{s}", [P, TB], F32R) for s in range(2)]
        q_b = [sb(f"q_b{s}", [HD + 1, TB], F32R) for s in range(2)]
        mx = sb("mx", [P, NT, 5])
        m = sb("m", [P, NT])
        mz = sb("mz", [P, NT, HD + 1])
        p_f = sb("p_f", [P, RING, TB])
        p_hi = sb("p_hi", [P, RING, TB], F32R)
        p_lo = sb("p_lo", [P, RING, TB], F32R)
        den = [sb(f"den{s}", [P, TB]) for s in range(2)]
        o_hi, o_out = sb("o_hi", [HD, TB]), sb("o_out", [HD, TB])
        recip = sb("recip", [P, NT])
        S = [ps(f"bank_s{i}", [P, TB]) for i in range(SBANKS)]
        M = [ps(f"bank_m{i}", [P, TB]) for i in range(MBANKS)]
        O = [ps(f"bank_o{i}", [P, TB]) for i in range(2)]
        B = ps("bank_b", [P, TB])
        (k_landed, v_landed, ones_landed, k_hi_done, k_lo_done, v_hi_done, v_lo_done, cleared, ones_row) = (
            sem(n) for n in ("k_landed", "v_landed", "ones_landed", "k_hi_done", "k_lo_done", "v_hi_done", "v_lo_done", "cleared", "ones_row"))
        loads_begun = sem("loads_begun")
        q_landed = [sem(f"q_landed{s}") for s in range(2)]
        q_hi_done, q_lo_done = sem("q_hi_done"), sem("q_lo_done")
        mx_done, mx_read, m_done, mz_done, row_done, row_read = (
            sem(n) for n in ("mx_done", "mx_read", "m_done", "mz_done", "row_done", "row_read"))
        s_done, p_done, hi_done, lo_done, den_done, pv_done = (
            sem(n) for n in ("s_done", "p_done", "hi_done", "lo_done", "den_done", "pv_done"))
        den_sum, o_hi_done, recip_done, r_row, o_sum, o_done, o_stored = (
            sem(n) for n in ("den_sum", "o_hi_done", "recip_done", "r_row", "o_sum", "o_done", "o_stored"))

        def need(eng, semaphore, n):
            if isinstance(n, int) and n <= 0:
                return
            eng.wait_ge(semaphore, UP + n)

        def steps(eng, body):
            last = GROUP_STEPS - 1
            for g in range(NKV):
                base = g * GROUP_STEPS
                body(base, 0, g, g - 1 if g else None, g)
                body(base + 1, 1, g, g, g)
                with eng.Fori(1, GROUP_STEPS // 2 - 1) as it:
                    for s in range(2):
                        body(it * 2 + (base + s), s, g, g, g)
                body(base + last - 1, 0, g, g, g)
                body(base + last, 1, g, g, g + 1 if g + 1 < NKV else None)

        nc.all_engine_barrier()
        with nc.Block() as block:
            @block.sync
            def _(sp):
                sp.dma_start(ones[:], d["ones"]).then_inc(ones_landed, 16)

                def load_q(i, s):
                    row, col = (i // NB) * HD, (i % NB) * TB
                    for half in range(2):
                        sp.dma_start(q_raw[s][HD * half:HD * (half + 1), :], d["qt"][ds(row, HD), ds(col, TB)]).then_inc(q_landed[s], 16)
                load_q(0, 0)
                for g in range(NKV):
                    if g:
                        sp.wait_ge(k_lo_done, UP + g)
                        sp.wait_ge(k_hi_done, UP + g)
                    for half in range(2):
                        sp.dma_start(k_raw[HD * half:HD * (half + 1), :], d["kt"][HD * g:HD * (g + 1), :]).then_inc(k_landed, 16)
                    if g:
                        sp.wait_ge(v_lo_done, UP + g)
                    sp.dma_start(v_raw[:], d["vtok"].rearrange("(t p) n -> p t n", p=P)[:, :, HD * g:HD * (g + 1)]).then_inc(v_landed, 16)
                    if g == 0:
                        load_q(1, 1)

                def body(i, s, g, before, after):
                    if not (isinstance(i, int) and i + 2 >= STEPS):
                        sp.wait_ge(q_hi_done, UP + 2 * i + 2)
                        sp.sem_inc(loads_begun, 1)
                        sp.wait_ge(q_lo_done, UP + i + 1)
                        sp.sem_inc(loads_begun, 1)
                        load_q(i + 2, s)
                    if before is not None:
                        sp.wait_ge(o_done, UP + i)
                        sp.dma_start(d["att"][ds(((i - 1) // NB) * HD, HD), ds(((i - 1) % NB) * TB, TB)], o_out[:]).then_inc(o_stored, 16)
                steps(sp, body)
                sp.wait_ge(o_done, UP + STEPS)
                sp.dma_start(d["att"][HD * (NQH - 1):HD * NQH, TB * (NB - 1):TB * NB], o_out[:]).then_inc(o_stored, 16)
                sp.wait_ge(o_stored, UP + 16 * STEPS)

            @block.gpsimd
            def _(pool):
                pool.memset(mz[:], 0.0).then_inc(cleared, 1)

                def body(i, s, g, before, after):
                    need(pool, den_sum, i - 1)
                    for kt in range(1, NKT):
                        pool.wait_ge(p_done, UP + i * NKT + kt + 1)
                        if kt > 1:
                            pool.wait_ge(den_done, UP + i * (NKT - 1) + kt - 1)
                        pool.tensor_tensor(den[s][:], p_f[:, 0, :] if kt == 1 else den[s][:], p_f[:, kt % RING, :], ALU.add).then_inc(den_done, 1)
                steps(pool, body)

            @block.tensor
            def _(pe):
                def piece(i, s, g, p):
                    qt, n = PIECES[p]
                    width = min(TB, KEYS - TB * n)
                    if p == 0:
                        pe.wait_ge(q_hi_done, UP + 2 * i + 2)
                        pe.wait_ge(q_lo_done, UP + i + 1)
                    need(pe, mx_read, i * NP + max(p - MBANKS + 1, 0))
                    pe.matmul(M[p % MBANKS][:, 0:width], q_a[s][:, P * qt:P * (qt + 1)], k_a[g][:, TB * n:TB * n + width],
                              start=True, stop=True).then_inc(mx_done, 1)

                def max_row(i):
                    pe.wait_ge(mz_done, UP + i + 1)
                    need(pe, o_done, i - 1)
                    for qt in range(NT):
                        last = pe.matmul(B[0:HD + 1, P * qt:P * (qt + 1)], mz[:, qt, :], ident[:], start=True, stop=True)
                    last.then_inc(row_done, 1)

                def weigh(i, s, g, kt):
                    pe.wait_ge(lo_done, UP + i * NKT + kt + 1)
                    if kt == 0:
                        need(pe, o_sum, i - 1)
                    pe.matmul(O[s][:], v_s[g][:, kt, :], p_hi[:, kt % RING, :], start=(kt == 0), stop=False)
                    pe.matmul(O[s][:], v_s[g][:, kt, :], p_lo[:, kt % RING, :], start=False, stop=(kt == NKT - 1)).then_inc(pv_done, 1)

                def sum_den(i, s):
                    pe.wait_ge(den_done, UP + (i + 1) * (NKT - 1))
                    pe.wait_ge(row_read, UP + i + 1)
                    for qt in range(NT):
                        last = pe.matmul(B[:, qt:qt + 1], den[s][:, P * qt:P * (qt + 1)], ones[:, 0:1], start=True, stop=True)
                    last.then_inc(den_sum, 1)

                def spread_reciprocal(i):
                    pe.wait_ge(recip_done, UP + i + 1)
                    for qt in range(NT):
                        last = pe.matmul(B[0:HD, P * qt:P * (qt + 1)], recip[:, qt:qt + 1].broadcast_to([P, HD]), ident[:],
                                         start=True, stop=True)
                    last.then_inc(r_row, 1)

                def body(i, s, g, before, after):
                    pe.wait_ge(row_read, UP + i + 1)
                    for kt in range(NKT):
                        need(pe, p_done, i * NKT + kt - SBANKS + 1)
                        keys = slice(P * kt, P * (kt + 1))
                        pe.matmul(S[kt % SBANKS][:], k_a[g][:, keys], q_a[s][:], start=True, stop=False)
                        pe.matmul(S[kt % SBANKS][:], k_b[g][:, keys], q_b[s][:], start=False, stop=True).then_inc(s_done, 1)
                        if kt >= WEIGH_LAG:
                            weigh(i, s, g, kt - WEIGH_LAG)
                        elif before is not None:
                            weigh(i - 1, 1 - s, before, NKT - WEIGH_LAG + kt)
                        if kt == 4 and before is not None:
                            sum_den(i - 1, 1 - s)
                        if kt == 6 and before is not None:
                            spread_reciprocal(i - 1)
                        if after is not None:
                            for p in TURN_PIECES[kt]:
                                piece(i + 1, 1 - s, after, p)
                            if kt == 16:
                                max_row(i + 1)
                pe.wait_ge(ones_landed, UP + 16)
                pe.wait_ge(cleared, UP + 1)
                pe.wait_ge(k_hi_done, UP + 1)
                for p in range(NP):
                    piece(0, 0, 0, p)
                max_row(0)
                pe.wait_ge(k_lo_done, UP + NKV)
                pe.wait_ge(v_lo_done, UP + NKV)
                pe.wait_ge(ones_row, UP + NKV)
                steps(pe, body)
                for kt in range(NKT - WEIGH_LAG, NKT):
                    weigh(STEPS - 1, 1, NKV - 1, kt)
                sum_den(STEPS - 1, 1)
                spread_reciprocal(STEPS - 1)

            @block.scalar
            def _(act):
                def round_kv(g):
                    act.wait_ge(k_landed, UP + 32 * g + 32)
                    act.activation(k_a[g][:], k_raw[:], ACT.Copy).then_inc(k_hi_done, 1)
                    act.wait_ge(v_landed, UP + 16 * g + 16)
                    act.activation(v_s[g][:, :, 0:HD], v_raw[:], ACT.Copy).then_inc(v_hi_done, 1)

                def round_q(i, s):
                    act.wait_ge(q_landed[s], UP + 32 * (i // 2) + 32)
                    need(act, s_done, (i - 1) * NKT)
                    for dst, rows in ((q_a[s], P), (q_b[s], HD)):
                        act.activation(dst[0:rows, :], q_raw[s][0:rows, :], ACT.Copy).then_inc(q_hi_done, 1)

                def read_row(i, s):
                    act.wait_ge(row_done, UP + i + 1)
                    act.activation(q_b[s][HD:HD + 1, :], B[HD:HD + 1, :], ACT.Copy).then_inc(row_read, 1)

                def round_p(i, kt):
                    act.wait_ge(p_done, UP + i * NKT + kt + 1)
                    need(act, pv_done, i * NKT + kt - RING + 1)
                    act.activation(p_hi[:, kt % RING, :], p_f[:, kt % RING, :], ACT.Copy).then_inc(hi_done, 1)

                def finish(i, s):
                    act.wait_ge(pv_done, UP + (i + 1) * NKT)
                    need(act, o_done, i)
                    act.activation(o_hi[:], O[s][HD:P, :], ACT.Copy).then_inc(o_hi_done, 1)

                def body(i, s, g, before, after):
                    for kt in range(NKT):
                        act.wait_ge(s_done, UP + i * NKT + kt + 1)
                        need(act, lo_done, i * NKT + kt - RING + 1)
                        used = 1 if kt == RING else kt - RING + (kt < RING)
                        need(act, den_done, i * (NKT - 1) + used)
                        act.activation(p_f[:, kt % RING, :], S[kt % SBANKS][:], ACT.Exp, scale=float(HD) ** -0.5).then_inc(p_done, 1)
                        if kt:
                            round_p(i, kt - 1)
                        elif before is not None:
                            round_p(i - 1, NKT - 1)
                        if kt == 0 and after is not None:
                            round_q(i + 1, 1 - s)
                        if kt == 7 and before is not None:
                            finish(i - 1, 1 - s)
                        if kt == 16 and after is not None:
                            read_row(i + 1, 1 - s)
                round_q(0, 0)
                for g in range(NKV):
                    round_kv(g)
                read_row(0, 0)
                steps(act, body)
                round_p(STEPS - 1, NKT - 1)
                finish(STEPS - 1, 1)

            @block.vector
            def _(dve):
                def split_kv(g):
                    for t in range(NKT):
                        last = dve.tensor_copy(k_b[g][HD:HD + 1, P * t:P * (t + 1)], ones[HD:HD + 1, :])
                    last.then_inc(ones_row, 1)
                    dve.wait_ge(k_hi_done, UP + g + 1)
                    dve.tensor_tensor(k_b[g][0:HD, :], k_raw[0:HD, :], k_a[g][0:HD, :].bitcast(F32), ALU.subtract).then_inc(k_lo_done, 1)
                    dve.wait_ge(v_hi_done, UP + g + 1)
                    dve.tensor_tensor(v_s[g][:, :, HD:P], v_raw[:], v_s[g][:, :, 0:HD].bitcast(F32), ALU.subtract).then_inc(v_lo_done, 1)

                def split_q(i, s):
                    dve.wait_ge(q_hi_done, UP + 2 * i + 2)
                    dve.tensor_tensor(q_a[s][HD:P, :], q_raw[s][HD:P, :], q_a[s][HD:P, :].bitcast(F32), ALU.subtract).then_inc(q_lo_done, 1)

                def reduce(i, p):
                    qt, n = PIECES[p]
                    dve.wait_ge(mx_done, UP + i * NP + p + 1)
                    if p == 0:
                        need(dve, m_done, i)
                    dve.reduce_max(mx[:, qt, n:n + 1], M[p % MBANKS][:, 0:min(TB, KEYS - TB * n)], AX_X).then_inc(mx_read, 1)

                def column(i):
                    dve.wait_ge(mx_read, UP + (i + 1) * NP)
                    need(dve, mz_done, i)
                    dve.reduce_max(m[:], mx[:], AX_X).then_inc(m_done, 1)
                    dve.wait_ge(m_done, UP + i + 1)
                    dve.wait_ge(cleared, UP + 1)
                    need(dve, row_done, i)
                    dve.tensor_scalar(mz[:, :, HD], m[:], -1.0, None, ALU.mult).then_inc(mz_done, 1)

                def split_p(i, kt):
                    dve.wait_ge(hi_done, UP + i * NKT + kt + 1)
                    need(dve, pv_done, i * NKT + kt - RING + 1)
                    dve.tensor_tensor(p_lo[:, kt % RING, :], p_f[:, kt % RING, :], p_hi[:, kt % RING, :].bitcast(F32), ALU.subtract).then_inc(lo_done, 1)

                def finish(i, s):
                    dve.wait_ge(o_hi_done, UP + i + 1)
                    dve.tensor_tensor(o_hi[:], O[s][0:HD, :], o_hi[:], ALU.add).then_inc(o_sum, 1)
                    dve.wait_ge(r_row, UP + i + 1)
                    dve.wait_ge(o_sum, UP + i + 1)
                    need(dve, o_stored, 16 * i)
                    dve.tensor_tensor(o_out[:], o_hi[:], B[0:HD, :], ALU.mult).then_inc(o_done, 1)

                def invert(i):
                    dve.wait_ge(den_sum, UP + i + 1)
                    need(dve, r_row, i)
                    dve.reciprocal(recip[:], B[:, 0:NT]).then_inc(recip_done, 1)

                def body(i, s, g, before, after):
                    for kt in range(NKT):
                        if kt >= SPLIT_LAG:
                            split_p(i, kt - SPLIT_LAG)
                        elif before is not None:
                            split_p(i - 1, NKT - SPLIT_LAG + kt)
                        if kt == 0 and after is not None:
                            split_q(i + 1, 1 - s)
                        if after is not None:
                            for p in TURN_PIECES[kt]:
                                reduce(i + 1, p)
                            if kt == 14:
                                column(i + 1)
                        if kt == 4 and before is not None:
                            invert(i - 1)
                        if kt == 8 and before is not None:
                            finish(i - 1, 1 - s)
                KV_SPLIT_AT = [4 + 8 * g for g in range(NKV)]
                dve.wait_ge(ones_landed, UP + 16)
                split_q(0, 0)
                for p in range(NP):
                    reduce(0, p)
                    if p in KV_SPLIT_AT:
                        split_kv(KV_SPLIT_AT.index(p))
                column(0)
                steps(dve, body)
                for kt in range(NKT - SPLIT_LAG, NKT):
                    split_p(STEPS - 1, kt)
                invert(STEPS - 1)
                finish(STEPS - 1, 1)


def output(nc, d, keep):
    NC = 4
    TILES = NC + KT
    with ExitStack() as ctx:
        sb, ps, sem = pools(nc, ctx, "out")
        cols, modv, ident = keep["cols"], keep["modv"], keep["ident"]

        def col(name, j):
            at = VROWS[name][0] + j
            return cols[:, at:at + 1]
        wo_hi, wo_lo = sb("wo_hi", [P, KT, D], F32R), sb("wo_lo", [P, KT, D], F32R)
        wp_hi, wp_lo = sb("wp_hi", [P, NC, TB], F32R), sb("wp_lo", [P, NC, TB], F32R)
        y = sb("y", [P, NC, TB])
        at = sb("at", [P, NC, TB])
        z = sb("z", [P, KT, TB])
        h1 = sb("h1", [P, KT, TB])
        c_hi, c_lo = sb("c_hi", [P, NC, TB], F32R), sb("c_lo", [P, NC, TB], F32R)
        f_hi, f_lo = sb("f_hi", [P, KT, TB], F32R), sb("f_lo", [P, KT, TB], F32R)
        sq = sb("sq", [P, TB])
        acc = sb("acc", [P, TB])
        th = sb("th", [P, TB])
        rs = sb("rs", [P, TB])
        ob = sb("ob", [P, 2, NT, P])
        ones = sb("ones", [P, P])
        half_lnb = sb("half_lnb", [P, NC])
        w_raw = [h1[:].rearrange("p a b -> p (a b)")[:, D * i:D * (i + 1)] for i in range(4)]
        G = [ps(f"bank_g{i}", [P, TB]) for i in range(2)]
        T = [ps(f"bank_t{i}", [P, TB]) for i in range(2)]
        BM, BV = ps("bank_m", [P, TB]), ps("bank_v", [P, TB])
        w_landed = [sem(f"w_landed{i}") for i in range(4)]
        loads_begun = sem("loads_begun")
        ones_landed, w_hi_done, w_lo_done, lnb_done = (sem(n) for n in ("ones_landed", "w_hi_done", "w_lo_done", "lnb_done"))
        y_landed, at_landed, za_landed, zc_landed, h1_landed = (
            sem(n) for n in ("y_landed", "at_landed", "za_landed", "zc_landed", "h1_landed"))
        biased, mean_sum, centred, squared, var_sum, var_done, ln_done, rs0_done, rs_step, normed, tanh_done, shifted, swished, c_hi_done, c_lo_done = (
            sem(n) for n in ("biased", "mean_sum", "centred", "squared", "var_sum", "var_done", "ln_done", "rs0_done", "rs_step",
                             "normed", "tanh_done", "shifted", "swished", "c_hi_done", "c_lo_done"))
        prod, gated, f_hi_done, f_lo_done, x_out, turned, t_read = (
            sem(n) for n in ("prod", "gated", "f_hi_done", "f_lo_done", "x_out", "turned", "t_read"))
        stored = [sem(f"stored{i}") for i in range(2)]
        wp_lo_done, gate_halved, y_added, sq_added = (sem(n) for n in ("wp_lo_done", "gate_halved", "y_added", "sq_added"))
        half_gate = sb("half_gate", [P, KT])
        NWT = KT + 2

        def tiles(name):
            return d[name].rearrange("(c p) t -> p c t", p=P)

        nc.all_engine_barrier()
        with nc.Block() as block:
            @block.sync
            def _(sp):
                sp.dma_start(ones[:], d["ones"]).then_inc(ones_landed, 16)
                y_src = tiles("conv_y")
                sp.dma_start(y[:], y_src[:, :, CONV_AT:CONV_AT + TB]).then_inc(y_landed, 16)
                for n in range(NWT):
                    if 4 <= n < 6:
                        sp.wait_ge(wp_lo_done, UP + n - 3)
                    elif n >= 6:
                        sp.wait_ge(w_lo_done, UP + n - 5)
                    if n < 2:
                        src = d["w_pw_2"].rearrange("(k p) n -> p k n", p=P)[:, 2 * n:2 * n + 2, :]
                        dst = w_raw[n % 4].rearrange("p (k n) -> p k n", k=2)
                    else:
                        src, dst = d["w_out_2"][P * (n - 2):P * (n - 1), :], w_raw[n % 4]
                    sp.dma_start(dst, src).then_inc(w_landed[n % 4], 16)
                    if n == 3:
                        sp.dma_start(at[:], tiles("att")[:, :, 0:TB]).then_inc(at_landed, 16)
                        sp.dma_start(z[:, 0:NC, :], tiles("za")[:, :, 0:TB]).then_inc(za_landed, 16)
                        sp.dma_start(z[:, NC:KT, :], tiles("zc")[:, :, 0:TB]).then_inc(zc_landed, 16)
                sp.wait_ge(w_lo_done, UP + KT)
                sp.dma_start(h1[:], tiles("h1t")[:, :, 0:TB]).then_inc(h1_landed, 16)
                with sp.Fori(0, NB) as b:
                    nxt = sp.snap((b + 1) % NB)
                    sp.wait_ge(c_lo_done, UP + 4 * b + 4)
                    sp.sem_inc(loads_begun, 1)
                    sp.dma_start(y[:], y_src[:, :, ds(nxt * TB + CONV_AT, TB)]).then_inc(y_landed, 16)
                    sp.wait_ge(gated, UP + 8 * b + 4)
                    sp.sem_inc(loads_begun, 1)
                    sp.dma_start(at[:], tiles("att")[:, :, ds(nxt * TB, TB)]).then_inc(at_landed, 16)
                    sp.wait_ge(f_lo_done, UP + 8 * b + 8)
                    sp.sem_inc(loads_begun, 1)
                    sp.dma_start(z[:, 0:NC, :], tiles("za")[:, :, ds(nxt * TB, TB)]).then_inc(za_landed, 16)
                    sp.dma_start(z[:, NC:KT, :], tiles("zc")[:, :, ds(nxt * TB, TB)]).then_inc(zc_landed, 16)
                    out = d["out"].rearrange("(t p) n -> p t n", p=P)
                    for c in range(KT):
                        sp.wait_ge(t_read, UP + 8 * b + c + 1)
                        sp.sem_inc(loads_begun, 1)
                        sp.dma_start(out[:, ds(b * NT, NT), P * c:P * (c + 1)], ob[:, c % 2, :, :]).then_inc(stored[c % 2], 16)
                    sp.dma_start(h1[:], tiles("h1t")[:, :, ds(nxt * TB, TB)]).then_inc(h1_landed, 16)
                for i in range(2):
                    sp.wait_ge(stored[i], UP + 16 * 4 * NB)
                for s in (y_landed, at_landed, za_landed, zc_landed, h1_landed):
                    sp.wait_ge(s, UP + 16 * (NB + 1))

            @block.gpsimd
            def _(pool):
                for n in range(2, NWT):
                    pool.wait_ge(w_hi_done, UP + n + 1)
                    pool.tensor_tensor(wo_lo[:, n - 2, :], w_raw[n % 4], wo_hi[:, n - 2, :].bitcast(F32), ALU.subtract).then_inc(w_lo_done, 1)

            @block.tensor
            def _(pe):
                def sums(b, bank, ready, src, done):
                    pe.wait_ge(ready, UP + (b + 1) * (NC - 1))
                    pe.matmul(bank[:], ones[:], src, start=True, stop=True).then_inc(done, 1)

                def turn_back(b, c):
                    pe.wait_ge(x_out, UP + 8 * b + c + 1)
                    if c >= 2:
                        pe.wait_ge(t_read, UP + 8 * b + c - 1)
                    else:
                        pe.wait_ge(t_read, UP + 8 * b)
                    for t in range(NT):
                        last = pe.transpose(T[c % 2][:, P * t:P * (t + 1)], h1[:, c, P * t:P * (t + 1)], ident[:])
                    last.then_inc(turned, 1)

                def product(b, n, kts, w_hi, w_lo, cols_of, a_hi, a_lo, ready):
                    if n < 2:
                        pe.wait_ge(x_out, UP + KT * b)
                    elif n < NC + 2:
                        pe.wait_ge(gated, UP + KT * b + NC + n - 1)
                    else:
                        pe.wait_ge(x_out, UP + KT * b + n - NC - 1)
                    for k in range(kts):
                        pe.wait_ge(ready, UP + b * kts + k + 1)
                        for i, (w, a) in enumerate(((w_hi, a_hi), (w_hi, a_lo), (w_lo, a_hi))):
                            last = pe.matmul(G[n % 2][:], w[:, k, cols_of], a[:, k, :], start=(k == 0 and i == 0),
                                             stop=(k == kts - 1 and i == 2))
                    last.then_inc(prod, 1)
                pe.wait_ge(ones_landed, UP + 16)
                sums(0, BM, y_added, acc[:], mean_sum)
                sums(0, BV, sq_added, acc[:], var_sum)
                pe.wait_ge(wp_lo_done, UP + 2)
                with pe.Fori(0, NB) as b:
                    for j in range(NC):
                        product(b, j, NC, wp_hi, wp_lo, slice(P * j, P * (j + 1)), c_hi, c_lo, c_lo_done)
                    pe.wait_ge(w_lo_done, UP + KT)
                    for c in range(KT):
                        product(b, NC + c, KT, wo_hi, wo_lo, slice(P * c, P * (c + 1)), f_hi, f_lo, f_lo_done)
                        if c >= 2:
                            turn_back(b, c - 2)
                        if c == 0:
                            sums(b + 1, BM, y_added, acc[:], mean_sum)
                        if c == 2:
                            sums(b + 1, BV, sq_added, acc[:], var_sum)
                    turn_back(b, KT - 2)
                    turn_back(b, KT - 1)

            @block.scalar
            def _(act):
                def square_y(b):
                    for k in range(NC):
                        act.wait_ge(centred, UP + 4 * b + k + 1)
                        if k < 2:
                            act.wait_ge(rs_step, UP + 4 * b)
                        else:
                            act.wait_ge(sq_added, UP + 3 * b + max(k - 2, 1))
                        act.activation((sq, th)[k % 2][:], y[:, k, :], ACT.Square).then_inc(squared, 1)

                def rsqrt_y(b):
                    act.wait_ge(var_done, UP + b + 1)
                    act.activation(rs[:], sq[:], ACT.Ln).then_inc(ln_done, 1)
                    act.wait_ge(ln_done, UP + b + 1)
                    act.activation(rs[:], rs[:], ACT.Exp, scale=-0.5).then_inc(rs0_done, 1)

                def tanh_y(b):
                    for k in range(NC):
                        act.wait_ge(normed, UP + 4 * b + k + 1)
                        act.wait_ge(swished, UP + 4 * b + k)
                        act.activation(th[:], y[:, k, :], ACT.Tanh, scale=0.5, bias=half_lnb[:, k:k + 1]).then_inc(tanh_done, 1)

                def round_y(b):
                    if not isinstance(b, int):
                        act.wait_ge(prod, UP + TILES * b - KT)
                    for k in range(NC):
                        act.wait_ge(swished, UP + 4 * b + k + 1)
                        act.activation(c_hi[:, k, :], y[:, k, :], ACT.Copy).then_inc(c_hi_done, 1)

                def read_turned(b, c):
                    act.wait_ge(turned, UP + 8 * b + c + 1)
                    act.wait_ge(stored[c % 2], UP + 64 * b + 16 * (c // 2))
                    act.activation(ob[:, c % 2, :, :], T[c % 2][:].rearrange("p (t i) -> p t i", t=NT), ACT.Copy).then_inc(t_read, 1)
                at0 = VROWS["conv_ln_b_2"][0]
                act.activation(half_lnb[:], cols[:, at0:at0 + NC], ACT.Copy, scale=0.5).then_inc(lnb_done, 1)
                act.wait_ge(lnb_done, UP + 1)

                def round_w(n):
                    act.wait_ge(w_landed[n % 4], UP + 16 * (n // 4) + 16)
                    if n < 2:
                        act.activation(wp_hi[:, 2 * n:2 * n + 2, :], w_raw[n % 4].rearrange("p (k n) -> p k n", k=2), ACT.Copy,
                                       scale=0.5).then_inc(w_hi_done, 1)
                    else:
                        act.activation(wo_hi[:, n - 2, :], w_raw[n % 4], ACT.Copy).then_inc(w_hi_done, 1)
                for n in range(2):
                    round_w(n)
                square_y(0)
                round_w(2)
                rsqrt_y(0)
                round_w(3)
                round_w(4)
                tanh_y(0)
                round_w(5)
                round_y(0)
                for n in range(6, NWT):
                    round_w(n)
                with act.Fori(0, NB) as b:
                    act.wait_ge(prod, UP + TILES * b)
                    for k in range(KT):
                        act.wait_ge(gated, UP + 8 * b + k + 1)
                        act.activation(f_hi[:, k, :], z[:, k, :], ACT.Copy).then_inc(f_hi_done, 1)
                    for c in range(KT):
                        if c >= 2:
                            read_turned(b, c - 2)
                        if c == 1:
                            square_y(b + 1)
                        if c == 3:
                            rsqrt_y(b + 1)
                        if c == 5:
                            tanh_y(b + 1)
                        if c == 6:
                            round_y(b + 1)
                    read_turned(b, KT - 2)
                    read_turned(b, KT - 1)

            @block.vector
            def _(dve):
                def bias_y(b):
                    dve.wait_ge(y_landed, UP + 16 * b + 16)
                    for k in range(NC):
                        dve.tensor_scalar(y[:, k, :], y[:, k, :], col("conv_b_2", k), None, ALU.add).then_inc(biased, 1)

                    for k in range(1, NC):
                        dve.wait_ge(biased, UP + 4 * b + k + 1)
                        if k == 1:
                            dve.wait_ge(var_sum, UP + b)
                        else:
                            dve.wait_ge(y_added, UP + 3 * b + k - 1)
                        dve.tensor_tensor(acc[:], y[:, 0, :] if k == 1 else acc[:], y[:, k, :], ALU.add).then_inc(y_added, 1)

                def centre_y(b):
                    dve.wait_ge(mean_sum, UP + b + 1)
                    for k in range(NC):
                        dve.scalar_tensor_tensor(y[:, k, :], BM[:], -1.0 / TB, y[:, k, :], ALU.mult, ALU.add).then_inc(centred, 1)

                def add_squares(b):
                    for k in range(1, NC):
                        dve.wait_ge(squared, UP + 4 * b + k + 1)
                        if k > 1:
                            dve.wait_ge(sq_added, UP + 3 * b + k - 1)
                        dve.tensor_tensor(acc[:], sq[:] if k == 1 else acc[:], (sq, th)[k % 2][:], ALU.add).then_inc(sq_added, 1)

                def var_y(b):
                    dve.wait_ge(var_sum, UP + b + 1)
                    dve.tensor_scalar(sq[:], BV[:], 1.0 / TB, EPS, ALU.mult, ALU.add).then_inc(var_done, 1)

                def norm_y(b):
                    dve.wait_ge(rs0_done, UP + b + 1)
                    newton_rsqrt(dve, rs[:], sq[:], th[:], rs_step, 4 * b)
                    dve.wait_ge(rs_step, UP + 4 * b + 4)
                    for k in range(NC):
                        dve.scalar_tensor_tensor(y[:, k, :], y[:, k, :], col("conv_ln_w_2", k), rs[:], ALU.mult, ALU.mult).then_inc(normed, 1)

                def swish_y(b):
                    for k in range(NC):
                        dve.wait_ge(tanh_done, UP + 4 * b + k + 1)
                        dve.tensor_scalar(y[:, k, :], y[:, k, :], col("conv_ln_b_2", k), None, ALU.add).then_inc(shifted, 1)
                        dve.wait_ge(shifted, UP + 4 * b + k + 1)
                        dve.scalar_tensor_tensor(y[:, k, :], th[:], 1.0, y[:, k, :], ALU.add, ALU.mult).then_inc(swished, 1)

                def rest_y(b):
                    for k in range(NC):
                        dve.wait_ge(c_hi_done, UP + 4 * b + k + 1)
                        dve.tensor_tensor(c_lo[:, k, :], y[:, k, :], c_hi[:, k, :].bitcast(F32), ALU.subtract).then_inc(c_lo_done, 1)

                def rest_f(b, k):
                    dve.wait_ge(f_hi_done, UP + 8 * b + k + 1)
                    dve.tensor_tensor(f_lo[:, k, :], z[:, k, :], f_hi[:, k, :].bitcast(F32), ALU.subtract).then_inc(f_lo_done, 1)

                dve.tensor_scalar(half_gate[:], modv[:, 1, 16:24], 0.5, None, ALU.mult).then_inc(gate_halved, 1)
                bias_y(0)
                centre_y(0)
                for n in range(2):
                    dve.wait_ge(w_hi_done, UP + n + 1)
                    dve.scalar_tensor_tensor(wp_lo[:, 2 * n:2 * n + 2, :], w_raw[n % 4].rearrange("p (k n) -> p k n", k=2), 0.5,
                                             wp_hi[:, 2 * n:2 * n + 2, :].bitcast(F32), ALU.mult, ALU.subtract).then_inc(wp_lo_done, 1)
                add_squares(0)
                var_y(0)
                norm_y(0)
                swish_y(0)
                rest_y(0)
                dve.wait_ge(gate_halved, UP + 1)
                with dve.Fori(0, NB) as b:
                    dve.wait_ge(at_landed, UP + 16 * b + 16)
                    dve.wait_ge(za_landed, UP + 16 * b + 16)
                    for k in range(NC):
                        dve.tensor_tensor(z[:, k, :], at[:, k, :], z[:, k, :], ALU.mult).then_inc(gated, 1)
                    for k in range(NC):
                        rest_f(b, k)
                    dve.wait_ge(zc_landed, UP + 16 * b + 16)
                    for j in range(NC):
                        dve.wait_ge(prod, UP + TILES * b + j + 1)
                        dve.scalar_tensor_tensor(z[:, NC + j, :], G[j % 2][:], col("b_pw_2", j), z[:, NC + j, :], ALU.add, ALU.mult).then_inc(gated, 1)
                        rest_f(b, NC + j)
                    bias_y(b + 1)
                    dve.wait_ge(h1_landed, UP + 16 * b + 16)
                    for c in range(KT):
                        dve.wait_ge(prod, UP + TILES * b + NC + c + 1)
                        dve.scalar_tensor_tensor(h1[:, c, :], G[c % 2][:], half_gate[:, c:c + 1], h1[:, c, :], ALU.mult, ALU.add).then_inc(x_out, 1)
                        if c == 0:
                            centre_y(b + 1)
                        if c == 1:
                            add_squares(b + 1)
                        if c == 2:
                            var_y(b + 1)
                        if c == 4:
                            norm_y(b + 1)
                        if c == 5:
                            swish_y(b + 1)
                        if c == 6:
                            rest_y(b + 1)

SCRATCH = {"h1t": (D, SEQ), "qt": (512, SEQ), "kt": (P, KEYS), "vtok": (KEYS, P), "za": (512, SEQ), "zc": (512, SEQ),
           "conv_y": (512, CONV_AT + SEQ), "att": (512, SEQ)}
PHASES = [modulation, gla_block, context_keys, projections, attention, output]


def program(nc, d, phases=PHASES):
    with ExitStack() as ctx:
        keep = {"ident": ctx.enter_context(nc.sbuf_tensor("ident_sb", [P, P], F32)),
                "cols": ctx.enter_context(nc.sbuf_tensor("cols", [P, P], F32)),
                "modv": ctx.enter_context(nc.sbuf_tensor("modv", [P, 3, 24], F32)),
                "gains": ctx.enter_context(nc.sbuf_tensor("gains", [P, 3, 8], F32)),
                "half_gn": ctx.enter_context(nc.sbuf_tensor("half_gn", [P, 2], F32))}
        for phase in phases:
            phase(nc, d, keep)


def shape_constants():
    i = np.arange(P)
    sel = ((i[:, None] <= i[None, :]) & (i[:, None] // CHUNK == i[None, :] // CHUNK)).astype(np.uint32)
    reset = np.broadcast_to((np.arange(TB) % CHUNK != 0).astype(np.float32), (P, TB)).copy()
    rot = np.zeros((P, P), np.float32)
    for m in range(P):
        if m % 32 < 16:
            rot[m + 16, m] = -1.0
        else:
            rot[m - 16, m] = 1.0
    freqs = np.float32(10000.0) ** (-np.arange(0, 32, 2, dtype=np.float32) / np.float32(32))
    t = np.arange(SEQ)
    place = np.where((i % HD < 32)[:, None], (t // 64)[None, :], (t % 64)[None, :]).astype(np.float32)
    angle = place * freqs[i % 16][:, None].astype(np.float32)
    head_ones = (i[:, None] // HD == i[None, :] // HD).astype(np.float32)
    return {"ident": np.eye(P, dtype=np.float32), "sel": sel, "reset": reset, "ones": np.ones((P, P), np.float32),
            "rot_t": rot, "head_ones": head_ones, "cos": np.cos(angle), "sin": np.sin(angle)}


_INS = ["x", "ctx_2", "c", "c_2", "c_ctx_2", "ada_w", "ada_b", "norm_g", "gla_w_in", "gla_w_alpha", "gla_b_alpha", "gla_norm_g",
        "gla_w_out", "final_g", "w_mod_2", "b_mod_2", "norm_w_2", "w_in_2", "q_norm_w_2", "k_norm_w_2", "conv_w_2", "conv_b_2",
        "conv_ln_w_2", "conv_ln_b_2", "w_pw_2", "b_pw_2", "w_out_2"]
_LEADING_ONE = [n for n in _INS if n not in ("final_g", "c_ctx_2")]


def kernel(**inputs):
    import concourse.bacc as bacc
    from concourse.bass_utils import run_bass_kernel_spmd

    nc = bacc.Bacc("TRN2", target_bir_lowering=False, num_devices=1)
    arrays, d = {}, {}
    for name in _INS:
        a = np.ascontiguousarray(inputs[name])
        arrays[name] = a[0] if name in _LEADING_ONE else a
    arrays.update(shape_constants())
    feeds = {}
    for name, a in arrays.items():
        d[name] = nc.dram_tensor(f"in_{name}", a.shape, mybir.dt.from_np(a.dtype), kind="ExternalInput").ap()
        feeds[f"in_{name}"] = a
    for name, shape in SCRATCH.items():
        d[name] = nc.dram_tensor(f"scratch_{name}", shape, F32).ap()
    d["out"] = nc.dram_tensor("out_0", (SEQ, D), F32, kind="ExternalOutput").ap()
    program(nc, d)
    result = run_bass_kernel_spmd(nc, [feeds], core_ids=[0])
    return np.asarray(result.results[0]["out_0"]).reshape(1, SEQ, D)
```
